# Optimizing a Trainium2 kernel written in Bass

```python
import jax, jax.numpy as jnp
from jax import lax
import numpy as np

D_MODEL = 2048
BATCH = 1
SEQ = 256
DEPTH = 1

N_META = 16
GLA_HEADS = 4
GLA_KDIM = D_MODEL // 2
GLA_VDIM = D_MODEL
GLA_DK = GLA_KDIM // GLA_HEADS
GLA_DV = GLA_VDIM // GLA_HEADS
GLA_GATE_RANK = 16
GLA_GATE_TAU = 16.0
GLA_CHUNK = 64
MLA_HEADS = D_MODEL // 128
MLA_Q_LORA = D_MODEL // 4
MLA_KV_LORA = D_MODEL // 4
MLA_NOPE = 128
MLA_ROPE = 64
MLA_QK = MLA_NOPE + MLA_ROPE
MLA_V = 128
ROPE_THETA = 10000.0
Q_BLOCK = 128
FF_HIDDEN = -(-(8 * D_MODEL) // (3 * 256)) * 256
EPS = 1e-6
IN_SPLITS = (GLA_KDIM, GLA_KDIM, GLA_VDIM, GLA_VDIM, GLA_GATE_RANK,
             MLA_Q_LORA, MLA_KV_LORA, MLA_ROPE, D_MODEL, D_MODEL)
N_IN = sum(IN_SPLITS)

kernel_name = "hybrid_gla_mla_gated_block"

def rmsnorm(x, g):
    xf = x.astype(jnp.float32)
    y = xf * lax.rsqrt(jnp.mean(xf * xf, axis=-1, keepdims=True) + EPS)
    return (y * g.astype(jnp.float32)).astype(x.dtype)

def rope_tables(length):
    inv = 1.0 / (ROPE_THETA ** (jnp.arange(0, MLA_ROPE, 2, dtype=jnp.float32) / MLA_ROPE))
    ang = jnp.arange(length, dtype=jnp.float32)[:, None] * inv[None, :]
    return jnp.cos(ang), jnp.sin(ang)

def apply_rope(x, cos, sin):
    xf = x.astype(jnp.float32)
    x1, x2 = jnp.split(xf, 2, axis=-1)
    return jnp.concatenate([x1 * cos - x2 * sin, x2 * cos + x1 * sin], axis=-1).astype(x.dtype)

def split_heads(t, n, d):
    b, l, _ = t.shape
    return t.reshape(b, l, n, d).transpose(0, 2, 1, 3)

def gla_chunk(state, xs):
    q, k, v, g = xs
    c = q.shape[2]
    b = jnp.cumsum(g, axis=2)
    qd = q * jnp.exp(b)
    causal = jnp.tril(jnp.ones((c, c), dtype=bool))
    a = jnp.einsum('bhtd,bhsd->bhts', qd, k * jnp.exp(-b))
    a = jnp.where(causal, a, 0.0)
    o = jnp.einsum('bhts,bhsv->bhtv', a, v) + jnp.einsum('bhtd,bhdv->bhtv', qd, state)
    b_last = b[:, :, -1, :]
    new_state = (jnp.exp(b_last)[..., None] * state
                 + jnp.einsum('bhsd,bhsv->bhdv', k * jnp.exp(b_last[:, :, None, :] - b), v))
    return new_state, o

def gla_scan(q, k, v, g):
    bsz, h, length, _ = q.shape
    n_real = length - N_META
    s0 = jnp.zeros((bsz, h, GLA_DK, GLA_DV), jnp.float32)
    s_meta, o_meta = gla_chunk(s0, (q[:, :, :N_META], k[:, :, :N_META],
                                    v[:, :, :N_META], g[:, :, :N_META]))
    n_chunks = n_real // GLA_CHUNK

    def to_chunks(t):
        return jnp.moveaxis(t[:, :, N_META:].reshape(bsz, h, n_chunks, GLA_CHUNK, t.shape[-1]), 2, 0)

    _, o_real = lax.scan(gla_chunk, s_meta, (to_chunks(q), to_chunks(k), to_chunks(v), to_chunks(g)))
    o_real = jnp.moveaxis(o_real, 0, 2).reshape(bsz, h, n_real, GLA_DV)
    return jnp.concatenate([o_meta, o_real], axis=2)

def gla_branch(zq, zk, zv, zr, zlr, gate_w2, gate_b, onorm_g):
    bsz, length, _ = zq.shape
    q = split_heads(zq, GLA_HEADS, GLA_DK).astype(jnp.float32) * (GLA_DK ** -0.5)
    k = split_heads(zk, GLA_HEADS, GLA_DK).astype(jnp.float32)
    v = split_heads(zv, GLA_HEADS, GLA_DV).astype(jnp.float32)
    logit = (zlr @ gate_w2 + gate_b).astype(jnp.float32)
    g = split_heads(jax.nn.log_sigmoid(logit) / GLA_GATE_TAU, GLA_HEADS, GLA_DK)
    o = gla_scan(q, k, v, g).transpose(0, 2, 1, 3)
    o = rmsnorm(o, onorm_g)
    r = zr.reshape(bsz, length, GLA_HEADS, GLA_DV).astype(jnp.float32)
    return (o * jax.nn.silu(r)).astype(zr.dtype).reshape(bsz, length, GLA_VDIM)

def causal_block_attention(q, k, v):
    bsz, h, length, dqk = q.shape
    scale = dqk ** -0.5
    s_m = jnp.einsum('bhqd,bhkd->bhqk', q[:, :, :N_META], k[:, :, :N_META]).astype(jnp.float32) * scale
    s_m = jnp.where(jnp.tril(jnp.ones((N_META, N_META), dtype=bool)), s_m, -1e30)
    o_meta = jnp.einsum('bhqk,bhkd->bhqd', jax.nn.softmax(s_m, axis=-1).astype(v.dtype), v[:, :, :N_META])
    n_real = length - N_META
    n_blocks = n_real // Q_BLOCK
    q_blocks = jnp.moveaxis(q[:, :, N_META:].reshape(bsz, h, n_blocks, Q_BLOCK, dqk), 2, 0)
    key_pos = jnp.arange(length)

    def one_block(args):
        qb, i = args
        q_pos = N_META + i * Q_BLOCK + jnp.arange(Q_BLOCK)
        s = jnp.einsum('bhqd,bhkd->bhqk', qb, k).astype(jnp.float32) * scale
        s = jnp.where(key_pos[None, :] <= q_pos[:, None], s, -1e30)
        p = jax.nn.softmax(s, axis=-1).astype(v.dtype)
        return jnp.einsum('bhqk,bhkd->bhqd', p, v)

    o_real = lax.map(one_block, (q_blocks, jnp.arange(n_blocks)))
    o_real = jnp.moveaxis(o_real, 0, 2).reshape(bsz, h, n_real, v.shape[-1])
    return jnp.concatenate([o_meta, o_real], axis=2)

def mla_branch(zcq, zckv, zkr, q_a_norm_g, w_uq, kv_a_norm_g, w_ukv, q_norm_g, k_norm_g, cos, sin):
    bsz, length, _ = zcq.shape
    q = (rmsnorm(zcq, q_a_norm_g) @ w_uq).reshape(bsz, length, MLA_HEADS, MLA_QK)
    kv = (rmsnorm(zckv, kv_a_norm_g) @ w_ukv).reshape(bsz, length, MLA_HEADS, MLA_NOPE + MLA_V)
    k_nope, v = kv[..., :MLA_NOPE], kv[..., MLA_NOPE:]
    k_rope = jnp.broadcast_to(zkr[:, :, None, :], (bsz, length, MLA_HEADS, MLA_ROPE))
    k = jnp.concatenate([k_nope, k_rope], axis=-1)
    q = rmsnorm(q, q_norm_g)
    k = rmsnorm(k, k_norm_g)
    cs, sn = cos[:, None, :], sin[:, None, :]
    q = jnp.concatenate([q[..., :MLA_NOPE], apply_rope(q[..., MLA_NOPE:], cs, sn)], axis=-1)
    k = jnp.concatenate([k[..., :MLA_NOPE], apply_rope(k[..., MLA_NOPE:], cs, sn)], axis=-1)
    o = causal_block_attention(q.transpose(0, 2, 1, 3), k.transpose(0, 2, 1, 3), v.transpose(0, 2, 1, 3))
    return o.transpose(0, 2, 1, 3).reshape(bsz, length, MLA_HEADS * MLA_V)

def setup_inputs(seed: int = 0) -> dict:
    key = jax.random.key(seed)
    ks = jax.random.split(key, 20)
    f32 = jnp.float32

    def nrm(k, shape, fan_in):
        return jax.random.normal(k, shape, f32) * (fan_in ** -0.5)

    def gain(k, shape):
        return 1.0 + 0.02 * jax.random.normal(k, shape, f32)

    return {
        "x": jax.random.normal(ks[0], (BATCH, SEQ, D_MODEL), f32),
        "meta_tokens": jax.random.normal(ks[1], (N_META, D_MODEL), f32),
        "norm1_g": gain(ks[2], (DEPTH, D_MODEL)),
        "w_in": nrm(ks[3], (DEPTH, D_MODEL, N_IN), D_MODEL),
        "gla_gate_w2": nrm(ks[4], (DEPTH, GLA_GATE_RANK, GLA_KDIM), GLA_GATE_RANK),
        "gla_gate_b": 0.1 * jax.random.normal(ks[5], (DEPTH, GLA_KDIM), f32),
        "gla_onorm_g": gain(ks[6], (DEPTH, GLA_DV)),
        "w_branch_a": nrm(ks[7], (DEPTH, GLA_VDIM, D_MODEL), GLA_VDIM),
        "q_a_norm_g": gain(ks[8], (DEPTH, MLA_Q_LORA)),
        "w_uq": nrm(ks[9], (DEPTH, MLA_Q_LORA, MLA_HEADS * MLA_QK), MLA_Q_LORA),
        "kv_a_norm_g": gain(ks[10], (DEPTH, MLA_KV_LORA)),
        "w_ukv": nrm(ks[11], (DEPTH, MLA_KV_LORA, MLA_HEADS * (MLA_NOPE + MLA_V)), MLA_KV_LORA),
        "q_norm_g": gain(ks[12], (DEPTH, MLA_QK)),
        "k_norm_g": gain(ks[13], (DEPTH, MLA_QK)),
        "w_branch_b": nrm(ks[14], (DEPTH, MLA_HEADS * MLA_V, D_MODEL), MLA_HEADS * MLA_V),
        "w_out": nrm(ks[15], (DEPTH, D_MODEL, D_MODEL), D_MODEL),
        "norm2_g": gain(ks[16], (DEPTH, D_MODEL)),
        "w_gate_up": nrm(ks[17], (DEPTH, D_MODEL, 2 * FF_HIDDEN), D_MODEL),
        "w_down": nrm(ks[18], (DEPTH, FF_HIDDEN, D_MODEL), FF_HIDDEN),
    }

def reference(x, meta_tokens, norm1_g, w_in, gla_gate_w2, gla_gate_b, gla_onorm_g, w_branch_a,
              q_a_norm_g, w_uq, kv_a_norm_g, w_ukv, q_norm_g, k_norm_g, w_branch_b, w_out,
              norm2_g, w_gate_up, w_down):
    bsz, seq, d = x.shape
    meta = jnp.broadcast_to(meta_tokens[None].astype(x.dtype), (bsz, N_META, d))
    h_res = jnp.concatenate([meta, x], axis=1)
    cos, sin = rope_tables(h_res.shape[1])
    split_idx = np.cumsum(IN_SPLITS)[:-1].tolist()
    for l in range(DEPTH):
        h = rmsnorm(h_res, norm1_g[l])
        z = h @ w_in[l]
        zq, zk, zv, zr, zlr, zcq, zckv, zkr, za, zb = jnp.split(z, split_idx, axis=-1)
        y_a = gla_branch(zq, zk, zv, zr, zlr, gla_gate_w2[l], gla_gate_b[l], gla_onorm_g[l]) @ w_branch_a[l]
        y_b = mla_branch(zcq, zckv, zkr, q_a_norm_g[l], w_uq[l], kv_a_norm_g[l], w_ukv[l],
                         q_norm_g[l], k_norm_g[l], cos, sin) @ w_branch_b[l]
        merged = jax.nn.sigmoid(za) * y_a + jax.nn.sigmoid(zb) * y_b
        h_res = h_res + merged @ w_out[l]
        h2 = rmsnorm(h_res, norm2_g[l])
        gu = h2 @ w_gate_up[l]
        g, u = gu[..., :FF_HIDDEN], gu[..., FF_HIDDEN:]
        h_res = h_res + (jax.nn.silu(g) * u) @ w_down[l]
    return h_res[:, N_META:]


_drawn_inputs = setup_inputs


def setup_inputs(seed=0):
    import zlib

    import numpy as np

    out = dict(_drawn_inputs(seed))
    spreads = {}
    factors = {'norm1_g': 3.769,
     'gla_gate_b': 3.622,
     'gla_onorm_g': 7.954,
     'q_a_norm_g': 8.0,
     'kv_a_norm_g': 8.0,
     'q_norm_g': 8.0,
     'k_norm_g': 8.0,
     'norm2_g': 13.071}
    for name, (base, spread) in spreads.items():
        noise = np.random.default_rng([zlib.crc32(name.encode()), seed]).standard_normal(out[name].shape)
        drawn = base * np.exp(spread * noise) if base else spread * noise
        out[name] = __import__('jax').numpy.asarray(drawn.astype(out[name].dtype))
    for name, factor in factors.items():
        out[name] = (out[name] * factor).astype(out[name].dtype)
    return out
```

```python
from contextlib import ExitStack

import numpy as np

import concourse.bass as bass
from concourse import mybir

F32 = mybir.dt.float32
F32R = mybir.dt.float32r
I32 = mybir.dt.int32
ACT = mybir.ActivationFunctionType
ALU = mybir.AluOpType

P = 128
D = 2048
META = 16
SEQ = 256
L = META + SEQ
KT = D // P
EPS = 1e-6
GLA_HEADS, DK, DV, RANK, TAU, CHUNK = 4, 256, 512, 16, 16.0, 64
HEADS, LORA, NOPE, ROPE, DVM = 16, 512, 128, 64, 128
QK = NOPE + ROPE
LT = LORA // P
FF = 5632
FT = FF // P
NEG = -1e30

C_Q, C_K, C_V, C_R = 0, 1024, 2048, 4096
C_LR = 6144
C_CQ = C_LR + RANK
C_CKV = C_CQ + LORA
C_KR = C_CKV + LORA
C_ZA = C_KR + ROPE
C_ZB = C_ZA + D

PANEL = 2048
RAW, SPL = 4, 2
PAIRS = HEADS // 2
P_LAT = 1
P_MLA, N_MLA = P_LAT + 8, 4
P_GLA, N_GLA = P_MLA + N_MLA * PAIRS, 12
P_MRG, N_MRG = P_GLA + N_GLA * GLA_HEADS, 12
P_OUT, N_OUT = P_MRG + N_MRG * 4, 4
P_FF, N_FF = P_OUT + N_OUT * 4, 4
P_DN, N_DN = P_FF + N_FF * (FF // 256), 4
PANELS = P_DN + N_DN * (FT // 4)

G_1, G_2, G_O, G_QA, G_KVA, G_QN, G_QR, G_KN, G_KR, G_B, G_ALL = 0, 16, 32, 36, 40, 44, 45, 46, 47, 48, 56

TOK = ((0, META), (META, META + P), (META + P, L))


def wait(eng, sem, value):
    if isinstance(value, int) and value <= 0:
        return
    eng.wait_ge(sem, value)


class Chain:

    def __init__(self, eng, sem):
        self.eng, self.sem, self.total, self.base, self.k = eng, sem, 0, 0, 0

    def link(self, ins):
        self.k += 1
        ins.then_inc(self.sem, 1)
        self.eng.wait_ge(self.sem, self.base + self.k)

    def enter(self, turn, per):
        self.close()
        self.base, self.per = turn * per + self.total, per

    def leave(self, turns):
        assert self.k == self.per, (self.k, self.per)
        self.total += turns * self.per
        self.base, self.k = self.total, 0

    def close(self):
        self.total += self.k
        self.base, self.k = self.total, 0


def build(nc, x, meta, w_in, w2, w_a, w_uq, w_ukv, w_b, w_out, w_gu, w_dn, gains, consts, out):
    ctx = ExitStack()
    with ctx:
        def sem(name):
            return ctx.enter_context(nc.semaphore(name))

        BASE = 16512
        top = [0]

        def put(name, shape, dt=F32, at=None):
            size = -(-4 * int(np.prod(shape[1:])) // 32) * 32
            if at is None:
                at = top[0]
                top[0] += size
            return nc.alloc_sbuf_tensor_at(name, list(shape), dt, offset=BASE + at)

        raw = [put(f"raw{s}", [P, PANEL]) for s in range(RAW)]
        whi = [put(f"whi{s}", [P, PANEL], F32R) for s in range(SPL)]
        wlo = [put(f"wlo{s}", [P, PANEL], F32R) for s in range(SPL)]
        ident = put("ident", [P, P])
        ones = put("ones", [P, P])
        gain = put("gain", [P, G_ALL])
        tick = put("tick", [P, 1])
        after_const = top[0]
        rot2 = put("rot2", [P, P])
        halves = put("halves", [P, 2, P])
        dup = put("dup", [ROPE, 2, P])
        causal = put("causal", [P, L])
        cos2 = put("cos2", [P, L])
        sin2 = put("sin2", [P, L])
        inchunk = put("inchunk", [P, P], I32)
        keep = put("keep", [P, L])
        h_hi = put("h_hi", [P, KT, L], F32R)
        h_lo = put("h_lo", [P, KT, L], F32R)
        mixers = top[0]
        o_mla = put("o_mla", [P, KT, SEQ])
        zb = put("zb", [P, KT, SEQ])
        lrT = put("lrT", [RANK, L])
        work = top[0]
        ckv_hi = put("ckv_hi", [P, LT, L], F32R)
        ckv_lo = put("ckv_lo", [P, LT, L], F32R)
        cq_hi = put("cq_hi", [P, LT, SEQ], F32R)
        cq_lo = put("cq_lo", [P, LT, SEQ], F32R)
        krr = put("krr", [P, L])
        krsq = put("krsq", [ROPE, L])
        after_lat = top[0]
        qn = put("qn", [P, 2, SEQ])
        qr = put("qr", [P, SEQ])
        qrg = put("qrg", [P, SEQ])
        kn = put("kn", [P, 2, L])
        vm0 = put("vm0", [META, 2, DVM])
        vm = put("vm", [P, 2, 2, DVM])
        qnsq = put("qnsq", [P, 2, SEQ])
        qrsq = put("qrsq", [P, SEQ])
        knsq = put("knsq", [P, 2, L])
        rq = put("rq", [P, 2, SEQ])
        rk = put("rk", [P, 2, L])
        qs = put("qs", [P, 2, SEQ])
        ks = put("ks", [P, 2, L])
        qc = put("qc", [P, SEQ])
        qsn = put("qsn", [P, SEQ])
        qrs = put("qrs", [P, SEQ])
        krs = put("krs", [P, 2, L])
        sc0 = put("sc0", [P, 2, META + P])
        sc1 = put("sc1", [P, 2, L])
        pt0 = put("pt0", [META, 2, SEQ])
        pt1 = put("pt1", [P, 2, SEQ])
        pt2 = put("pt2", [P, 2, P])
        mx = put("mx", [P, 4])
        nb = put("nb", [P, 4])
        sm = put("sm", [P, 4])
        rs = put("rs", [P, 4])
        end_mla = top[0]
        top[0] = after_lat
        kr = put("kr", [ROPE, L])
        krg = put("krg", [ROPE, L])
        krc = put("krc", [P, L])
        krn = put("krn", [P, L])
        lat = put("lat", [P, 2, LT, L])
        latsq = put("latsq", [P, 2, LT, L])
        rlat = put("rlat", [P, 2, L])
        end_lat = top[0]
        top[0] = mixers
        xm = put("xm", [META, D])
        xn = put("xn", [P, 2, D])
        xT = put("xT", [P, KT, L])
        xsq = put("xsq", [P, KT, L])
        r1 = put("r1", [P, L])
        end_x = top[0]
        top[0] = work
        o_gla = put("o_gla", [P, KT, SEQ])
        w2h = put("w2h", [RANK, DK])
        gx = put("gx", [P, 2, L])
        gl = put("gl", [P, 2, L])
        gb = put("gb", [P, 2, L])
        eb = put("eb", [P, 2, L])
        enb = put("enb", [P, 2, L])
        kf = gl
        qd = put("qd", [P, 2, SEQ])
        ke = put("ke", [P, 2, L])
        kd = put("kd", [P, 2, L])
        kdn0 = put("kdn0", [META, DK])
        kdn = put("kdn", [P, 2, DK])
        va0 = put("va0", [META, DV])
        va = put("va", [P, 2, DV])
        am = put("am", [P, 2, P])
        st = put("st", [P, 4, 2, DV])
        osq = put("osq", [P, 4, SEQ])
        sr = put("sr", [P, 4, SEQ])
        ro = enb[:, 0, 0:SEQ]
        end_gla = top[0]
        o_lo_m = put("o_lo_m", [P, KT, SEQ], F32R, at=mixers)
        m_lo = put("m_lo", [P, KT, SEQ], F32R, at=mixers + 4 * KT * SEQ)
        o_lo_g = put("o_lo_g", [P, KT, SEQ], F32R, at=work)
        top[0] = work + 4 * KT * SEQ
        o_hi_m = put("o_hi_m", [P, KT, SEQ], F32R)
        o_hi_g = put("o_hi_g", [P, KT, SEQ], F32R)
        m_hi = put("m_hi", [P, KT, SEQ], F32R)
        sb = put("sb", [P, 2, SEQ])
        end_mrg = top[0]
        sa = put("sa", [P, 2, SEQ], at=after_const)
        mb = put("mb", [P, 2, SEQ], at=after_const + 2048)
        mf = put("mf", [P, 2, SEQ], at=after_const + 4096)
        top[0] = after_const
        x2 = put("x2", [P, KT, SEQ])
        h2_hi = put("h2_hi", [P, KT, SEQ], F32R)
        h2_lo = put("h2_lo", [P, KT, SEQ], F32R)
        a_hi = put("a_hi", [P, FT, SEQ], F32R)
        a_lo = put("a_lo", [P, FT, SEQ], F32R)
        sg = put("sg", [P, 2, SEQ])
        af = put("af", [P, 2, SEQ])
        end_ff = top[0]
        for name, end in (("mla", end_mla), ("lat", end_lat), ("x", end_x), ("gla", end_gla), ("mrg", end_mrg), ("ff", end_ff)):
            assert BASE + end <= nc.sbuf_usable_end, (name, BASE + end - nc.sbuf_usable_end)
        top[0] = work
        xs = put("xs", [P, 2, 2, 2 * P])
        x2sq = put("x2sq", [P, 2, SEQ])
        ssum = put("ssum", [P, 2, SEQ])
        r2 = put("r2", [P, SEQ])
        h2f = put("h2f", [P, 4, SEQ])
        yT = put("yT", [P, 2, 4, SEQ], at=after_const + 4 * KT * SEQ)
        yn = put("yn", [P, 2, 2, 4 * P], at=after_const + 4 * KT * SEQ + 8192)

        psum = ctx.enter_context(nc.psum_tensor("psum", [P, 8, 512], F32))

        def pair(b, n):
            return psum[:, b:b + 2, 0:n]

        raw_in = [sem(f"raw_in{s}") for s in range(RAW)]
        hi_done = sem("hi_done")
        lo_done = sem("lo_done")
        used = sem("used")
        act_own, dve_own, pool_own = sem("act_own"), sem("dve_own"), sem("pool_own")

        block = ctx.enter_context(nc.Block())

        def after(p0, per, i, j):
            return i * per + (p0 + j + 1)

        def raw_value(p0, per, i, j):
            p = p0 + j
            return i * (16 * per // RAW) + 16 * (p // RAW + 1)

        def slot(p0, j, n):
            return (p0 + j) % n

        UQ_PARTS = ((0, NOPE, 0), (NOPE, QK, LT * 2 * NOPE))

        def uq_part(t, a, b, at, from_raw):
            if from_raw:
                return t[:, 0:LT * 2 * QK].rearrange("p (k h c) -> p k h c", k=LT, h=2)[:, :, :, a:b]
            return t[:, at:at + LT * 2 * (b - a)].rearrange("p (k h c) -> p k h c", k=LT, h=2)

        S = {}

        def s(name):
            if name not in S:
                S[name] = sem(name)
            return S[name]

        @block.sync
        def _(sp):
            def load(p0, per, i, j, dst, src):
                if p0 + j >= RAW:
                    sp.wait_ge(lo_done, after(p0, per, i, j) - RAW)
                sp.dma_start(dst, src).then_inc(raw_in[slot(p0, j, RAW)], 16)

            def wide(p0, per, i, j, w, row0, col0):
                dst = raw[slot(p0, j, RAW)][:, :].rearrange("p (k c) -> p k c", k=8)
                src = w[row0:row0 + 8 * P, :].rearrange("(k p) c -> p k c", p=P)[:, :, bass.ds(col0, 256)]
                load(p0, per, i, j, dst, src)

            sp.dma_start(ident[:, :], consts["ident"]).then_inc(s("ident_in"), 16)
            sp.dma_start(xm[:, :], meta).then_inc(s("xm_in"), 16)
            xv = x.rearrange("o (t p) d -> p (o t) d", p=P)
            for f in range(4):
                sp.dma_start(xn[:, :, f * 512:(f + 1) * 512], xv[:, :, f * 512:(f + 1) * 512]).then_inc(s(f"xn_in{f}"), 16)
            sp.dma_start(gain[:, :], gains).then_inc(s("gain_in"), 16)
            small = raw[0][:, 0:KT * (RANK + ROPE)].rearrange("p (k c) -> p k c", k=KT)
            wk = w_in.rearrange("(k p) c -> p k c", p=P)
            sp.dma_start(small[:, :, 0:RANK], wk[:, :, C_LR:C_LR + RANK]).then_inc(s("lr_in"), 16)
            sp.dma_start(small[:, :, RANK:], wk[:, :, C_KR:C_KR + ROPE]).then_inc(raw_in[0], 16)
            for j in range(3):
                wide(P_LAT, 8, 0, j, w_in, (j % 2) * 8 * P, C_CQ + 256 * (j // 2))
            for t, name in ((rot2, "rot2"), (halves, "halves"), (dup, "dup"), (causal, "causal"), (cos2, "cos2"), (sin2, "sin2"),
                            (inchunk, "inchunk"), (keep, "keep")):
                sp.dma_start(t[:], consts[name]).then_inc(s(f"const_{name}"), 16)
            for j in range(3, 8):
                wide(P_LAT, 8, 0, j, w_in, (j % 2) * 8 * P, C_CQ + 256 * (j // 2))
            uq = w_uq.rearrange("(k p) c -> p k c", p=P)
            ukv = w_ukv.rearrange("(k p) c -> p k c", p=P)
            with sp.Fori(0, PAIRS) as i:
                uq_col, ukv_col = sp.snap(i * (2 * QK)), sp.snap(i * 512)
                load(P_MLA, N_MLA, i, 0, raw[slot(P_MLA, 0, RAW)][:, 0:LT * 2 * QK].rearrange("p (k c) -> p k c", k=LT),
                     uq[:, :, bass.ds(uq_col, 2 * QK)])
                load(P_MLA, N_MLA, i, 1, raw[slot(P_MLA, 1, RAW)][:, :].rearrange("p (k c) -> p k c", k=LT),
                     ukv[:, :, bass.ds(ukv_col, 512)])
                for kh in range(2):
                    wide(P_MLA, N_MLA, i, 2 + kh, w_in, kh * 8 * P, i * 256 + C_ZB)
            with sp.Fori(0, GLA_HEADS) as i:
                for j, col in enumerate((C_K, C_Q)):
                    for kh in range(2):
                        wide(P_GLA, N_GLA, i, 2 * j + kh, w_in, kh * 8 * P, i * DK + col)
                    if j == 0:
                        sp.wait_ge(s("om_out"), PAIRS)
                        sp.dma_start(w2h[:, :], w2[:, bass.ds(i * DK, DK)]).then_inc(s("w2_in"), 16)
                for b in range(2):
                    for kh in range(2):
                        wide(P_GLA, N_GLA, i, 4 + 2 * b + kh, w_in, kh * 8 * P, i * DV + (C_V + 256 * b))
                for b in range(2):
                    for kh in range(2):
                        wide(P_GLA, N_GLA, i, 8 + 2 * b + kh, w_in, kh * 8 * P, i * DV + (C_R + 256 * b))
            with sp.Fori(0, 4) as i:
                for b in range(2):
                    for j, (w, col) in enumerate(((w_in, C_ZA), (w_a, 0), (w_b, 0))):
                        for kh in range(2):
                            step = P >> j
                            at = (i * (512 // step) + 256 * b // step) * step + col if j else i * 512 + (col + 256 * b)
                            wide(P_MRG, N_MRG, i, 6 * b + 2 * j + kh, w, kh * 8 * P, at)
            with sp.Fori(0, 4) as i:
                for b in range(2):
                    for kh in range(2):
                        wide(P_OUT, N_OUT, i, 2 * b + kh, w_out, kh * 8 * P, i * 512 + 256 * b)
                    sp.wait_ge(used, after(P_MRG, N_MRG, 3, 11))
                    sp.wait_ge(used, after(P_OUT, N_OUT, i, 2 * b + 1) - N_OUT)
                    sp.dma_start(xs[:, b], xv[:, :, bass.ds(i * 512 + 256 * b, 256)]).then_inc(s(f"xs_in{b}"), 16)
            with sp.Fori(0, FF // 256) as i:
                for j in range(2):
                    for kh in range(2):
                        wide(P_FF, N_FF, i, 2 * j + kh, w_gu, kh * 8 * P, i * 256 + FF * j)
            dn = w_dn.rearrange("(g k p) c -> g p k c", p=P, k=4)
            with sp.Fori(0, FT // 4) as i:
                for c in range(4):
                    load(P_DN, N_DN, i, c, raw[slot(P_DN, c, RAW)][:, :].rearrange("p (k c) -> p k c", k=4),
                         dn[bass.ds(i, 1), :, :, c * 512:(c + 1) * 512].rearrange("g p k c -> p (g k) c"))
            ov = out.rearrange("o (t p) d -> p (o t) d", p=P)
            for c in range(4):
                sp.wait_ge(s("yn_done"), 2 * (c + 1))
                sp.dma_start(ov[:, :, c * 512:(c + 1) * 512], yn[:, c % 2]).then_inc(s(f"out_done{c}"), 16)
            for c in range(4):
                sp.wait_ge(s(f"out_done{c}"), 16)

        @block.gpsimd
        def _(pool):
            own = Chain(pool, pool_own)

            def mult(o, a):
                return nc.gpsimd.tensor_tensor(o, a, a, ALU.mult)

            nc.gpsimd.memset(ones[:, :], 1.0).then_inc(s("ones_set"), 1)
            pool.wait_ge(s("lat_lo"), 2)
            with pool.Fori(0, PAIRS) as i:
                wait(pool, s("norm_sums"), i)
                pool.wait_ge(s("qn_out"), i + 1)
                mult(qnsq[:, :, :], qn[:, :, :]).then_inc(s("mla_sq"), 1)
                pool.wait_ge(s("qr_out"), i + 1)
                mult(qrsq[:, :], qr[:, :]).then_inc(s("mla_sq"), 1)
                pool.wait_ge(s("kn_out"), i + 1)
                mult(knsq[:, :, :], kn[:, :, :]).then_inc(s("mla_sq"), 1)
            with pool.Fori(0, GLA_HEADS) as i:
                pool.wait_ge(s("o_out"), i + 1)
                og = o_gla[:, bass.ds(i * 4, 4), :]
                nc.gpsimd.tensor_tensor(osq[:, :, :], og, og, ALU.mult).then_inc(s("o_sq"), 1)
            pool.wait_ge(used, after(P_MRG, N_MRG, 3, 11))
            own.link(nc.gpsimd.memset(ssum[:, :, :], 0.0))
            with pool.Fori(0, 4) as i:
                own.enter(i, 4)
                for b in range(2):
                    pool.wait_ge(s(f"x2_out{b}"), i + 1)
                    xb = x2[:, bass.ds(i * 4 + 2 * b, 2), :]
                    own.link(nc.gpsimd.tensor_tensor(x2sq[:, :, :], xb, xb, ALU.mult))
                    own.link(nc.gpsimd.tensor_tensor(ssum[:, :, :], ssum[:, :, :], x2sq[:, :, :], ALU.add))
            own.leave(4)
            own.link(nc.gpsimd.tensor_tensor(x2sq[:, 0, :], ssum[:, 0, :], ssum[:, 1, :], ALU.add))
            nc.gpsimd.tensor_copy(ssum[:, 0, :], x2sq[:, 0, :]).then_inc(s("x2_sum"), 1)

        @block.scalar
        def _(act):
            own = Chain(act, act_own)
            A = nc.scalar.activation

            def split(p0, per, i, j, n=PANEL, uq=False):
                if p0 + j >= PANELS and isinstance(i, int) and i == 0:
                    return
                act.wait_ge(raw_in[slot(p0, j, RAW)], raw_value(p0, per, i, j))
                if p0 + j >= SPL:
                    act.wait_ge(used, after(p0, per, i, j) - SPL)
                hi, src = whi[slot(p0, j, SPL)], raw[slot(p0, j, RAW)]
                if uq:
                    for part in UQ_PARTS:
                        last = A(uq_part(hi, *part, False), uq_part(src, *part, True), ACT.Copy)
                else:
                    last = A(hi[:, 0:n], src[:, 0:n], ACT.Copy)
                last.then_inc(hi_done, 1)

            def panel_over(p0, per, i, j, uq=False):
                split(p0, per, i, j + SPL, uq=uq)
                act.wait_ge(used, after(p0, per, i, j))

            def rstd(o, sums, n):
                own.link(A(o, sums, ACT.Ln, bias=EPS, scale=1.0 / n))
                return A(o, o, ACT.Exp, scale=-0.5)

            for f in range(KT):
                act.wait_ge(s("x_turned"), f + 1)
                A(xT[:, f, :], psum[:, f % 4, 0:L], ACT.Copy).then_inc(s("xT_out"), 1)
            act.wait_ge(s("x_sums"), 1)
            rstd(r1[:, :], psum[:, 4, 0:L], D).then_inc(s("r1_done"), 1)
            for q in range(4):
                act.wait_ge(s("h_done"), q + 1)
                A(h_hi[:, 4 * q:4 * q + 4, :], xT[:, 4 * q:4 * q + 4, :], ACT.Copy).then_inc(s("h_hi_done"), 1)
                if q == 0:
                    act.wait_ge(s("lr_in"), 16)
                    split(0, 1, 0, 0, KT * (RANK + ROPE))
                if q == 1:
                    split(0, 1, 0, 1)
            panel_over(0, 1, 0, 0)
            A(lrT[:, :], psum[0:RANK, 0, 0:L], ACT.Copy).then_inc(s("lr_out"), 1)
            A(kr[:, :], psum[0:ROPE, 1, 0:L], ACT.Copy).then_inc(s("kr_out"), 1)
            for b in range(4):
                side, lo, n = (0, META, SEQ) if b < 2 else (1, 0, L)
                for kh in range(2):
                    panel_over(P_LAT, 8, 0, 2 * b + kh, uq=b == 3 and kh == 0)
                A(lat[:, side, 2 * (b % 2):2 * (b % 2) + 2, lo:L], pair(2 * (b % 2), n), ACT.Copy).then_inc(s("lat_out"), 1)
                if b % 2:
                    act.wait_ge(s("lat_sums"), side + 1)
                    rstd(rlat[:, side, lo:L], psum[:, 6 + side, 0:n], LORA).then_inc(s("rlat_done"), 1)
                    act.wait_ge(s("lat_done"), side + 1)
                    A((cq_hi if side == 0 else ckv_hi)[:, :, :], lat[:, side, :, lo:L], ACT.Copy).then_inc(s("lat_hi"), 1)

            def pt_out(i):
                act.wait_ge(s("p_turned"), i)
                wait(act, s("pv_done"), i - 1)
                A(pt0[:, :, :], psum[0:META, 6:8, 0:SEQ], ACT.Copy)
                A(pt1[:, :, :], psum[:, 6:8, SEQ:2 * SEQ], ACT.Copy)
                A(pt2[:, :, :], psum[:, 4, 0:2 * P].rearrange("p (h q) -> p h q", h=2), ACT.Copy).then_inc(s("pt_out"), 1)

            def om_out(i):
                act.wait_ge(s("pv_done"), i)
                dst = o_mla[:, bass.ds(i * 2 - 2, 2), :]
                A(dst, psum[:, 5, :].rearrange("p (h q) -> p h q", h=2), ACT.Copy).then_inc(s("om_out"), 1)

            def mla_turn(i, first, last):
                panel_over(P_MLA, N_MLA, i, 0)
                A(qn[:, :, :], psum[:, 0, :].rearrange("p (h q) -> p h q", h=2), ACT.Copy).then_inc(s("qn_out"), 1)
                if not first:
                    pt_out(i)
                panel_over(P_MLA, N_MLA, i, 1)
                A(qr[:, :], psum[:, 1, 0:SEQ], ACT.Copy).then_inc(s("qr_out"), 1)
                A(qrg[:, :], psum[:, 1, 0:SEQ], ACT.Copy, scale=gain[:, G_QR:G_QR + 1]).then_inc(s("qrg_out"), 1)
                A(kn[:, :, :], pair(2, L), ACT.Copy).then_inc(s("kn_out"), 1)
                if not first:
                    om_out(i)
                A(vm0[:, :, :], psum[0:META, 1, SEQ:2 * SEQ].rearrange("p (h d) -> p h d", h=2), ACT.Copy)
                A(vm[:, :, :, :].rearrange("p t h d -> p (t h d)"), psum[:, 7, :], ACT.Copy).then_inc(s("vm_out"), 1)
                panel_over(P_MLA, N_MLA, i, 2, uq=not last)
                act.wait_ge(s("norm_sums"), i + 1)
                own.link(A(rq[:, :, :], psum[:, 4, :].rearrange("p (h q) -> p h q", h=2), ACT.Ln, bias=EPS, scale=1.0 / QK))
                A(rq[:, :, :], rq[:, :, :], ACT.Exp, scale=-0.5).then_inc(s("rq_done"), 1)
                own.link(A(rk[:, :, :], pair(5, L), ACT.Ln, bias=EPS, scale=1.0 / QK))
                A(rk[:, :, :], rk[:, :, :], ACT.Exp, scale=-0.5).then_inc(s("rk_done"), 1)
                panel_over(P_MLA, N_MLA, i, 3)
                A(zb[:, bass.ds(i * 2, 2), :], pair(0, SEQ), ACT.Copy).then_inc(s("zb_out"), 1)
                act.wait_ge(s("nb_done"), i + 1)
                for h in range(2):
                    A(sc0[:, h, :], sc0[:, h, :], ACT.Exp, bias=nb[:, 2 * h:2 * h + 1], scale=QK ** -0.5,
                      accum_out=sm[:, 2 * h:2 * h + 1])
                    A(sc1[:, h, :], sc1[:, h, :], ACT.Exp, bias=nb[:, 2 * h + 1:2 * h + 2], scale=QK ** -0.5,
                      accum_out=sm[:, 2 * h + 1:2 * h + 2]).then_inc(s("p_exp"), 1)

            own.enter(0, 2)
            mla_turn(0, True, False)
            own.leave(1)
            with act.Fori(1, PAIRS - 1) as i:
                own.enter(i - 1, 2)
                mla_turn(i, False, False)
            own.leave(PAIRS - 2)
            own.enter(0, 2)
            mla_turn(PAIRS - 1, False, True)
            own.leave(1)

            def gla_turn(i, per):
                own.enter(i, per)
                panel_over(P_GLA, N_GLA, i, 0)
                act.wait_ge(s("logits"), i + 1)
                for dt in range(2):
                    bias = gain[:, bass.ds(i * 2 + (G_B + dt), 1)]
                    A(gx[:, dt, :], psum[:, 6 + dt, 0:L], ACT.Identity, bias=bias)
                    last = A(gl[:, dt, :], psum[:, 6 + dt, 0:L], ACT.Abs, bias=bias)
                last.then_inc(s("logits_out"), 1)
                act.wait_ge(s("logits_out"), i + 1)
                own.link(A(gl[:, :, :], gl[:, :, :], ACT.Exp, scale=-1.0))
                A(gl[:, :, :], gl[:, :, :], ACT.Ln, bias=1.0).then_inc(s("gl_done"), 1)
                panel_over(P_GLA, N_GLA, i, 1)
                act.wait_ge(s("decay"), i + 1)
                A(eb[:, :, :], gb[:, :, :], ACT.Exp, scale=1.0 / TAU)
                A(enb[:, :, :], gb[:, :, :], ACT.Exp, scale=-1.0 / TAU)
                kr3 = kf[:, :, 0:META + 3 * CHUNK]
                A(kr3, kr3, ACT.Exp, scale=1.0 / TAU).then_inc(s("decay_exp"), 1)
                for j in (2, 3, 4, 5):
                    panel_over(P_GLA, N_GLA, i, j)
                vout = nc.scalar.activation
                wait(act, s("o_added"), i)
                vout(va[:, :, 0:256], pair(0, 256), ACT.Copy)
                vout(va0[:, 0:256], psum[0:META, 4, 0:256], ACT.Copy).then_inc(s("v_out"), 1)
                act.wait_ge(s("kd_turned"), i + 1)
                A(kdn[:, 0, :], psum[:, 6, 0:DK], ACT.Copy)
                A(kdn0[:, :], psum[0:META, 6, DK:2 * DK], ACT.Copy)
                A(kdn[0:CHUNK, 1, :], psum[0:CHUNK, 7, 0:DK], ACT.Copy).then_inc(s("kdn_out"), 1)
                panel_over(P_GLA, N_GLA, i, 6)
                panel_over(P_GLA, N_GLA, i, 7)
                vout(va[:, :, 256:512], pair(2, 256), ACT.Copy)
                vout(va0[:, 256:512], psum[0:META, 5, 0:256], ACT.Copy).then_inc(s("v_out"), 1)
                panel_over(P_GLA, N_GLA, i, 8)
                panel_over(P_GLA, N_GLA, i, 9)
                wait(act, s("gated"), i)
                A(sr[:, 0:2, :], pair(0, SEQ), ACT.Silu).then_inc(s("sr_out"), 1)
                panel_over(P_GLA, N_GLA, i, 10)
                act.wait_ge(s("o_added"), i + 1)
                A(o_gla[:, bass.ds(i * 4, 4), :], psum[:, 6:8, :].rearrange("p b (v q) -> p (b v) q", q=SEQ), ACT.Copy).then_inc(s("o_out"), 1)
                panel_over(P_GLA, N_GLA, i, 11)
                A(sr[:, 2:4, :], pair(2, SEQ), ACT.Silu).then_inc(s("sr_out"), 1)
                act.wait_ge(s("o_sums"), i + 1)
                own.link(A(ro, psum[:, 4, 0:SEQ], ACT.Ln, bias=EPS, scale=1.0 / DV))
                A(ro, ro, ACT.Exp, scale=-0.5).then_inc(s("ro_done"), 1)

            pt_out(PAIRS)
            om_out(PAIRS)
            with act.Fori(0, GLA_HEADS) as i:
                gla_turn(i, 2)
            own.leave(GLA_HEADS)

            act.wait_ge(s("gated"), GLA_HEADS)
            for n, (dst, src) in enumerate(((o_hi_g, o_gla), (o_hi_m, o_mla))):
                for q in range(4):
                    A(dst[:, 4 * q:4 * q + 4, :], src[:, 4 * q:4 * q + 4, :], ACT.Copy).then_inc(s("o_hi"), 1)
            with act.Fori(0, 4) as i:
                for b in range(2):
                    blk = i * 2 + b
                    for j in range(2):
                        panel_over(P_MRG, N_MRG, i, 6 * b + j)
                    wait(act, s("merged"), blk)
                    A(sa[:, :, :], pair(0, SEQ), ACT.Sigmoid).then_inc(s("sa_done"), 1)
                    A(sb[:, :, :], zb[:, bass.ds(i * 4 + 2 * b, 2), :], ACT.Sigmoid).then_inc(s("sb_done"), 1)
                    for j in range(2, 6):
                        panel_over(P_MRG, N_MRG, i, 6 * b + j)
                    act.wait_ge(s("mf_done"), blk + 1)
                    A(m_hi[:, bass.ds(i * 4 + 2 * b, 2), :], mf[:, :, :], ACT.Copy).then_inc(s("m_hi_done"), 1)
            with act.Fori(0, 4) as i:
                for j in range(4):
                    panel_over(P_OUT, N_OUT, i, j)
            act.wait_ge(s("x2_sums"), 1)
            rstd(r2[:, :], psum[:, 4, 0:SEQ], D).then_inc(s("r2_done"), 1)
            for q in range(4):
                act.wait_ge(s("h2_done"), q + 1)
                A(h2_hi[:, 4 * q:4 * q + 4, :], h2f[:, :, :], ACT.Copy).then_inc(s("h2_hi_done"), 1)
            with act.Fori(0, FF // 256) as i:
                panel_over(P_FF, N_FF, i, 0)
                panel_over(P_FF, N_FF, i, 1)
                wait(act, s("af_done"), i)
                A(sg[:, :, :], pair(0, SEQ), ACT.Silu).then_inc(s("sg_done"), 1)
                panel_over(P_FF, N_FF, i, 2)
                panel_over(P_FF, N_FF, i, 3)
                act.wait_ge(s("af_done"), i + 1)
                A(a_hi[:, bass.ds(i * 2, 2), :], af[:, :, :], ACT.Copy).then_inc(s("a_hi_done"), 1)
            last_turn = FT // 4 - 1
            with act.Fori(0, last_turn) as i:
                for c in range(4):
                    panel_over(P_DN, N_DN, i, c)
            for c in range(2):
                split(P_DN, N_DN, last_turn, c + 2)
            for c in range(4):
                act.wait_ge(s("y_turned"), c + 1)
                if c >= 2:
                    act.wait_ge(s(f"out_done{c - 2}"), 16)
                A(yn[:, c % 2, 0, :], psum[:, 2 * c, :], ACT.Copy).then_inc(s("yn_done"), 1)
                A(yn[:, c % 2, 1, :], psum[:, 2 * c + 1, :], ACT.Copy).then_inc(s("yn_done"), 1)

        @block.vector
        def _(dve):
            own = Chain(dve, dve_own)
            V = nc.vector

            def split(p0, per, i, j, n=PANEL, uq=False):
                dve.wait_ge(hi_done, after(p0, per, i, j))
                k = slot(p0, j, SPL)
                lo, hi, src = wlo[k], whi[k], raw[slot(p0, j, RAW)]
                if uq:
                    for part in UQ_PARTS:
                        last = V.tensor_tensor(uq_part(lo, *part, False), uq_part(src, *part, True),
                                               uq_part(hi, *part, False).bitcast(F32), ALU.subtract)
                else:
                    last = V.tensor_tensor(lo[:, 0:n], src[:, 0:n], hi[:, 0:n].bitcast(F32), ALU.subtract)
                last.then_inc(lo_done, 1)

            def panel_over(p0, per, i, j, uq=False):
                split(p0, per, i, j + SPL, uq=uq)
                dve.wait_ge(used, after(p0, per, i, j))

            for f in range(KT):
                dve.wait_ge(s("xT_out"), f + 1)
                V.tensor_tensor(xsq[:, f, :], xT[:, f, :], xT[:, f, :], ALU.mult).then_inc(s("x_sq"), 1)
            dve.wait_ge(s("r1_done"), 1)
            dve.wait_ge(s("gain_in"), 16)
            for q in range(4):
                for f in range(4 * q, 4 * q + 4):
                    last = V.scalar_tensor_tensor(xT[:, f, :], xT[:, f, :], gain[:, G_1 + f:G_1 + f + 1], r1[:, :],
                                                  ALU.mult, ALU.mult)
                last.then_inc(s("h_done"), 1)
            for q in range(4):
                dve.wait_ge(s("h_hi_done"), q + 1)
                V.tensor_tensor(h_lo[:, 4 * q:4 * q + 4, :], xT[:, 4 * q:4 * q + 4, :],
                                h_hi[:, 4 * q:4 * q + 4, :].bitcast(F32), ALU.subtract).then_inc(s("h_lo_done"), 1)
                if q == 0:
                    split(0, 1, 0, 0, KT * (RANK + ROPE))
                if q == 1:
                    split(0, 1, 0, 1)
            panel_over(0, 1, 0, 0)
            dve.wait_ge(s("kr_out"), 1)
            V.tensor_tensor(krsq[:, :], kr[:, :], kr[:, :], ALU.mult).then_inc(s("kr_sq"), 1)
            V.tensor_scalar(krg[:, :], kr[:, :], gain[0:ROPE, G_KR:G_KR + 1], None, ALU.mult).then_inc(s("krg_done"), 1)
            for b in range(4):
                side, lo = (0, META) if b < 2 else (1, 0)
                for kh in range(2):
                    panel_over(P_LAT, 8, 0, 2 * b + kh, uq=b == 3 and kh == 0)
                if b == 0:
                    dve.wait_ge(s("kr_dup"), 1)
                    dve.wait_ge(s("const_cos2"), 16)
                    dve.wait_ge(s("const_sin2"), 16)
                    V.tensor_tensor(krc[:, :], cos2[:, :], psum[:, 4, 0:L], ALU.mult)
                    own.link(V.tensor_tensor(krn[:, :], sin2[:, :], psum[:, 5, 0:L], ALU.mult))
                    V.tensor_tensor(krr[:, :], krc[:, :], krn[:, :], ALU.add).then_inc(s("krr_done"), 1)
                dve.wait_ge(s("lat_out"), b + 1)
                t = slice(2 * (b % 2), 2 * (b % 2) + 2)
                V.tensor_tensor(latsq[:, side, t, lo:L], lat[:, side, t, lo:L], lat[:, side, t, lo:L],
                                ALU.mult).then_inc(s("lat_sq"), 1)
                if b % 2:
                    dve.wait_ge(s("rlat_done"), side + 1)
                    g0 = G_QA if side == 0 else G_KVA
                    for k in range(LT):
                        last = V.scalar_tensor_tensor(lat[:, side, k, lo:L], lat[:, side, k, lo:L],
                                                      gain[:, g0 + k:g0 + k + 1], rlat[:, side, lo:L], ALU.mult, ALU.mult)
                    last.then_inc(s("lat_done"), 1)
                    dve.wait_ge(s("lat_hi"), side + 1)
                    hi, lw = (cq_hi, cq_lo) if side == 0 else (ckv_hi, ckv_lo)
                    V.tensor_tensor(lw[:, :, :], lat[:, side, :, lo:L], hi[:, :, :].bitcast(F32),
                                    ALU.subtract).then_inc(s("lat_lo"), 1)

            def half(h):
                return slice(ROPE * h, ROPE * h + ROPE)

            def mla_turn(i, last_one):
                panel_over(P_MLA, N_MLA, i, 0)
                panel_over(P_MLA, N_MLA, i, 1)
                panel_over(P_MLA, N_MLA, i, 2, uq=not last_one)
                dve.wait_ge(s("norm_sums"), i + 1)
                dve.wait_ge(s("qrg_out"), i + 1)
                V.tensor_tensor(qc[:, :], qrg[:, :], cos2[:, META:L], ALU.mult)
                own.link(V.tensor_tensor(qsn[:, :], sin2[:, META:L], psum[:, 7, 0:SEQ], ALU.mult))
                own.link(V.tensor_tensor(qc[:, :], qc[:, :], qsn[:, :], ALU.add))
                dve.wait_ge(s("rq_done"), i + 1)
                for h in range(2):
                    V.scalar_tensor_tensor(qs[:, h, :], qn[:, h, :], gain[:, G_QN:G_QN + 1], rq[:, h, :], ALU.mult, ALU.mult)
                    V.tensor_tensor(qrs[half(h), :], qc[half(h), :], rq[half(h), h, :], ALU.mult)
                dve.wait_ge(s("rk_done"), i + 1)
                for h in range(2):
                    V.scalar_tensor_tensor(ks[:, h, :], kn[:, h, :], gain[:, G_KN:G_KN + 1], rk[:, h, :], ALU.mult, ALU.mult)
                    last = V.tensor_tensor(krs[half(h), h, :], krr[half(h), :], rk[half(h), h, :], ALU.mult)
                last.then_inc(s("qk_done"), 1)
                panel_over(P_MLA, N_MLA, i, 3)
                dve.wait_ge(s("scores"), i + 1)
                wait(dve, s("p_turned"), i)
                dve.wait_ge(s("const_causal"), 16)
                V.memset(tick[:, :], 0.0)
                for h in range(2):
                    V.tensor_tensor_reduce(out=sc0[:, h, :], in0=psum[:, 4 + h, 0:META + P], in1=causal[:, P:L], scale=1.0,
                                           scalar=-3e38, op0=ALU.add, op1=ALU.max, accum_out=mx[:, 2 * h:2 * h + 1])
                    last = V.tensor_tensor_reduce(out=sc1[:, h, :], in0=psum[:, 4 + h, META + P:META + P + L], in1=causal[:, :],
                                                  scale=1.0, scalar=-3e38, op0=ALU.add, op1=ALU.max,
                                                  accum_out=mx[:, 2 * h + 1:2 * h + 2])
                own.link(last)
                V.tensor_scalar(nb[:, :], mx[:, :], -(QK ** -0.5), None, ALU.mult).then_inc(s("nb_done"), 1)
                dve.wait_ge(s("p_exp"), 2 * i + 2)
                own.link(V.reciprocal(rs[:, :], sm[:, :]))
                for h in range(2):
                    V.tensor_scalar(sc0[:, h, :], sc0[:, h, :], rs[:, 2 * h:2 * h + 1], None, ALU.mult)
                    last = V.tensor_scalar(sc1[:, h, :], sc1[:, h, :], rs[:, 2 * h + 1:2 * h + 2], None, ALU.mult)
                last.then_inc(s("p_done"), 1)

            for h in range(2):
                V.memset(krs[half(1 - h), h, :], 0.0)
            with dve.Fori(0, PAIRS - 1) as i:
                own.enter(i, 4)
                mla_turn(i, False)
            own.leave(PAIRS - 1)
            own.enter(0, 4)
            mla_turn(PAIRS - 1, True)
            own.leave(1)

            dve.wait_ge(s("om_out"), PAIRS)
            dve.wait_ge(s("const_keep"), 16)
            own.link(V.memset(am[:, :, :], 0.0))

            def gla_turn(i):
                own.enter(i, 6)
                panel_over(P_GLA, N_GLA, i, 0)
                dve.wait_ge(s("gl_done"), i + 1)
                own.link(V.scalar_tensor_tensor(gx[:, :, :], gx[:, :, :], 0.0, gl[:, :, :], ALU.min, ALU.subtract))
                for dt in range(2):
                    last = V.tensor_tensor_scan(gb[:, dt, :], keep[:, :], gx[:, dt, :], 0.0, ALU.mult, ALU.add)
                own.link(last)
                for dt in range(2):
                    V.tensor_tensor(kf[:, dt, 0:META], gb[:, dt, META - 1:META].broadcast_to([P, META]),
                                    gb[:, dt, 0:META], ALU.subtract)
                    g3 = gb[:, dt, META:META + 3 * CHUNK].rearrange("p (c t) -> p c t", t=CHUNK)
                    last = V.tensor_tensor(kf[:, dt, META:META + 3 * CHUNK].rearrange("p (c t) -> p c t", t=CHUNK),
                                           g3[:, :, CHUNK - 1:CHUNK].broadcast_to([P, 3, CHUNK]), g3, ALU.subtract)
                last.then_inc(s("decay"), 1)
                panel_over(P_GLA, N_GLA, i, 1)
                dve.wait_ge(s("decay_exp"), i + 1)
                V.tensor_tensor(ke[:, :, :], enb[:, :, :], pair(0, L), ALU.mult)
                n = META + 3 * CHUNK
                V.tensor_tensor(kd[:, :, 0:n], kf[:, :, 0:n], pair(0, n), ALU.mult).then_inc(s("kd_done"), 1)
                panel_over(P_GLA, N_GLA, i, 2)
                panel_over(P_GLA, N_GLA, i, 3)
                V.scalar_tensor_tensor(qd[:, :, :], pair(2, SEQ), DK ** -0.5, eb[:, :, META:L], ALU.mult,
                                       ALU.mult).then_inc(s("qd_done"), 1)
                panel_over(P_GLA, N_GLA, i, 4)
                panel_over(P_GLA, N_GLA, i, 5)
                dve.wait_ge(s("a_in"), i + 1)
                dve.wait_ge(s("const_inchunk"), 16)
                V.memset(tick[:, :], 0.0)
                for c in range(2):
                    last = V.copy_predicated(am[:, c, :], inchunk[:, :], psum[:, 5, c * P:(c + 1) * P])
                last.then_inc(s("am_done"), 1)
                panel_over(P_GLA, N_GLA, i, 6)
                panel_over(P_GLA, N_GLA, i, 7)
                panel_over(P_GLA, N_GLA, i, 8)
                for c in range(4):
                    for dt in range(2):
                        n = 2 * c + dt
                        dve.wait_ge(s("ds_in"), i * 8 + (n + 1))
                        src = psum[:, (6, 7, 4, 5)[n % 4], :]
                        if c == 0:
                            ins = V.tensor_copy(st[:, 0, dt, :], src)
                        else:
                            end = META + c * CHUNK - 1
                            ins = V.scalar_tensor_tensor(st[:, c, dt, :], st[:, c - 1, dt, :], eb[:, dt, end:end + 1], src,
                                                         ALU.mult, ALU.add)
                        ins.then_inc(s("st_done"), 1)
                        dve.wait_ge(s("st_done"), i * 8 + (n + 1))
                panel_over(P_GLA, N_GLA, i, 9)
                panel_over(P_GLA, N_GLA, i, 10)
                panel_over(P_GLA, N_GLA, i, 11)
                dve.wait_ge(s("ro_done"), i + 1)
                for v in range(4):
                    ov = o_gla[:, bass.ds(i * 4 + v, 1), :].rearrange("p a q -> p (a q)")
                    own.link(V.scalar_tensor_tensor(ov, ov, gain[:, G_O + v:G_O + v + 1], ro, ALU.mult, ALU.mult))
                dve.wait_ge(s("sr_out"), i * 2 + 2)
                og = o_gla[:, bass.ds(i * 4, 4), :]
                V.tensor_tensor(og, og, sr[:, :, :], ALU.mult).then_inc(s("gated"), 1)

            with dve.Fori(0, GLA_HEADS) as i:
                gla_turn(i)
            own.leave(GLA_HEADS)

            for n, (dst, src, hi) in enumerate(((o_lo_g, o_gla, o_hi_g), (o_lo_m, o_mla, o_hi_m))):
                for q in range(4):
                    t = slice(4 * q, 4 * q + 4)
                    dve.wait_ge(s("o_hi"), 4 * n + q + 1)
                    V.tensor_tensor(dst[:, t, :], src[:, t, :], hi[:, t, :].bitcast(F32), ALU.subtract).then_inc(s("o_lo"), 1)
            with dve.Fori(0, 4) as i:
                own.enter(i, 4)
                for b in range(2):
                    blk = i * 2 + b
                    for j in range(4):
                        panel_over(P_MRG, N_MRG, i, 6 * b + j)
                    dve.wait_ge(s("sa_done"), blk + 1)
                    own.link(V.tensor_tensor(mf[:, :, :], sa[:, :, :], pair(2, SEQ), ALU.mult))
                    for j in range(4, 6):
                        panel_over(P_MRG, N_MRG, i, 6 * b + j)
                    dve.wait_ge(s("sb_done"), blk + 1)
                    own.link(V.tensor_tensor(mb[:, :, :], sb[:, :, :], pair(4, SEQ), ALU.mult))
                    V.tensor_tensor(mf[:, :, :], mf[:, :, :], mb[:, :, :], ALU.add).then_inc(s("mf_done"), 1)
                    dve.wait_ge(s("m_hi_done"), blk + 1)
                    t = bass.ds(i * 4 + 2 * b, 2)
                    V.tensor_tensor(m_lo[:, t, :], mf[:, :, :], m_hi[:, t, :].bitcast(F32), ALU.subtract).then_inc(s("merged"), 1)
            own.leave(4)
            with dve.Fori(0, 4) as i:
                for b in range(2):
                    for kh in range(2):
                        panel_over(P_OUT, N_OUT, i, 2 * b + kh)
                    V.tensor_copy(x2[:, bass.ds(i * 4 + 2 * b, 2), :], pair(2 * b, SEQ)).then_inc(s(f"x2_out{b}"), 1)
            dve.wait_ge(s("r2_done"), 1)
            for q in range(4):
                for f in range(4):
                    last = V.scalar_tensor_tensor(h2f[:, f, :], x2[:, 4 * q + f, :], gain[:, G_2 + 4 * q + f:G_2 + 4 * q + f + 1],
                                                  r2[:, :], ALU.mult, ALU.mult)
                last.then_inc(s("h2_done"), 1)
                dve.wait_ge(s("h2_hi_done"), q + 1)
                V.tensor_tensor(h2_lo[:, 4 * q:4 * q + 4, :], h2f[:, :, :],
                                h2_hi[:, 4 * q:4 * q + 4, :].bitcast(F32), ALU.subtract).then_inc(s("h2_lo_done"), 1)
                dve.wait_ge(s("h2_lo_done"), q + 1)
            with dve.Fori(0, FF // 256) as i:
                for j in range(4):
                    panel_over(P_FF, N_FF, i, j)
                dve.wait_ge(s("sg_done"), i + 1)
                wait(dve, s("a_lo_done"), i)
                V.tensor_tensor(af[:, :, :], sg[:, :, :], pair(2, SEQ), ALU.mult).then_inc(s("af_done"), 1)
                dve.wait_ge(s("a_hi_done"), i + 1)
                t = bass.ds(i * 2, 2)
                V.tensor_tensor(a_lo[:, t, :], af[:, :, :], a_hi[:, t, :].bitcast(F32), ALU.subtract).then_inc(s("a_lo_done"), 1)
            last_turn = FT // 4 - 1
            with dve.Fori(0, last_turn) as i:
                for c in range(4):
                    panel_over(P_DN, N_DN, i, c)
            for c in range(4):
                if c < 2:
                    split(P_DN, N_DN, last_turn, c + 2)
                dve.wait_ge(used, after(P_DN, N_DN, last_turn, c))
                if c >= 2:
                    dve.wait_ge(s("y_turned"), c - 1)
                V.tensor_tensor(yT[:, c % 2], x2[:, 4 * c:4 * c + 4, :],
                                psum[:, 2 * c:2 * c + 2, :].rearrange("p b (v q) -> p (b v) q", q=SEQ), ALU.add).then_inc(s("y_done"), 1)

        @block.tensor
        def _(pe):
            M = nc.tensor.matmul

            def three(o, a, b, start, stop, skip=False):
                M(o, a[0], b[0], start=start, stop=False, skip_group_check=skip)
                M(o, a[0], b[1], start=False, stop=False, skip_group_check=skip)
                return M(o, a[1], b[0], start=False, stop=stop, skip_group_check=skip)

            def panel(p0, per, i, j):
                pe.wait_ge(lo_done, after(p0, per, i, j))
                k = slot(p0, j, SPL)
                return whi[k], wlo[k]

            def wide(p0, per, i, j, kh, b0, src, lo=META, start=True):
                hi_lo = [w[:, :].rearrange("p (k c) -> p k c", k=8) for w in panel(p0, per, i, j)]
                n = L - lo if src is h_pair else SEQ
                for k in range(8):
                    kk = 8 * kh + k
                    rhs = [t[:, kk, lo:L] if src is h_pair else t[:, kk, :] for t in src]
                    for m in range(2):
                        lhs = [w[:, k, m * P:(m + 1) * P] for w in hi_lo]
                        last = three(psum[:, b0 + m, 0:n], lhs, rhs, start and kh == 0 and k == 0, kh == 1 and k == 7)
                last.then_inc(used, 1)

            h_pair = (h_hi, h_lo)

            pe.wait_ge(s("ident_in"), 16)
            pe.wait_ge(s("xm_in"), 16)

            def x_sum(f):
                pe.wait_ge(s("x_sq"), f + 1)
                return M(psum[:, 4, 0:L], ones[:, :], xsq[:, f, :], start=f == 0, stop=f == KT - 1)

            pe.wait_ge(s("ones_set"), 1)
            for f in range(KT):
                if f % 4 == 0:
                    pe.wait_ge(s(f"xn_in{f // 4}"), 16)
                if f >= 4:
                    pe.wait_ge(s("xT_out"), f - 3)
                cols = slice(f * P, (f + 1) * P)
                nc.tensor.transpose(psum[:, f % 4, 0:META], xm[:, cols], ident[0:META, 0:META])
                for t in range(2):
                    last = nc.tensor.transpose(psum[:, f % 4, META + t * P:META + (t + 1) * P], xn[:, t, cols], ident[:, :])
                last.then_inc(s("x_turned"), 1)
                if f >= 4:
                    x_sum(f - 4)
            for f in range(KT - 4, KT):
                last = x_sum(f)
            last.then_inc(s("x_sums"), 1)

            hi_lo = [w[:, 0:KT * (RANK + ROPE)].rearrange("p (k c) -> p k c", k=KT) for w in panel(0, 1, 0, 0)]
            for k in range(KT):
                if k % 4 == 0:
                    pe.wait_ge(s("h_lo_done"), k // 4 + 1)
                rhs = [t[:, k, :] for t in h_pair]
                three(psum[0:RANK, 0, 0:L], [w[:, k, 0:RANK] for w in hi_lo], rhs, k == 0, k == KT - 1)
                last = three(psum[0:ROPE, 1, 0:L], [w[:, k, RANK:] for w in hi_lo], rhs, k == 0, k == KT - 1)
            last.then_inc(used, 1)

            def lat_sum(side):
                lo = META if side == 0 else 0
                pe.wait_ge(s("lat_sq"), 2 * side + 2)
                for k in range(LT):
                    last = M(psum[:, 6 + side, 0:L - lo], ones[:, :], latsq[:, side, k, lo:L], start=k == 0, stop=k == LT - 1)
                last.then_inc(s("lat_sums"), 1)

            for b in range(4):
                if b > 1:
                    pe.wait_ge(s("lat_out"), b - 1)
                if b == 0:
                    pe.wait_ge(s("kr_out"), 1)
                for kh in range(2):
                    wide(P_LAT, 8, 0, 2 * b + kh, kh, 2 * (b % 2), h_pair, META if b < 2 else 0)
                    if b == 0 and kh == 0:
                        pe.wait_ge(s("krg_done"), 1)
                        pe.wait_ge(s("const_dup"), 16)
                        M(psum[:, 4, 0:L], dup[:, 0, :], krg[:, :], start=True, stop=True)
                        M(psum[:, 5, 0:L], dup[:, 1, :], krg[:, :], start=True, stop=True).then_inc(s("kr_dup"), 1)
                    if b == 2 and kh == 0:
                        lat_sum(0)
            lat_sum(1)

            def mla_norms(i):
                pe.wait_ge(s("mla_sq"), 3 * i + 3)
                for h in range(2):
                    o = psum[:, 4, h * SEQ:(h + 1) * SEQ]
                    M(o, ones[:, :], qnsq[:, h, :], start=True, stop=False)
                    M(o, halves[:, h, :], qrsq[:, :], start=False, stop=True)
                    o = psum[:, 5 + h, 0:L]
                    M(o, ones[:, :], knsq[:, h, :], start=True, stop=False)
                    M(o, ones[0:ROPE, :], krsq[:, :], start=False, stop=True)
                pe.wait_ge(s("vm_out"), i + 1)
                M(psum[:, 7, 0:SEQ], rot2[:, :], qrg[:, :], start=True, stop=True).then_inc(s("norm_sums"), 1)

            def mla_scores(i):
                pe.wait_ge(s("qk_done"), i + 1)
                for h in range(2):
                    for t, (c0, n) in enumerate(((0, META + P), (META + P, L))):
                        o = psum[:, 4 + h, c0:c0 + n]
                        q = slice(t * P, (t + 1) * P)
                        M(o, qs[:, h, q], ks[:, h, 0:n], start=True, stop=False)
                        last = M(o, qrs[:, q], krs[:, h, 0:n], start=False, stop=True)
                last.then_inc(s("scores"), 1)

            def mla_turn_p(i):
                T = nc.tensor.transpose
                pe.wait_ge(s("p_done"), i)
                for h in range(2):
                    for t, sc in enumerate((sc0, sc1)):
                        q = slice(t * P, (t + 1) * P)
                        T(psum[0:META, 6 + h, q], sc[:, h, 0:META], ident[:, :])
                        T(psum[:, 6 + h, SEQ + t * P:SEQ + (t + 1) * P], sc[:, h, META:META + P], ident[:, :])
                    last = T(psum[:, 4, h * P:(h + 1) * P], sc1[:, h, META + P:L], ident[:, :])
                last.then_inc(s("p_turned"), 1)

            def mla_pv(i):
                pe.wait_ge(s("pt_out"), i)
                for h in range(2):
                    o = psum[:, 5, h * SEQ:(h + 1) * SEQ]
                    M(o, vm0[:, h, :], pt0[:, h, :], start=True, stop=False)
                    M(o, vm[:, 0, h, :], pt1[:, h, :], start=False, stop=False)
                    last = M(o[:, P:SEQ], vm[:, 1, h, :], pt2[:, h, :], start=False, stop=True)
                last.then_inc(s("pv_done"), 1)

            def mla_turn(i, first):
                hi_lo = panel(P_MLA, N_MLA, i, 0)
                nope = [uq_part(w, *UQ_PARTS[0], False) for w in hi_lo]
                rope = [w[:, LT * 2 * NOPE:LT * 2 * QK].rearrange("p (k c) -> p k c", k=LT) for w in hi_lo]
                if first:
                    pe.wait_ge(s("lat_lo"), 1)
                    pe.wait_ge(s("lat_out"), 4)
                else:
                    pe.wait_ge(s("zb_out"), i)
                c_q = (cq_hi, cq_lo)
                for h in range(2):
                    for k in range(LT):
                        three(psum[:, 0, h * SEQ:(h + 1) * SEQ], [w[:, k, h, :] for w in nope], [t[:, k, :] for t in c_q],
                              k == 0, k == LT - 1)
                for k in range(LT):
                    last = three(psum[:, 1, 0:SEQ], [w[:, k, :] for w in rope], [t[:, k, :] for t in c_q],
                                 k == 0, k == LT - 1)
                last.then_inc(used, 1)
                if not first:
                    mla_turn_p(i)
                hi_lo = [w[:, :].rearrange("p (k h c) -> p k h c", k=LT, h=2) for w in panel(P_MLA, N_MLA, i, 1)]
                if first:
                    pe.wait_ge(s("lat_lo"), 2)
                for h in range(2):
                    for k in range(LT):
                        three(psum[:, 2 + h, 0:L], [w[:, k, h, 0:NOPE] for w in hi_lo], [ckv_hi[:, k, :], ckv_lo[:, k, :]],
                              k == 0, k == LT - 1)
                if not first:
                    pe.wait_ge(s("pt_out"), i)
                for t, (a, b) in enumerate(TOK):
                    o = psum[0:META, 1, SEQ:2 * SEQ] if t == 0 else psum[:, 7, (t - 1) * SEQ:t * SEQ]
                    o = o.rearrange("p (h d) -> p h d", h=2)
                    for k in range(LT):
                        last = three(o, [ckv_hi[:, k, a:b], ckv_lo[:, k, a:b]], [w[:, k, :, NOPE:] for w in hi_lo],
                                     k == 0, k == LT - 1)
                last.then_inc(used, 1)
                if not first:
                    mla_pv(i)
                pe.wait_ge(s("vm_out"), i + 1)
                wide(P_MLA, N_MLA, i, 2, 0, 0, h_pair)
                if not first:
                    pe.wait_ge(s("om_out"), i)
                mla_norms(i)
                wide(P_MLA, N_MLA, i, 3, 1, 0, h_pair)
                mla_scores(i)

            pe.wait_ge(s("const_rot2"), 16)
            pe.wait_ge(s("const_halves"), 16)
            mla_turn(0, True)
            with pe.Fori(1, PAIRS) as i:
                mla_turn(i, False)
            mla_turn_p(PAIRS)
            mla_pv(PAIRS)

            def values(i, j, kh, b0, bm):
                hi_lo = [w[:, :].rearrange("p (k c) -> p k c", k=8) for w in panel(P_GLA, N_GLA, i, j)]
                for k in range(8):
                    kk = 8 * kh + k
                    for t, (a, b) in enumerate(TOK):
                        o = psum[0:META, bm, 0:256] if t == 0 else psum[:, b0 + t - 1, 0:256]
                        last = three(o, [h_hi[:, kk, a:b], h_lo[:, kk, a:b]], [w[:, k, :] for w in hi_lo],
                                     kk == 0, kk == KT - 1)
                last.then_inc(used, 1)

            def gla_turn(i):
                G = (P_GLA, N_GLA, i)
                wait(pe, s("sr_out"), i * 2)
                wide(*G, 0, 0, 0, h_pair, 0)
                pe.wait_ge(s("w2_in"), i * 16 + 16)
                wait(pe, s("o_out"), i)
                for dt in range(2):
                    last = M(psum[:, 6 + dt, 0:L], w2h[:, dt * P:(dt + 1) * P], lrT[:, :], start=True, stop=True)
                last.then_inc(s("logits"), 1)
                wide(*G, 1, 1, 0, h_pair, 0)
                wide(*G, 2, 0, 2, h_pair)
                wide(*G, 3, 1, 2, h_pair)
                pe.wait_ge(s("kd_done"), i + 1)
                wait(pe, s("ro_done"), i)
                values(i, 4, 0, 0, 4)
                values(i, 5, 1, 0, 4)
                T = nc.tensor.transpose
                for dt in range(2):
                    d = slice(dt * P, (dt + 1) * P)
                    T(psum[:, 6, d], kd[:, dt, META:META + P], ident[:, :])
                    T(psum[0:META, 6, DK + dt * P:DK + (dt + 1) * P], kd[:, dt, 0:META], ident[:, :])
                    last = T(psum[0:CHUNK, 7, d], kd[:, dt, META + P:META + P + CHUNK], ident[:, :])
                last.then_inc(s("kd_turned"), 1)
                pe.wait_ge(s("qd_done"), i + 1)
                for c in range(2):
                    for dt in range(2):
                        last = M(psum[:, 5, c * P:(c + 1) * P], ke[:, dt, META + c * P:META + (c + 1) * P],
                                 qd[:, dt, c * P:(c + 1) * P], start=dt == 0, stop=dt == 1)
                last.then_inc(s("a_in"), 1)
                pe.wait_ge(s("am_done"), i + 1)
                values(i, 6, 0, 2, 5)
                values(i, 7, 1, 2, 5)
                pe.wait_ge(s("v_out"), i * 2 + 1)
                wide(*G, 8, 0, 0, h_pair)
                pe.wait_ge(s("v_out"), i * 2 + 2)
                pe.wait_ge(s("kdn_out"), i + 1)
                for c in range(4):
                    for dt in range(2):
                        n = 2 * c + dt
                        d = slice(dt * P, (dt + 1) * P)
                        if n >= 4:
                            pe.wait_ge(s("st_done"), i * 8 + (n - 3))
                        o = psum[:, (6, 7, 4, 5)[n % 4], :]
                        if c == 0:
                            last = M(o, kdn0[:, d], va0[:, :], start=True, stop=True)
                        else:
                            t, r = (c - 1) // 2, (c - 1) % 2
                            rows = slice(CHUNK * r, CHUNK * r + CHUNK)
                            last = M(o, kdn[rows, t, d], va[rows, t, :], start=True, stop=True)
                        last.then_inc(s("ds_in"), 1)
                wide(*G, 9, 1, 0, h_pair)
                wide(*G, 10, 0, 2, h_pair)
                pe.wait_ge(s("st_done"), i * 8 + 8)
                for v in range(4):
                    vs = slice(v * P, (v + 1) * P)
                    for c in range(2):
                        col = (v % 2) * SEQ + c * P
                        o = psum[:, 6 + v // 2, col:col + P]
                        M(o, va[:, c, vs], am[:, c, :], start=True, stop=False)
                        for r in range(2):
                            q = 2 * c + r
                            for dt in range(2):
                                last = M(o[:, r * CHUNK:(r + 1) * CHUNK], st[:, q, dt, vs],
                                         qd[:, dt, q * CHUNK:(q + 1) * CHUNK], start=False, stop=dt == 1 and r == 1)
                last.then_inc(s("o_added"), 1)
                wide(*G, 11, 1, 2, h_pair)
                pe.wait_ge(s("o_sq"), i + 1)
                for v in range(4):
                    last = M(psum[:, 4, 0:SEQ], ones[:, :], osq[:, v, :], start=v == 0, stop=v == 3)
                last.then_inc(s("o_sums"), 1)

            pe.wait_ge(s("zb_out"), PAIRS)
            pe.wait_ge(s("om_out"), PAIRS)
            with pe.Fori(0, GLA_HEADS) as i:
                gla_turn(i)

            pe.wait_ge(s("sr_out"), 2 * GLA_HEADS)
            pe.wait_ge(s("ro_done"), GLA_HEADS)
            def merge_turn(i, first):
                for b in range(2):
                    G = (P_MRG, N_MRG, i)
                    wait(pe, s("sa_done"), i * 2 + b)
                    for kh in range(2):
                        wide(*G, 6 * b + kh, kh, 0, h_pair)
                    wait(pe, s("mf_done"), i * 2 + b)
                    if first and b == 0:
                        pe.wait_ge(s("o_lo"), 4)
                    for kh in range(2):
                        wide(*G, 6 * b + 2 + kh, kh, 2, (o_hi_g, o_lo_g))
                    if first and b == 0:
                        pe.wait_ge(s("o_lo"), 8)
                    for kh in range(2):
                        wide(*G, 6 * b + 4 + kh, kh, 4, (o_hi_m, o_lo_m))

            merge_turn(0, True)
            with pe.Fori(1, 4) as i:
                merge_turn(i, False)

            pe.wait_ge(s("merged"), 8)
            with pe.Fori(0, 4) as i:
                for b in range(2):
                    pe.wait_ge(s(f"x2_out{b}"), i)
                    for kh in range(2):
                        hi_lo = [w[:, :].rearrange("p (k c) -> p k c", k=8) for w in panel(P_OUT, N_OUT, i, 2 * b + kh)]
                        for k in range(8):
                            kk = 8 * kh + k
                            for m in range(2):
                                last = three(psum[:, 2 * b + m, 0:SEQ], [w[:, k, m * P:(m + 1) * P] for w in hi_lo],
                                             [m_hi[:, kk, :], m_lo[:, kk, :]], kk == 0, False, skip=True)
                        if kh == 0:
                            last.then_inc(used, 1)
                    pe.wait_ge(s(f"xs_in{b}"), i * 16 + 16)
                    for m in range(2):
                        for t in range(2):
                            last = M(psum[:, 2 * b + m, t * P:(t + 1) * P], xs[:, b, t, m * P:(m + 1) * P], ident[:, :],
                                     start=False, stop=t == 1, skip_group_check=True)
                    last.then_inc(used, 1)
            pe.wait_ge(s("x2_sum"), 1)
            M(psum[:, 4, 0:SEQ], ones[:, :], ssum[:, 0, :], start=True, stop=True).then_inc(s("x2_sums"), 1)

            pe.wait_ge(s("h2_lo_done"), 4)
            with pe.Fori(0, FF // 256) as i:
                wait(pe, s("sg_done"), i)
                for kh in range(2):
                    wide(P_FF, N_FF, i, kh, kh, 0, (h2_hi, h2_lo))
                wait(pe, s("af_done"), i)
                for kh in range(2):
                    wide(P_FF, N_FF, i, 2 + kh, kh, 2, (h2_hi, h2_lo))

            def down(i, c, first, last_one):
                hi_lo = [w[:, :].rearrange("p (k c) -> p k c", k=4) for w in panel(P_DN, N_DN, i, c)]
                for m in range(4):
                    o = psum[:, 2 * c + m // 2, (m % 2) * SEQ:(m % 2 + 1) * SEQ]
                    for k in range(4):
                        rhs = [t[:, bass.ds(i * 4 + k, 1), :].rearrange("p a q -> p (a q)") for t in (a_hi, a_lo)]
                        last = three(o, [w[:, k, m * P:(m + 1) * P] for w in hi_lo], rhs,
                                     first and k == 0 and m % 2 == 0, last_one and k == 3, skip=True)
                last.then_inc(used, 1)

            pe.wait_ge(s("a_lo_done"), FF // 256)
            for c in range(4):
                down(0, c, True, False)
            last_turn = FT // 4 - 1
            with pe.Fori(1, last_turn) as i:
                for c in range(4):
                    down(i, c, False, False)

            def turn(c):
                pe.wait_ge(s("y_done"), c + 1)
                for t in range(2):
                    for m in range(4):
                        last = nc.tensor.transpose(psum[:, 2 * c + t, m * P:(m + 1) * P], yT[:, c % 2, m, t * P:(t + 1) * P],
                                                   ident[:, :])
                last.then_inc(s("y_turned"), 1)

            for c in range(4):
                down(last_turn, c, False, True)
                if c:
                    turn(c - 1)
            turn(3)


def tables():
    i = np.arange(P)
    f32 = np.float32
    swap = np.zeros((ROPE, ROPE), f32)
    h = ROPE // 2
    swap[np.arange(h) + h, np.arange(h)] = -1.0
    swap[np.arange(h), np.arange(h) + h] = 1.0
    eye = np.eye(ROPE, dtype=f32)
    causal = np.zeros((P, L), f32)
    causal[:, META + P:] = np.where(i[None, :] <= i[:, None], 0.0, NEG)
    inv = (1.0 / (f32(10000.0) ** (np.arange(0, ROPE, 2, dtype=f32) / f32(ROPE)))).astype(f32)
    ang = np.tile(np.arange(L, dtype=f32)[None, :] * inv[:, None], (4, 1))
    keep = np.ones((P, L), f32)
    keep[:, 0] = 0.0
    keep[:, META::CHUNK] = 0.0
    return {
        "ident": np.eye(P, dtype=f32),
        "rot2": np.kron(np.eye(2, dtype=f32), swap),
        "halves": np.stack([np.repeat(i[:, None] < ROPE, P, 1), np.repeat(i[:, None] >= ROPE, P, 1)], 1).astype(f32),
        "dup": np.stack([np.tile(eye, (1, 2)), np.tile(swap, (1, 2))], 1),
        "causal": causal,
        "cos2": np.cos(ang),
        "sin2": np.sin(ang),
        "inchunk": ((i[:, None] <= i[None, :]) & (i[:, None] // CHUNK == i[None, :] // CHUNK)).astype(np.int32),
        "keep": keep,
    }


def kernel(x, meta_tokens, norm1_g, w_in, gla_gate_w2, gla_gate_b, gla_onorm_g, w_branch_a, q_a_norm_g, w_uq,
           kv_a_norm_g, w_ukv, q_norm_g, k_norm_g, w_branch_b, w_out, norm2_g, w_gate_up, w_down):
    import concourse.bacc as bacc
    from concourse.bass_utils import run_bass_kernel_spmd

    def columns(g):
        return np.asarray(g).reshape(-1, P).T

    qg, kg = np.asarray(q_norm_g)[0], np.asarray(k_norm_g)[0]
    gains = np.concatenate(
        [columns(norm1_g), columns(norm2_g), columns(gla_onorm_g), columns(q_a_norm_g), columns(kv_a_norm_g),
         columns(qg[:NOPE]), columns(np.concatenate([qg[NOPE:], qg[NOPE:]])),
         columns(kg[:NOPE]), columns(np.concatenate([kg[NOPE:], kg[NOPE:]])), columns(gla_gate_b)], axis=1)
    arrays = {
        "x": x, "meta": meta_tokens, "w_in": w_in, "w2": gla_gate_w2, "w_a": w_branch_a, "w_uq": w_uq, "w_ukv": w_ukv,
        "w_b": w_branch_b, "w_out": w_out, "w_gu": w_gate_up, "w_dn": w_down, "gains": gains,
    }
    arrays = {f"in_{n}": np.ascontiguousarray(a) for n, a in arrays.items()}
    fixed = tables()
    arrays |= {f"const_{n}": np.ascontiguousarray(a) for n, a in fixed.items()}
    nc = bacc.Bacc("TRN2", target_bir_lowering=False, num_devices=1)
    ap = {n: nc.dram_tensor(n, a.shape, mybir.dt.from_np(a.dtype), kind="ExternalInput").ap() for n, a in arrays.items()}
    out = nc.dram_tensor("out", (1, SEQ, D), F32, kind="ExternalOutput").ap()

    def two_d(n):
        a = ap[f"in_{n}"]
        return a.rearrange("o k c -> (o k) c")

    build(nc, ap["in_x"], ap["in_meta"], two_d("w_in"), two_d("w2"), two_d("w_a"), two_d("w_uq"), two_d("w_ukv"),
          two_d("w_b"), two_d("w_out"), two_d("w_gu"), two_d("w_dn"), ap["in_gains"],
          {n: ap[f"const_{n}"] for n in fixed}, out)
    r = run_bass_kernel_spmd(nc, [arrays], core_ids=[0])
    return r.results[0]["out"]
```

```python
from contextlib import ExitStack

import numpy as np

import concourse.bass as bass
from concourse import mybir

F32 = mybir.dt.float32
F32R = mybir.dt.float32r
I32 = mybir.dt.int32
ACT = mybir.ActivationFunctionType
ALU = mybir.AluOpType

P = 128
D = 2048
META = 16
SEQ = 256
L = META + SEQ
KT = D // P
EPS = 1e-6
GLA_HEADS, DK, DV, RANK, TAU, CHUNK = 4, 256, 512, 16, 16.0, 64
HEADS, LORA, NOPE, ROPE, DVM = 16, 512, 128, 64, 128
QK = NOPE + ROPE
LT = LORA // P
FF = 5632
FT = FF // P
NEG = -1e30
LN_EXP = "natural_log_exp_and_others"

C_Q, C_K, C_V, C_R = 0, 1024, 2048, 4096
C_LR = 6144
C_CQ = C_LR + RANK
C_CKV = C_CQ + LORA
C_KR = C_CKV + LORA
C_ZA = C_KR + ROPE
C_ZB = C_ZA + D

PANEL = 2048
RAW, SPL = 4, 2
PAIRS = HEADS // 2
P_LAT = 1
P_MLA, N_MLA = P_LAT + 8, 4
P_GLA, N_GLA = P_MLA + N_MLA * PAIRS, 12
P_MRG, N_MRG = P_GLA + N_GLA * GLA_HEADS, 12
P_OUT, N_OUT = P_MRG + N_MRG * 4, 4
P_FF, N_FF = P_OUT + N_OUT * 4, 4
P_DN, N_DN = P_FF + N_FF * (FF // 256), 4
PANELS = P_DN + N_DN * (FT // 4)

G_1, G_2, G_O, G_QA, G_KVA, G_QN, G_QR, G_KN, G_KR, G_B, G_ALL = 0, 16, 32, 36, 40, 44, 45, 46, 47, 48, 56

TOK = ((0, META), (META, META + P), (META + P, L))


def wait(eng, sem, value):
    if isinstance(value, int) and value <= 0:
        return
    eng.wait_ge(sem, value)


class Chain:

    def __init__(self, eng, sem):
        self.eng, self.sem, self.total, self.base, self.k = eng, sem, 0, 0, 0

    def link(self, ins):
        self.k += 1
        ins.then_inc(self.sem, 1)
        self.eng.wait_ge(self.sem, self.base + self.k)

    def enter(self, turn, per):
        self.close()
        self.base, self.per = turn * per + self.total, per

    def leave(self, turns):
        assert self.k == self.per, (self.k, self.per)
        self.total += turns * self.per
        self.base, self.k = self.total, 0

    def close(self):
        self.total += self.k
        self.base, self.k = self.total, 0


def build(nc, x, meta, w_in, w2, w_a, w_uq, w_ukv, w_b, w_out, w_gu, w_dn, gains, consts, out):
    ctx = ExitStack()
    with ctx:
        def sem(name):
            return ctx.enter_context(nc.semaphore(name))

        BASE = 16512
        top = [0]

        def put(name, shape, dt=F32, at=None):
            size = -(-4 * int(np.prod(shape[1:])) // 32) * 32
            if at is None:
                at = top[0]
                top[0] += size
            return nc.alloc_sbuf_tensor_at(name, list(shape), dt, offset=BASE + at)

        raw = [put(f"raw{s}", [P, PANEL]) for s in range(RAW)]
        whi = [put(f"whi{s}", [P, PANEL], F32R) for s in range(SPL)]
        wlo = [put(f"wlo{s}", [P, PANEL], F32R) for s in range(SPL)]
        ident = put("ident", [P, P])
        ones = put("ones", [P, P])
        gain = put("gain", [P, G_ALL])
        tick = put("tick", [P, 1])
        after_const = top[0]
        rot2 = put("rot2", [P, P])
        dup = put("dup", [ROPE, 2, P])
        causal = put("causal", [P, L])
        cos2 = put("cos2", [P, L])
        sin2 = put("sin2", [P, L])
        inchunk = put("inchunk", [P, P], I32)
        keep = put("keep", [P, L])
        h_hi = put("h_hi", [P, KT, L], F32R)
        h_lo = put("h_lo", [P, KT, L], F32R)
        mixers = top[0]
        o_mla = put("o_mla", [P, KT, SEQ])
        zb = put("zb", [P, KT, SEQ])
        lrT = put("lrT", [RANK, L])
        work = top[0]
        ckv_hi = put("ckv_hi", [P, LT, L], F32R)
        ckv_lo = put("ckv_lo", [P, LT, L], F32R)
        cq_hi = put("cq_hi", [P, LT, SEQ], F32R)
        cq_lo = put("cq_lo", [P, LT, SEQ], F32R)
        krr = put("krr", [P, L])
        krsq = put("krsq", [ROPE, L])
        after_lat = top[0]
        qn = put("qn", [P, 2, SEQ])
        qr = put("qr", [P, SEQ])
        qrg = put("qrg", [P, SEQ])
        kn = put("kn", [P, 2, L])
        vm0 = put("vm0", [META, 2, DVM])
        vm = put("vm", [P, 2, 2, DVM])
        qnsq = put("qnsq", [P, 2, SEQ])
        qrsq = put("qrsq", [P, SEQ])
        knsq = put("knsq", [P, 2, L])
        rq = put("rq", [P, 2, SEQ])
        rk = put("rk", [P, 2, L])
        qs = put("qs", [P, 2, SEQ])
        ks = put("ks", [P, 2, L])
        qc = put("qc", [P, SEQ])
        qsn = put("qsn", [P, SEQ])
        qrs = put("qrs", [P, SEQ])
        krs = put("krs", [P, 2, L])
        sc0 = put("sc0", [P, 2, META + P])
        sc1 = put("sc1", [P, 2, L])
        pt0 = put("pt0", [META, 2, SEQ])
        pt1 = put("pt1", [P, 2, SEQ])
        pt2 = put("pt2", [P, 2, P])
        mx = put("mx", [P, 4])
        nb = put("nb", [P, 4])
        sm = put("sm", [P, 4])
        rs = put("rs", [P, 4])
        end_mla = top[0]
        top[0] = after_lat
        kr = put("kr", [ROPE, L])
        krg = put("krg", [ROPE, L])
        krc = put("krc", [P, L])
        krn = put("krn", [P, L])
        lat = put("lat", [P, 2, LT, L])
        latsq = put("latsq", [P, 2, LT, L])
        rlat = put("rlat", [P, 2, L])
        end_lat = top[0]
        top[0] = mixers
        xm = put("xm", [META, D])
        xn = put("xn", [P, 2, D])
        xT = put("xT", [P, KT, L])
        xsq = put("xsq", [P, KT, L])
        r1 = put("r1", [P, L])
        end_x = top[0]
        top[0] = work
        o_gla = put("o_gla", [P, KT, SEQ])
        w2h = put("w2h", [RANK, DK])
        gx = put("gx", [P, 2, L])
        gl = put("gl", [P, 2, L])
        gb = put("gb", [P, 2, L])
        eb = put("eb", [P, 2, L])
        enb = put("enb", [P, 2, L])
        vT = gx
        kf = gl
        qd = put("qd", [P, 2, SEQ])
        ke = put("ke", [P, 2, L])
        kd = put("kd", [P, 2, L])
        kdn0 = put("kdn0", [META, DK])
        kdn = put("kdn", [P, 2, DK])
        va0 = put("va0", [META, DV])
        va = put("va", [P, 2, DV])
        am = put("am", [P, 2, P])
        st = put("st", [P, 4, 2, DV])
        osq = put("osq", [P, 4, SEQ])
        sr = put("sr", [P, 4, SEQ])
        ro = enb[:, 0, 0:SEQ]
        end_gla = top[0]
        o_lo_m = put("o_lo_m", [P, KT, SEQ], F32R, at=mixers)
        m_lo = put("m_lo", [P, KT, SEQ], F32R, at=mixers + 4 * KT * SEQ)
        o_lo_g = put("o_lo_g", [P, KT, SEQ], F32R, at=work)
        top[0] = work + 4 * KT * SEQ
        o_hi_m = put("o_hi_m", [P, KT, SEQ], F32R)
        o_hi_g = put("o_hi_g", [P, KT, SEQ], F32R)
        m_hi = put("m_hi", [P, KT, SEQ], F32R)
        sb = put("sb", [P, 2, SEQ])
        end_mrg = top[0]
        sa = put("sa", [P, 2, SEQ], at=after_const)
        mb = put("mb", [P, 2, SEQ], at=after_const + 2048)
        mf = put("mf", [P, 2, SEQ], at=after_const + 4096)
        top[0] = after_const
        x2 = put("x2", [P, KT, SEQ])
        h2_hi = put("h2_hi", [P, KT, SEQ], F32R)
        h2_lo = put("h2_lo", [P, KT, SEQ], F32R)
        a_hi = put("a_hi", [P, FT, SEQ], F32R)
        a_lo = put("a_lo", [P, FT, SEQ], F32R)
        sg = put("sg", [P, 2, SEQ])
        af = put("af", [P, 2, SEQ])
        r2 = put("r2", [P, 2, SEQ])
        end_ff = top[0]
        for name, end in (("mla", end_mla), ("lat", end_lat), ("x", end_x), ("gla", end_gla), ("mrg", end_mrg), ("ff", end_ff)):
            assert BASE + end <= nc.sbuf_usable_end, (name, BASE + end - nc.sbuf_usable_end)
        top[0] = work
        xs = put("xs", [P, 2, 2, 2 * P])
        x2sq = put("x2sq", [P, 2, SEQ])
        ssum = put("ssum", [P, 2, SEQ])
        yT = put("yT", [P, 2, 4, SEQ], at=after_const + 4 * KT * SEQ)
        yn = put("yn", [P, 2, 2, 4 * P], at=after_const + 4 * KT * SEQ + 8192)

        psum = ctx.enter_context(nc.psum_tensor("psum", [P, 8, 512], F32))

        def pair(b, n):
            return psum[:, b:b + 2, 0:n]

        raw_in = [sem(f"raw_in{s}") for s in range(RAW)]
        hi_done = sem("hi_done")
        lo_done = sem("lo_done")
        used = sem("used")
        act_own, dve_own, pool_own = sem("act_own"), sem("dve_own"), sem("pool_own")

        block = ctx.enter_context(nc.Block())

        def after(p0, per, i, j):
            return i * (2 * per) + 2 * (p0 + j + 1)

        def raw_value(p0, per, i, j):
            p = p0 + j
            return i * (16 * per // RAW) + 16 * (p // RAW + 1)

        def slot(p0, j, n):
            return (p0 + j) % n

        UQ_PARTS = ((0, NOPE, 0), (NOPE, QK, LT * 2 * NOPE))

        def uq_part(t, a, b, at, from_raw):
            if from_raw:
                return t[:, 0:LT * 2 * QK].rearrange("p (k h c) -> p k h c", k=LT, h=2)[:, :, :, a:b]
            return t[:, at:at + LT * 2 * (b - a)].rearrange("p (k h c) -> p k h c", k=LT, h=2)

        S = {}

        def s(name):
            if name not in S:
                S[name] = sem(name)
            return S[name]

        FREE = {"pe": ("norm_sums", "o_added", "p_turned"),
                "act": ("sr_out", "o_out", "ro_done"),
                "dve": ("x2_out0", "x2_out1", "af_done", "gated", "merged", "a_lo_done")}

        def free_at_start(eng, owner):
            for name in FREE[owner]:
                eng.sem_inc(s(name), 1)

        @block.sync
        def _(sp):
            def load(p0, per, i, j, dst, src):
                if p0 + j >= RAW:
                    sp.wait_ge(lo_done, after(p0, per, i, j) - 2 * RAW)
                sp.dma_start(dst, src).then_inc(raw_in[slot(p0, j, RAW)], 16)

            def wide(p0, per, i, j, w, row0, col0):
                dst = raw[slot(p0, j, RAW)][:, :].rearrange("p (k c) -> p k c", k=8)
                src = w[row0:row0 + 8 * P, :].rearrange("(k p) c -> p k c", p=P)[:, :, bass.ds(col0, 256)]
                load(p0, per, i, j, dst, src)

            sp.dma_start(ident[:, :], consts["ident"]).then_inc(s("ident_in"), 16)
            sp.dma_start(xm[:, :], meta).then_inc(s("xm_in"), 16)
            xv = x.rearrange("o (t p) d -> p (o t) d", p=P)
            for f in range(4):
                sp.dma_start(xn[:, :, f * 512:(f + 1) * 512], xv[:, :, f * 512:(f + 1) * 512]).then_inc(s(f"xn_in{f}"), 16)
            sp.dma_start(gain[:, :], gains).then_inc(s("gain_in"), 16)
            small = raw[0][:, 0:KT * (RANK + ROPE)].rearrange("p (k c) -> p k c", k=KT)
            wk = w_in.rearrange("(k p) c -> p k c", p=P)
            sp.dma_start(small[:, :, 0:RANK], wk[:, :, C_LR:C_LR + RANK]).then_inc(s("lr_in"), 16)
            sp.dma_start(small[:, :, RANK:], wk[:, :, C_KR:C_KR + ROPE]).then_inc(raw_in[0], 16)
            for j in range(3):
                wide(P_LAT, 8, 0, j, w_in, (j % 2) * 8 * P, C_CQ + 256 * (j // 2))
            for t, name in ((rot2, "rot2"), (dup, "dup"), (causal, "causal"), (cos2, "cos2"), (sin2, "sin2"),
                            (inchunk, "inchunk"), (keep, "keep")):
                sp.dma_start(t[:], consts[name]).then_inc(s(f"const_{name}"), 16)
            for j in range(3, 8):
                wide(P_LAT, 8, 0, j, w_in, (j % 2) * 8 * P, C_CQ + 256 * (j // 2))
            uq = w_uq.rearrange("(k p) c -> p k c", p=P)
            ukv = w_ukv.rearrange("(k p) c -> p k c", p=P)
            with sp.Fori(0, PAIRS) as i:
                uq_col, ukv_col = sp.snap(i * (2 * QK)), sp.snap(i * 512)
                load(P_MLA, N_MLA, i, 0, raw[slot(P_MLA, 0, RAW)][:, 0:LT * 2 * QK].rearrange("p (k c) -> p k c", k=LT),
                     uq[:, :, bass.ds(uq_col, 2 * QK)])
                load(P_MLA, N_MLA, i, 1, raw[slot(P_MLA, 1, RAW)][:, :].rearrange("p (k c) -> p k c", k=LT),
                     ukv[:, :, bass.ds(ukv_col, 512)])
                for kh in range(2):
                    wide(P_MLA, N_MLA, i, 2 + kh, w_in, kh * 8 * P, i * 256 + C_ZB)
            with sp.Fori(0, GLA_HEADS) as i:
                for j, col in enumerate((C_K, C_Q)):
                    for kh in range(2):
                        wide(P_GLA, N_GLA, i, 2 * j + kh, w_in, kh * 8 * P, i * DK + col)
                    if j == 0:
                        sp.wait_ge(s("om_out"), PAIRS)
                        sp.dma_start(w2h[:, :], w2[:, bass.ds(i * DK, DK)]).then_inc(s("w2_in"), 16)
                for b in range(2):
                    for kh in range(2):
                        wide(P_GLA, N_GLA, i, 4 + 2 * b + kh, w_in, kh * 8 * P, i * DV + (C_V + 256 * b))
                for b in range(2):
                    for kh in range(2):
                        wide(P_GLA, N_GLA, i, 8 + 2 * b + kh, w_in, kh * 8 * P, i * DV + (C_R + 256 * b))
            with sp.Fori(0, 4) as i:
                for b in range(2):
                    for j, (w, col) in enumerate(((w_in, C_ZA), (w_a, 0), (w_b, 0))):
                        for kh in range(2):
                            step = P >> j
                            at = (i * (512 // step) + 256 * b // step) * step + col if j else i * 512 + (col + 256 * b)
                            wide(P_MRG, N_MRG, i, 6 * b + 2 * j + kh, w, kh * 8 * P, at)
            with sp.Fori(0, 4) as i:
                for b in range(2):
                    for kh in range(2):
                        wide(P_OUT, N_OUT, i, 2 * b + kh, w_out, kh * 8 * P, i * 512 + 256 * b)
                    sp.wait_ge(used, after(P_MRG, N_MRG, 3, 11))
                    sp.wait_ge(used, after(P_OUT, N_OUT, i, 2 * b + 1) - 2 * N_OUT)
                    sp.dma_start(xs[:, b], xv[:, :, bass.ds(i * 512 + 256 * b, 256)]).then_inc(s(f"xs_in{b}"), 16)
            with sp.Fori(0, FF // 256) as i:
                for j in range(2):
                    for kh in range(2):
                        wide(P_FF, N_FF, i, 2 * j + kh, w_gu, kh * 8 * P, i * 256 + FF * j)
            dn = w_dn.rearrange("(g k p) c -> g p k c", p=P, k=4)
            with sp.Fori(0, FT // 4) as i:
                for c in range(4):
                    load(P_DN, N_DN, i, c, raw[slot(P_DN, c, RAW)][:, :].rearrange("p (k c) -> p k c", k=4),
                         dn[bass.ds(i, 1), :, :, c * 512:(c + 1) * 512].rearrange("g p k c -> p (g k) c"))
            ov = out.rearrange("o (t p) d -> p (o t) d", p=P)
            for c in range(4):
                sp.wait_ge(s("yn_done"), 2 * (c + 1))
                sp.dma_start(ov[:, :, c * 512:(c + 1) * 512], yn[:, c % 2]).then_inc(s(f"out_done{c}"), 16)
            for c in range(4):
                sp.wait_ge(s(f"out_done{c}"), 16)

        @block.gpsimd
        def _(pool):
            own = Chain(pool, pool_own)

            def mult(o, a):
                return nc.gpsimd.tensor_tensor(o, a, a, ALU.mult)

            nc.gpsimd.memset(ones[:, :], 1.0).then_inc(s("ones_set"), 1)
            pool.wait_ge(s("lat_lo"), 2)
            with pool.Fori(0, PAIRS) as i:
                own.enter(i, 5)
                pool.wait_ge(s("norm_sums"), i + 1)
                pool.wait_ge(s("qn_out"), i + 1)
                mult(qnsq[:, :, :], qn[:, :, :])
                pool.wait_ge(s("qr_out"), i + 1)
                own.link(mult(qrsq[:, :], qr[:, :]))
                for h in range(2):
                    rows = slice(ROPE * h, ROPE * h + ROPE)
                    own.link(nc.gpsimd.tensor_tensor(qnsq[rows, h, :], qnsq[rows, h, :], qrsq[rows, :], ALU.add))
                pool.wait_ge(s("kn_out"), i + 1)
                own.link(mult(knsq[:, :, :], kn[:, :, :]))
                for h in range(2):
                    last = nc.gpsimd.tensor_tensor(knsq[0:ROPE, h, :], knsq[0:ROPE, h, :], krsq[:, :], ALU.add)
                    if h == 0:
                        own.link(last)
                last.then_inc(s("mla_sq"), 1)
            own.leave(PAIRS)
            with pool.Fori(0, GLA_HEADS) as i:
                pool.wait_ge(s("o_out"), i + 2)
                og = o_gla[:, bass.ds(i * 4, 4), :]
                nc.gpsimd.tensor_tensor(osq[:, :, :], og, og, ALU.mult).then_inc(s("o_sq"), 1)
            pool.wait_ge(used, after(P_MRG, N_MRG, 3, 11))
            own.link(nc.gpsimd.memset(ssum[:, :, :], 0.0))
            with pool.Fori(0, 4) as i:
                own.enter(i, 4)
                for b in range(2):
                    pool.wait_ge(s(f"x2_out{b}"), i + 2)
                    xb = x2[:, bass.ds(i * 4 + 2 * b, 2), :]
                    own.link(nc.gpsimd.tensor_tensor(x2sq[:, :, :], xb, xb, ALU.mult))
                    own.link(nc.gpsimd.tensor_tensor(ssum[:, :, :], ssum[:, :, :], x2sq[:, :, :], ALU.add))
            own.leave(4)
            nc.gpsimd.tensor_tensor(ssum[:, 0, :], ssum[:, 0, :], ssum[:, 1, :], ALU.add).then_inc(s("x2_sum"), 1)
            pool.wait_ge(s("r2_done"), 1)
            with pool.Fori(0, FF // 256) as i:
                pool.wait_ge(s("sg_done"), i + 1)
                nc.gpsimd.tensor_tensor(sg[:, :, :], sg[:, :, :], r2[:, :, :], ALU.mult).then_inc(s("sgr_done"), 1)

        @block.scalar
        def _(act):
            own = Chain(act, act_own)
            free_at_start(act, "act")
            A = nc.scalar.activation

            def split(p0, per, i, j, n=PANEL, uq=False):
                if p0 + j >= PANELS and isinstance(i, int) and i == 0:
                    return
                act.wait_ge(raw_in[slot(p0, j, RAW)], raw_value(p0, per, i, j))
                hi, src = whi[slot(p0, j, SPL)], raw[slot(p0, j, RAW)]
                for half in range(2):
                    if p0 + j >= SPL:
                        act.wait_ge(used, after(p0, per, i, j) - 2 * SPL - 1 + half)
                    if uq:
                        part = UQ_PARTS[half]
                        A(uq_part(hi, *part, False), uq_part(src, *part, True), ACT.Copy).then_inc(hi_done, 1)
                    else:
                        cols = slice(half * n // 2, (half + 1) * n // 2)
                        A(hi[:, cols], src[:, cols], ACT.Copy).then_inc(hi_done, 1)

            def panel_over(p0, per, i, j, uq=False):
                split(p0, per, i, j + SPL, uq=uq)
                act.wait_ge(used, after(p0, per, i, j))

            def rstd(o, sums, n):
                own.link(A(o, sums, ACT.Ln, bias=EPS, scale=1.0 / n))
                return A(o, o, ACT.Exp, scale=-0.5)

            act.preload_act_table_set(LN_EXP)
            for f in range(KT):
                act.wait_ge(s("x_turned"), f + 1)
                A(xT[:, f, :], psum[:, f % 4, 0:L], ACT.Copy).then_inc(s("xT_out"), 1)
            act.wait_ge(s("x_sums"), 1)
            rstd(r1[:, :], psum[:, 4, 0:L], D).then_inc(s("r1_done"), 1)
            for q in range(4):
                act.wait_ge(s("h_done"), q + 1)
                A(h_hi[:, 4 * q:4 * q + 4, :], xT[:, 4 * q:4 * q + 4, :], ACT.Copy).then_inc(s("h_hi_done"), 1)
                if q == 0:
                    act.wait_ge(s("lr_in"), 16)
                    split(0, 1, 0, 0, KT * (RANK + ROPE))
                if q == 1:
                    split(0, 1, 0, 1)
            panel_over(0, 1, 0, 0)
            A(lrT[:, :], psum[0:RANK, 0, 0:L], ACT.Copy).then_inc(s("lr_out"), 1)
            A(kr[:, :], psum[0:ROPE, 1, 0:L], ACT.Copy).then_inc(s("kr_out"), 1)
            for b in range(4):
                side, lo, n = (0, META, SEQ) if b < 2 else (1, 0, L)
                for kh in range(2):
                    panel_over(P_LAT, 8, 0, 2 * b + kh, uq=b == 3 and kh == 0)
                A(lat[:, side, 2 * (b % 2):2 * (b % 2) + 2, lo:L], pair(2 * (b % 2), n), ACT.Copy).then_inc(s("lat_out"), 1)
                if b % 2:
                    act.wait_ge(s("lat_sums"), side + 1)
                    rstd(rlat[:, side, lo:L], psum[:, 6 + side, 0:n], LORA).then_inc(s("rlat_done"), 1)
                    act.wait_ge(s("lat_done"), side + 1)
                    A((cq_hi if side == 0 else ckv_hi)[:, :, :], lat[:, side, :, lo:L], ACT.Copy).then_inc(s("lat_hi"), 1)

            def pt_out(i):
                act.wait_ge(s("p_turned"), i + 1)
                wait(act, s("pv_done"), i - 1)
                A(pt0[:, :, :], psum[0:META, 6:8, 0:SEQ], ACT.Copy)
                A(pt1[:, :, :], psum[:, 6:8, SEQ:2 * SEQ], ACT.Copy)
                A(pt2[:, :, :], psum[:, 4, 0:2 * P].rearrange("p (h q) -> p h q", h=2), ACT.Copy).then_inc(s("pt_out"), 1)

            def om_out(i):
                act.wait_ge(s("pv_done"), i)
                dst = o_mla[:, bass.ds(i * 2 - 2, 2), :]
                A(dst, psum[:, 7, :].rearrange("p (h q) -> p h q", h=2), ACT.Copy).then_inc(s("om_out"), 1)

            def mla_turn(i, first, last):
                panel_over(P_MLA, N_MLA, i, 0)
                A(qn[:, :, :], psum[:, 0, :].rearrange("p (h q) -> p h q", h=2), ACT.Copy).then_inc(s("qn_out"), 1)
                if not first:
                    pt_out(i)
                panel_over(P_MLA, N_MLA, i, 1)
                A(qr[:, :], psum[:, 1, 0:SEQ], ACT.Copy).then_inc(s("qr_out"), 1)
                A(qrg[:, :], psum[:, 1, 0:SEQ], ACT.Copy, scale=gain[:, G_QR:G_QR + 1]).then_inc(s("qrg_out"), 1)
                A(kn[:, :, :], pair(2, L), ACT.Copy).then_inc(s("kn_out"), 1)
                if not first:
                    om_out(i)
                A(vm0[:, :, :], psum[0:META, 1, SEQ:2 * SEQ].rearrange("p (h d) -> p h d", h=2), ACT.Copy)
                A(vm[:, :, :, :].rearrange("p t h d -> p (t h d)"), psum[:, 5, :], ACT.Copy).then_inc(s("vm_out"), 1)
                panel_over(P_MLA, N_MLA, i, 2, uq=not last)
                act.wait_ge(s("norm_sums"), i + 2)
                own.link(A(rq[:, :, :], psum[:, 4, :].rearrange("p (h q) -> p h q", h=2), ACT.Ln, bias=EPS, scale=1.0 / QK))
                A(rq[:, :, :], rq[:, :, :], ACT.Exp, scale=-0.5).then_inc(s("rq_done"), 1)
                A(rk[:, 0, :], psum[:, 1, 0:L], ACT.Ln, bias=EPS, scale=1.0 / QK)
                own.link(A(rk[:, 1, :], psum[:, 5, 0:L], ACT.Ln, bias=EPS, scale=1.0 / QK))
                A(rk[:, :, :], rk[:, :, :], ACT.Exp, scale=-0.5).then_inc(s("rk_done"), 1)
                panel_over(P_MLA, N_MLA, i, 3)
                A(zb[:, bass.ds(i * 2, 1), :], psum[:, 0:1, 0:SEQ], ACT.Copy)
                A(zb[:, bass.ds(i * 2 + 1, 1), :], psum[:, 6:7, 0:SEQ], ACT.Copy).then_inc(s("zb_out"), 1)
                act.wait_ge(s("nb_done"), i + 1)
                for h in range(2):
                    A(sc0[:, h, :], sc0[:, h, :], ACT.Exp, bias=nb[:, 2 * h:2 * h + 1], scale=QK ** -0.5,
                      accum_out=sm[:, 2 * h:2 * h + 1])
                    A(sc1[:, h, :], sc1[:, h, :], ACT.Exp, bias=nb[:, 2 * h + 1:2 * h + 2], scale=QK ** -0.5,
                      accum_out=sm[:, 2 * h + 1:2 * h + 2]).then_inc(s("p_exp"), 1)

            own.enter(0, 2)
            mla_turn(0, True, False)
            own.leave(1)
            with act.Fori(1, PAIRS - 1) as i:
                own.enter(i - 1, 2)
                mla_turn(i, False, False)
            own.leave(PAIRS - 2)
            own.enter(0, 2)
            mla_turn(PAIRS - 1, False, True)
            own.leave(1)

            def gla_turn(i, per):
                own.enter(i, per)
                panel_over(P_GLA, N_GLA, i, 0)
                act.wait_ge(s("logits"), i + 1)
                for dt in range(2):
                    bias = gain[:, bass.ds(i * 2 + (G_B + dt), 1)]
                    A(gx[:, dt, :], psum[:, 6 + dt, 0:L], ACT.Identity, bias=bias)
                    last = A(gl[:, dt, :], psum[:, 6 + dt, 0:L], ACT.Abs, bias=bias)
                last.then_inc(s("logits_out"), 1)
                act.wait_ge(s("logits_out"), i + 1)
                own.link(A(gl[:, :, :], gl[:, :, :], ACT.Exp, scale=-1.0))
                A(gl[:, :, :], gl[:, :, :], ACT.Ln, bias=1.0).then_inc(s("gl_done"), 1)
                panel_over(P_GLA, N_GLA, i, 1)
                act.wait_ge(s("decay"), i + 1)
                A(eb[:, :, :], gb[:, :, :], ACT.Exp, scale=1.0 / TAU)
                A(enb[:, :, :], gb[:, :, :], ACT.Exp, scale=-1.0 / TAU)
                kr3 = kf[:, :, 0:META + 3 * CHUNK]
                A(kr3, kr3, ACT.Exp, scale=1.0 / TAU).then_inc(s("decay_exp"), 1)
                for j in (2, 3, 4, 5):
                    panel_over(P_GLA, N_GLA, i, j)
                A(vT[:, :, :], pair(0, L), ACT.Copy).then_inc(s("vT_out"), 1)
                act.wait_ge(s("kd_turned"), i + 1)
                A(kdn[:, 0, :], psum[:, 6, 0:DK], ACT.Copy)
                A(kdn0[:, :], psum[0:META, 6, DK:2 * DK], ACT.Copy)
                A(kdn[0:CHUNK, 1, :], psum[0:CHUNK, 7, 0:DK], ACT.Copy).then_inc(s("kdn_out"), 1)

                def v_out(b):
                    act.wait_ge(s("v_turned"), i * 2 + (b + 1))
                    act.wait_ge(s("o_added"), i + 1)
                    c = slice(256 * b, 256 * b + 256)
                    A(va[:, :, c], psum[:, 4 + b, :].rearrange("p (t d) -> p t d", t=2), ACT.Copy)
                    A(va0[:, c], psum[0:META, 7, DK:2 * DK], ACT.Copy).then_inc(s("v_out"), 1)

                panel_over(P_GLA, N_GLA, i, 6)
                v_out(0)
                panel_over(P_GLA, N_GLA, i, 7)
                A(vT[:, :, :], pair(2, L), ACT.Copy).then_inc(s("vT_out"), 1)
                panel_over(P_GLA, N_GLA, i, 8)
                v_out(1)
                panel_over(P_GLA, N_GLA, i, 9)
                act.wait_ge(s("gated"), i + 1)
                A(sr[:, 0:2, :], pair(0, SEQ), ACT.Silu).then_inc(s("sr_out"), 1)
                panel_over(P_GLA, N_GLA, i, 10)
                act.wait_ge(s("o_added"), i + 2)
                A(o_gla[:, bass.ds(i * 4, 4), :], psum[:, 6:8, :].rearrange("p b (v q) -> p (b v) q", q=SEQ), ACT.Copy).then_inc(s("o_out"), 1)
                panel_over(P_GLA, N_GLA, i, 11)
                A(sr[:, 2:4, :], pair(2, SEQ), ACT.Silu).then_inc(s("sr_out"), 1)
                act.preload_act_table_set(LN_EXP)
                act.wait_ge(s("o_sums"), i + 1)
                own.link(A(ro, psum[:, 4, 0:SEQ], ACT.Ln, bias=EPS, scale=1.0 / DV))
                A(ro, ro, ACT.Exp, scale=-0.5).then_inc(s("ro_done"), 1)

            pt_out(PAIRS)
            om_out(PAIRS)
            with act.Fori(0, GLA_HEADS) as i:
                gla_turn(i, 2)
            own.leave(GLA_HEADS)

            def o_his(dst, src):
                for q in range(4):
                    A(dst[:, 4 * q:4 * q + 4, :], src[:, 4 * q:4 * q + 4, :], ACT.Copy).then_inc(s("o_hi"), 1)

            def merge_turn(i, first):
                for b in range(2):
                    blk = i * 2 + b
                    for j in range(2):
                        panel_over(P_MRG, N_MRG, i, 6 * b + j)
                        if first and b == 0:
                            if j == 0:
                                act.wait_ge(s("gated"), GLA_HEADS + 1)
                            o_his(*((o_hi_g, o_gla), (o_hi_m, o_mla))[j])
                    act.wait_ge(s("merged"), blk + 1)
                    A(sa[:, :, :], pair(0, SEQ), ACT.Sigmoid).then_inc(s("sa_done"), 1)
                    A(sb[:, :, :], zb[:, bass.ds(i * 4 + 2 * b, 2), :], ACT.Sigmoid).then_inc(s("sb_done"), 1)
                    for j in range(2, 6):
                        panel_over(P_MRG, N_MRG, i, 6 * b + j)
                    act.wait_ge(s("mf_done"), blk + 1)
                    A(m_hi[:, bass.ds(i * 4 + 2 * b, 2), :], mf[:, :, :], ACT.Copy).then_inc(s("m_hi_done"), 1)

            merge_turn(0, True)
            with act.Fori(1, 4) as i:
                merge_turn(i, False)
            with act.Fori(0, 4) as i:
                for b in range(2):
                    for kh in range(2):
                        panel_over(P_OUT, N_OUT, i, 2 * b + kh)
                    act.wait_ge(s(f"x2_out{b}"), i + 2)
                    for m in range(2):
                        f = i * 4 + (2 * b + m)
                        last = A(h2_hi[:, bass.ds(f, 1), :], x2[:, bass.ds(f, 1), :], ACT.Copy,
                                 scale=gain[:, bass.ds(i * 4 + (G_2 + 2 * b + m), 1)])
                    last.then_inc(s("h2_hi_done"), 1)

            def ff_turn(i, first):
                panel_over(P_FF, N_FF, i, 0)
                panel_over(P_FF, N_FF, i, 1)
                if first:
                    act.preload_act_table_set(LN_EXP)
                    act.wait_ge(s("x2_sums"), 1)
                    own.link(A(r2[:, 0, :], psum[:, 4, 0:SEQ], ACT.Ln, bias=EPS, scale=1.0 / D))
                    own.link(A(r2[:, 0, :], r2[:, 0, :], ACT.Exp, scale=-0.5))
                    A(r2[:, 1, :], r2[:, 0, :], ACT.Copy).then_inc(s("r2_done"), 1)
                act.wait_ge(s("gate_out"), i + 1)
                A(sg[:, :, :], sg[:, :, :], ACT.Silu).then_inc(s("sg_done"), 1)
                panel_over(P_FF, N_FF, i, 2)
                panel_over(P_FF, N_FF, i, 3)
                act.wait_ge(s("af_done"), i + 2)
                A(a_hi[:, bass.ds(i * 2, 2), :], af[:, :, :], ACT.Copy).then_inc(s("a_hi_done"), 1)

            ff_turn(0, True)
            with act.Fori(1, FF // 256) as i:
                ff_turn(i, False)
            last_turn = FT // 4 - 1
            with act.Fori(0, last_turn) as i:
                for c in range(4):
                    panel_over(P_DN, N_DN, i, c)
            for c in range(2):
                split(P_DN, N_DN, last_turn, c + 2)
            for c in range(4):
                act.wait_ge(s("y_turned"), c + 1)
                if c >= 2:
                    act.wait_ge(s(f"out_done{c - 2}"), 16)
                A(yn[:, c % 2, 0, :], psum[:, 2 * c, :], ACT.Copy).then_inc(s("yn_done"), 1)
                A(yn[:, c % 2, 1, :], psum[:, 2 * c + 1, :], ACT.Copy).then_inc(s("yn_done"), 1)

        @block.vector
        def _(dve):
            own = Chain(dve, dve_own)
            V = nc.vector
            free_at_start(dve, "dve")

            def split(p0, per, i, j, n=PANEL, uq=False):
                k = slot(p0, j, SPL)
                lo, hi, src = wlo[k], whi[k], raw[slot(p0, j, RAW)]
                for half in range(2):
                    dve.wait_ge(hi_done, after(p0, per, i, j) - 1 + half)
                    if uq:
                        part = UQ_PARTS[half]
                        V.tensor_tensor(uq_part(lo, *part, False), uq_part(src, *part, True),
                                        uq_part(hi, *part, False).bitcast(F32), ALU.subtract).then_inc(lo_done, 1)
                    else:
                        cols = slice(half * n // 2, (half + 1) * n // 2)
                        V.tensor_tensor(lo[:, cols], src[:, cols], hi[:, cols].bitcast(F32), ALU.subtract).then_inc(lo_done, 1)

            def panel_over(p0, per, i, j, uq=False):
                split(p0, per, i, j + SPL, uq=uq)
                dve.wait_ge(used, after(p0, per, i, j))

            for f in range(KT):
                dve.wait_ge(s("xT_out"), f + 1)
                V.tensor_tensor(xsq[:, f, :], xT[:, f, :], xT[:, f, :], ALU.mult).then_inc(s("x_sq"), 1)
            dve.wait_ge(s("r1_done"), 1)
            dve.wait_ge(s("gain_in"), 16)
            for q in range(4):
                for f in range(4 * q, 4 * q + 4):
                    last = V.scalar_tensor_tensor(xT[:, f, :], xT[:, f, :], gain[:, G_1 + f:G_1 + f + 1], r1[:, :],
                                                  ALU.mult, ALU.mult)
                last.then_inc(s("h_done"), 1)
            for q in range(4):
                dve.wait_ge(s("h_hi_done"), q + 1)
                V.tensor_tensor(h_lo[:, 4 * q:4 * q + 4, :], xT[:, 4 * q:4 * q + 4, :],
                                h_hi[:, 4 * q:4 * q + 4, :].bitcast(F32), ALU.subtract).then_inc(s("h_lo_done"), 1)
                if q == 0:
                    split(0, 1, 0, 0, KT * (RANK + ROPE))
                if q == 1:
                    split(0, 1, 0, 1)
            panel_over(0, 1, 0, 0)
            dve.wait_ge(s("kr_out"), 1)
            V.tensor_tensor(krsq[:, :], kr[:, :], kr[:, :], ALU.mult).then_inc(s("kr_sq"), 1)
            V.tensor_scalar(krg[:, :], kr[:, :], gain[0:ROPE, G_KR:G_KR + 1], None, ALU.mult).then_inc(s("krg_done"), 1)
            for b in range(4):
                side, lo = (0, META) if b < 2 else (1, 0)
                for kh in range(2):
                    panel_over(P_LAT, 8, 0, 2 * b + kh, uq=b == 3 and kh == 0)
                if b == 0:
                    dve.wait_ge(s("kr_dup"), 1)
                    dve.wait_ge(s("const_cos2"), 16)
                    dve.wait_ge(s("const_sin2"), 16)
                    V.tensor_tensor(krc[:, :], cos2[:, :], psum[:, 4, 0:L], ALU.mult)
                    own.link(V.tensor_tensor(krn[:, :], sin2[:, :], psum[:, 5, 0:L], ALU.mult))
                    V.tensor_tensor(krr[:, :], krc[:, :], krn[:, :], ALU.add).then_inc(s("krr_done"), 1)
                dve.wait_ge(s("lat_out"), b + 1)
                t = slice(2 * (b % 2), 2 * (b % 2) + 2)
                V.tensor_tensor(latsq[:, side, t, lo:L], lat[:, side, t, lo:L], lat[:, side, t, lo:L],
                                ALU.mult).then_inc(s("lat_sq"), 1)
                if b % 2:
                    dve.wait_ge(s("rlat_done"), side + 1)
                    g0 = G_QA if side == 0 else G_KVA
                    for k in range(LT):
                        last = V.scalar_tensor_tensor(lat[:, side, k, lo:L], lat[:, side, k, lo:L],
                                                      gain[:, g0 + k:g0 + k + 1], rlat[:, side, lo:L], ALU.mult, ALU.mult)
                    last.then_inc(s("lat_done"), 1)
                    dve.wait_ge(s("lat_hi"), side + 1)
                    hi, lw = (cq_hi, cq_lo) if side == 0 else (ckv_hi, ckv_lo)
                    V.tensor_tensor(lw[:, :, :], lat[:, side, :, lo:L], hi[:, :, :].bitcast(F32),
                                    ALU.subtract).then_inc(s("lat_lo"), 1)

            def half(h):
                return slice(ROPE * h, ROPE * h + ROPE)

            def mla_turn(i, last_one):
                panel_over(P_MLA, N_MLA, i, 0)
                panel_over(P_MLA, N_MLA, i, 1)
                panel_over(P_MLA, N_MLA, i, 2, uq=not last_one)
                dve.wait_ge(s("norm_sums"), i + 2)
                dve.wait_ge(s("qrg_out"), i + 1)
                V.tensor_tensor(qc[:, :], qrg[:, :], cos2[:, META:L], ALU.mult)
                own.link(V.tensor_tensor(qsn[:, :], sin2[:, META:L], psum[:, 7, 0:SEQ], ALU.mult))
                own.link(V.tensor_tensor(qc[:, :], qc[:, :], qsn[:, :], ALU.add))
                dve.wait_ge(s("rq_done"), i + 1)
                for h in range(2):
                    V.scalar_tensor_tensor(qs[:, h, :], qn[:, h, :], gain[:, G_QN:G_QN + 1], rq[:, h, :], ALU.mult, ALU.mult)
                    V.tensor_tensor(qrs[half(h), :], qc[half(h), :], rq[half(h), h, :], ALU.mult)
                dve.wait_ge(s("rk_done"), i + 1)
                for h in range(2):
                    V.scalar_tensor_tensor(ks[:, h, :], kn[:, h, :], gain[:, G_KN:G_KN + 1], rk[:, h, :], ALU.mult, ALU.mult)
                    last = V.tensor_tensor(krs[half(h), h, :], krr[half(h), :], rk[half(h), h, :], ALU.mult)
                last.then_inc(s("qk_done"), 1)
                panel_over(P_MLA, N_MLA, i, 3)
                dve.wait_ge(s("scores"), i + 1)
                dve.wait_ge(s("p_turned"), i + 1)
                dve.wait_ge(s("const_causal"), 16)
                V.memset(tick[:, :], 0.0)
                for h in range(2):
                    V.tensor_tensor_reduce(out=sc0[:, h, :], in0=psum[:, 4 + h, 0:META + P], in1=causal[:, P:L], scale=1.0,
                                           scalar=-3e38, op0=ALU.add, op1=ALU.max, accum_out=mx[:, 2 * h:2 * h + 1])
                    last = V.tensor_tensor_reduce(out=sc1[:, h, :], in0=psum[:, 4 + h, META + P:META + P + L], in1=causal[:, :],
                                                  scale=1.0, scalar=-3e38, op0=ALU.add, op1=ALU.max,
                                                  accum_out=mx[:, 2 * h + 1:2 * h + 2])
                own.link(last)
                V.tensor_scalar(nb[:, :], mx[:, :], -(QK ** -0.5), None, ALU.mult).then_inc(s("nb_done"), 1)
                dve.wait_ge(s("p_exp"), 2 * i + 2)
                own.link(V.reciprocal(rs[:, :], sm[:, :]))
                for h in range(2):
                    V.tensor_scalar(sc0[:, h, :], sc0[:, h, :], rs[:, 2 * h:2 * h + 1], None, ALU.mult)
                    last = V.tensor_scalar(sc1[:, h, :], sc1[:, h, :], rs[:, 2 * h + 1:2 * h + 2], None, ALU.mult)
                last.then_inc(s("p_done"), 1)

            for h in range(2):
                V.memset(krs[half(1 - h), h, :], 0.0)
            with dve.Fori(0, PAIRS - 1) as i:
                own.enter(i, 4)
                mla_turn(i, False)
            own.leave(PAIRS - 1)
            own.enter(0, 4)
            mla_turn(PAIRS - 1, True)
            own.leave(1)

            dve.wait_ge(s("om_out"), PAIRS)
            dve.wait_ge(s("const_keep"), 16)
            own.link(V.memset(am[:, :, :], 0.0))

            def gla_turn(i):
                own.enter(i, 6)
                panel_over(P_GLA, N_GLA, i, 0)
                dve.wait_ge(s("gl_done"), i + 1)
                own.link(V.scalar_tensor_tensor(gx[:, :, :], gx[:, :, :], 0.0, gl[:, :, :], ALU.min, ALU.subtract))
                for dt in range(2):
                    last = V.tensor_tensor_scan(gb[:, dt, :], keep[:, :], gx[:, dt, :], 0.0, ALU.mult, ALU.add)
                own.link(last)
                for dt in range(2):
                    V.tensor_tensor(kf[:, dt, 0:META], gb[:, dt, META - 1:META].broadcast_to([P, META]),
                                    gb[:, dt, 0:META], ALU.subtract)
                    g3 = gb[:, dt, META:META + 3 * CHUNK].rearrange("p (c t) -> p c t", t=CHUNK)
                    last = V.tensor_tensor(kf[:, dt, META:META + 3 * CHUNK].rearrange("p (c t) -> p c t", t=CHUNK),
                                           g3[:, :, CHUNK - 1:CHUNK].broadcast_to([P, 3, CHUNK]), g3, ALU.subtract)
                last.then_inc(s("decay"), 1)
                panel_over(P_GLA, N_GLA, i, 1)
                dve.wait_ge(s("decay_exp"), i + 1)
                V.tensor_tensor(ke[:, :, :], enb[:, :, :], pair(0, L), ALU.mult)
                n = META + 3 * CHUNK
                V.tensor_tensor(kd[:, :, 0:n], kf[:, :, 0:n], pair(0, n), ALU.mult).then_inc(s("kd_done"), 1)
                panel_over(P_GLA, N_GLA, i, 2)
                panel_over(P_GLA, N_GLA, i, 3)
                V.scalar_tensor_tensor(qd[:, :, :], pair(2, SEQ), DK ** -0.5, eb[:, :, META:L], ALU.mult,
                                       ALU.mult).then_inc(s("qd_done"), 1)
                panel_over(P_GLA, N_GLA, i, 4)
                panel_over(P_GLA, N_GLA, i, 5)
                dve.wait_ge(s("a_in"), i + 1)
                dve.wait_ge(s("const_inchunk"), 16)
                V.memset(tick[:, :], 0.0)
                for c in range(2):
                    last = V.copy_predicated(am[:, c, :], inchunk[:, :], psum[:, 5, c * P:(c + 1) * P])
                last.then_inc(s("am_done"), 1)
                panel_over(P_GLA, N_GLA, i, 6)
                panel_over(P_GLA, N_GLA, i, 7)
                panel_over(P_GLA, N_GLA, i, 8)
                panel_over(P_GLA, N_GLA, i, 9)
                for c in range(4):
                    for dt in range(2):
                        n = 2 * c + dt
                        dve.wait_ge(s("ds_in"), i * 8 + (n + 1))
                        src = psum[:, (6, 7, 4, 5)[n % 4], :]
                        if c == 0:
                            ins = V.tensor_copy(st[:, 0, dt, :], src)
                        else:
                            end = META + c * CHUNK - 1
                            ins = V.scalar_tensor_tensor(st[:, c, dt, :], st[:, c - 1, dt, :], eb[:, dt, end:end + 1], src,
                                                         ALU.mult, ALU.add)
                        ins.then_inc(s("st_done"), 1)
                        dve.wait_ge(s("st_done"), i * 8 + (n + 1))
                panel_over(P_GLA, N_GLA, i, 10)
                panel_over(P_GLA, N_GLA, i, 11)
                dve.wait_ge(s("ro_done"), i + 2)
                for v in range(4):
                    ov = o_gla[:, bass.ds(i * 4 + v, 1), :].rearrange("p a q -> p (a q)")
                    own.link(V.scalar_tensor_tensor(ov, ov, gain[:, G_O + v:G_O + v + 1], ro, ALU.mult, ALU.mult))
                dve.wait_ge(s("sr_out"), i * 2 + 3)
                og = o_gla[:, bass.ds(i * 4, 4), :]
                V.tensor_tensor(og, og, sr[:, :, :], ALU.mult).then_inc(s("gated"), 1)

            with dve.Fori(0, GLA_HEADS) as i:
                gla_turn(i)
            own.leave(GLA_HEADS)

            def o_los(n, dst, src, hi):
                for q in range(4):
                    t = slice(4 * q, 4 * q + 4)
                    dve.wait_ge(s("o_hi"), 4 * n + q + 1)
                    V.tensor_tensor(dst[:, t, :], src[:, t, :], hi[:, t, :].bitcast(F32), ALU.subtract).then_inc(s("o_lo"), 1)

            def merge_turn(i, first):
                own.enter(0 if first else i - 1, 4)
                for b in range(2):
                    blk = i * 2 + b
                    for j in range(4):
                        panel_over(P_MRG, N_MRG, i, 6 * b + j)
                        if first and b == 0 and j < 2:
                            o_los(j, *((o_lo_g, o_gla, o_hi_g), (o_lo_m, o_mla, o_hi_m))[j])
                    dve.wait_ge(s("sa_done"), blk + 1)
                    own.link(V.tensor_tensor(mf[:, :, :], sa[:, :, :], pair(2, SEQ), ALU.mult))
                    for j in range(4, 6):
                        panel_over(P_MRG, N_MRG, i, 6 * b + j)
                    dve.wait_ge(s("sb_done"), blk + 1)
                    own.link(V.tensor_tensor(mb[:, :, :], sb[:, :, :], pair(4, SEQ), ALU.mult))
                    V.tensor_tensor(mf[:, :, :], mf[:, :, :], mb[:, :, :], ALU.add).then_inc(s("mf_done"), 1)
                    dve.wait_ge(s("m_hi_done"), blk + 1)
                    t = bass.ds(i * 4 + 2 * b, 2)
                    V.tensor_tensor(m_lo[:, t, :], mf[:, :, :], m_hi[:, t, :].bitcast(F32), ALU.subtract).then_inc(s("merged"), 1)

            merge_turn(0, True)
            own.leave(1)
            with dve.Fori(1, 4) as i:
                merge_turn(i, False)
            own.leave(3)
            with dve.Fori(0, 4) as i:
                for b in range(2):
                    for kh in range(2):
                        panel_over(P_OUT, N_OUT, i, 2 * b + kh)
                    V.tensor_copy(x2[:, bass.ds(i * 4 + 2 * b, 2), :], pair(2 * b, SEQ)).then_inc(s(f"x2_out{b}"), 1)
                    dve.wait_ge(s("h2_hi_done"), i * 2 + (b + 1))
                    for m in range(2):
                        f = i * 4 + (2 * b + m)
                        last = V.scalar_tensor_tensor(h2_lo[:, bass.ds(f, 1), :], x2[:, bass.ds(f, 1), :],
                                                      gain[:, bass.ds(i * 4 + (G_2 + 2 * b + m), 1)],
                                                      h2_hi[:, bass.ds(f, 1), :].bitcast(F32), ALU.mult, ALU.subtract)
                    last.then_inc(s("h2_lo_done"), 1)
            def ff_turn(i, first):
                for j in range(2):
                    panel_over(P_FF, N_FF, i, j)
                if first:
                    dve.wait_ge(s("r2_done"), 1)
                dve.wait_ge(s("af_done"), i + 1)
                V.tensor_tensor(sg[:, :, :], r2[:, :, :], pair(0, SEQ), ALU.mult).then_inc(s("gate_out"), 1)
                for j in range(2, 4):
                    panel_over(P_FF, N_FF, i, j)
                dve.wait_ge(s("sgr_done"), i + 1)
                dve.wait_ge(s("a_lo_done"), i + 1)
                V.tensor_tensor(af[:, :, :], sg[:, :, :], pair(2, SEQ), ALU.mult).then_inc(s("af_done"), 1)
                dve.wait_ge(s("a_hi_done"), i + 1)
                t = bass.ds(i * 2, 2)
                V.tensor_tensor(a_lo[:, t, :], af[:, :, :], a_hi[:, t, :].bitcast(F32), ALU.subtract).then_inc(s("a_lo_done"), 1)

            ff_turn(0, True)
            with dve.Fori(1, FF // 256) as i:
                ff_turn(i, False)
            last_turn = FT // 4 - 1
            with dve.Fori(0, last_turn) as i:
                for c in range(4):
                    panel_over(P_DN, N_DN, i, c)
            for c in range(4):
                if c < 2:
                    split(P_DN, N_DN, last_turn, c + 2)
                dve.wait_ge(used, after(P_DN, N_DN, last_turn, c))
                if c >= 2:
                    dve.wait_ge(s("y_turned"), c - 1)
                V.tensor_tensor(yT[:, c % 2], x2[:, 4 * c:4 * c + 4, :],
                                psum[:, 2 * c:2 * c + 2, :].rearrange("p b (v q) -> p (b v) q", q=SEQ), ALU.add).then_inc(s("y_done"), 1)

        @block.tensor
        def _(pe):
            M = nc.tensor.matmul
            free_at_start(pe, "pe")

            def three(o, a, b, start, stop, skip=False):
                M(o, a[0], b[0], start=start, stop=False, skip_group_check=skip)
                M(o, a[0], b[1], start=False, stop=False, skip_group_check=skip)
                return M(o, a[1], b[0], start=False, stop=stop, skip_group_check=skip)

            def panel(p0, per, i, j):
                pe.wait_ge(lo_done, after(p0, per, i, j) - 1)
                k = slot(p0, j, SPL)
                return whi[k], wlo[k]

            def second_half(p0, per, i, j, last=None):
                if last is not None:
                    last.then_inc(used, 1)
                pe.wait_ge(lo_done, after(p0, per, i, j))

            def wide(p0, per, i, j, kh, b0, src, lo=META, start=True):
                banks = b0 if isinstance(b0, tuple) else (b0, b0 + 1)
                hi_lo = [w[:, :].rearrange("p (k c) -> p k c", k=8) for w in panel(p0, per, i, j)]
                n = L - lo if src is h_pair else SEQ
                for k in range(8):
                    kk = 8 * kh + k
                    rhs = [t[:, kk, lo:L] if src is h_pair else t[:, kk, :] for t in src]
                    for m in range(2):
                        lhs = [w[:, k, m * P:(m + 1) * P] for w in hi_lo]
                        last = three(psum[:, banks[m], 0:n], lhs, rhs, start and kh == 0 and k == 0, kh == 1 and k == 7)
                    if k == 3:
                        second_half(p0, per, i, j, last)
                last.then_inc(used, 1)

            h_pair = (h_hi, h_lo)

            pe.wait_ge(s("ident_in"), 16)
            pe.wait_ge(s("xm_in"), 16)

            def x_sum(f):
                pe.wait_ge(s("x_sq"), f + 1)
                return M(psum[:, 4, 0:L], ones[:, :], xsq[:, f, :], start=f == 0, stop=f == KT - 1)

            pe.wait_ge(s("ones_set"), 1)
            for f in range(KT):
                if f % 4 == 0:
                    pe.wait_ge(s(f"xn_in{f // 4}"), 16)
                if f >= 4:
                    pe.wait_ge(s("xT_out"), f - 3)
                cols = slice(f * P, (f + 1) * P)
                nc.tensor.transpose(psum[:, f % 4, 0:META], xm[:, cols], ident[0:META, 0:META])
                for t in range(2):
                    last = nc.tensor.transpose(psum[:, f % 4, META + t * P:META + (t + 1) * P], xn[:, t, cols], ident[:, :])
                last.then_inc(s("x_turned"), 1)
                if f >= 4:
                    x_sum(f - 4)
            for f in range(KT - 4, KT):
                last = x_sum(f)
            last.then_inc(s("x_sums"), 1)

            hi_lo = [w[:, 0:KT * (RANK + ROPE)].rearrange("p (k c) -> p k c", k=KT) for w in panel(0, 1, 0, 0)]
            for k in range(KT):
                if k == KT // 2:
                    second_half(0, 1, 0, 0)
                if k % 4 == 0:
                    pe.wait_ge(s("h_lo_done"), k // 4 + 1)
                rhs = [t[:, k, :] for t in h_pair]
                three(psum[0:RANK, 0, 0:L], [w[:, k, 0:RANK] for w in hi_lo], rhs, k == 0, k == KT - 1)
                last = three(psum[0:ROPE, 1, 0:L], [w[:, k, RANK:] for w in hi_lo], rhs, k == 0, k == KT - 1)
            last.then_inc(used, 2)

            def lat_sum(side):
                lo = META if side == 0 else 0
                pe.wait_ge(s("lat_sq"), 2 * side + 2)
                for k in range(LT):
                    last = M(psum[:, 6 + side, 0:L - lo], ones[:, :], latsq[:, side, k, lo:L], start=k == 0, stop=k == LT - 1)
                last.then_inc(s("lat_sums"), 1)

            for b in range(4):
                if b > 1:
                    pe.wait_ge(s("lat_out"), b - 1)
                if b == 0:
                    pe.wait_ge(s("kr_out"), 1)
                for kh in range(2):
                    wide(P_LAT, 8, 0, 2 * b + kh, kh, 2 * (b % 2), h_pair, META if b < 2 else 0)
                    if b == 0 and kh == 0:
                        pe.wait_ge(s("krg_done"), 1)
                        pe.wait_ge(s("const_dup"), 16)
                        M(psum[:, 4, 0:L], dup[:, 0, :], krg[:, :], start=True, stop=True)
                        M(psum[:, 5, 0:L], dup[:, 1, :], krg[:, :], start=True, stop=True).then_inc(s("kr_dup"), 1)
                    if b == 2 and kh == 0:
                        lat_sum(0)
            lat_sum(1)

            def mla_norms(i):
                pe.wait_ge(s("mla_sq"), i + 1)
                pe.wait_ge(s("vm_out"), i + 1)
                for h in range(2):
                    M(psum[:, 4, h * SEQ:(h + 1) * SEQ], ones[:, :], qnsq[:, h, :], start=True, stop=True)
                    M(psum[:, 1 + 4 * h, 0:L], ones[:, :], knsq[:, h, :], start=True, stop=True)
                M(psum[:, 7, 0:SEQ], rot2[:, :], qrg[:, :], start=True, stop=True).then_inc(s("norm_sums"), 1)

            def mla_scores(i):
                pe.wait_ge(s("qk_done"), i + 1)
                for h in range(2):
                    for t, (c0, n) in enumerate(((0, META + P), (META + P, L))):
                        o = psum[:, 4 + h, c0:c0 + n]
                        q = slice(t * P, (t + 1) * P)
                        M(o, qs[:, h, q], ks[:, h, 0:n], start=True, stop=False)
                        last = M(o, qrs[:, q], krs[:, h, 0:n], start=False, stop=True)
                last.then_inc(s("scores"), 1)

            def mla_turn_p(i):
                T = nc.tensor.transpose
                pe.wait_ge(s("p_done"), i)
                for h in range(2):
                    for t, sc in enumerate((sc0, sc1)):
                        q = slice(t * P, (t + 1) * P)
                        T(psum[0:META, 6 + h, q], sc[:, h, 0:META], ident[:, :])
                        T(psum[:, 6 + h, SEQ + t * P:SEQ + (t + 1) * P], sc[:, h, META:META + P], ident[:, :])
                    last = T(psum[:, 4, h * P:(h + 1) * P], sc1[:, h, META + P:L], ident[:, :])
                last.then_inc(s("p_turned"), 1)

            def mla_pv(i):
                pe.wait_ge(s("pt_out"), i)
                for h in range(2):
                    o = psum[:, 7, h * SEQ:(h + 1) * SEQ]
                    M(o, vm0[:, h, :], pt0[:, h, :], start=True, stop=False)
                    M(o, vm[:, 0, h, :], pt1[:, h, :], start=False, stop=False)
                    last = M(o[:, P:SEQ], vm[:, 1, h, :], pt2[:, h, :], start=False, stop=True)
                last.then_inc(s("pv_done"), 1)

            def mla_turn(i, first):
                hi_lo = panel(P_MLA, N_MLA, i, 0)
                nope = [uq_part(w, *UQ_PARTS[0], False) for w in hi_lo]
                rope = [w[:, LT * 2 * NOPE:LT * 2 * QK].rearrange("p (k c) -> p k c", k=LT) for w in hi_lo]
                if first:
                    pe.wait_ge(s("lat_lo"), 1)
                    pe.wait_ge(s("lat_out"), 4)
                else:
                    pe.wait_ge(s("zb_out"), i)
                c_q = (cq_hi, cq_lo)
                for h in range(2):
                    for k in range(LT):
                        last = three(psum[:, 0, h * SEQ:(h + 1) * SEQ], [w[:, k, h, :] for w in nope], [t[:, k, :] for t in c_q],
                              k == 0, k == LT - 1)
                second_half(P_MLA, N_MLA, i, 0, last)
                for k in range(LT):
                    last = three(psum[:, 1, 0:SEQ], [w[:, k, :] for w in rope], [t[:, k, :] for t in c_q],
                                 k == 0, k == LT - 1)
                last.then_inc(used, 1)
                hi_lo = [w[:, :].rearrange("p (k h c) -> p k h c", k=LT, h=2) for w in panel(P_MLA, N_MLA, i, 1)]
                second_half(P_MLA, N_MLA, i, 1)
                if first:
                    pe.wait_ge(s("lat_lo"), 2)
                for h in range(2):
                    for k in range(LT):
                        three(psum[:, 2 + h, 0:L], [w[:, k, h, 0:NOPE] for w in hi_lo], [ckv_hi[:, k, :], ckv_lo[:, k, :]],
                              k == 0, k == LT - 1)
                if not first:
                    mla_turn_p(i)
                for t, (a, b) in enumerate(TOK):
                    o = psum[0:META, 1, SEQ:2 * SEQ] if t == 0 else psum[:, 5, (t - 1) * SEQ:t * SEQ]
                    o = o.rearrange("p (h d) -> p h d", h=2)
                    for k in range(LT):
                        last = three(o, [ckv_hi[:, k, a:b], ckv_lo[:, k, a:b]], [w[:, k, :, NOPE:] for w in hi_lo],
                                     k == 0, k == LT - 1)
                last.then_inc(used, 2)
                if not first:
                    mla_pv(i)
                pe.wait_ge(s("qn_out"), i + 1)
                wide(P_MLA, N_MLA, i, 2, 0, (0, 6), h_pair)
                if not first:
                    pe.wait_ge(s("om_out"), i)
                mla_norms(i)
                wide(P_MLA, N_MLA, i, 3, 1, (0, 6), h_pair)
                mla_scores(i)

            pe.wait_ge(s("const_rot2"), 16)
            mla_turn(0, True)
            with pe.Fori(1, PAIRS) as i:
                mla_turn(i, False)
            mla_turn_p(PAIRS)
            mla_pv(PAIRS)

            def turn_values(i, b):
                pe.wait_ge(s("vT_out"), i * 2 + (b + 1))
                if b == 0:
                    pe.wait_ge(s("kdn_out"), i + 1)
                else:
                    pe.wait_ge(s("v_out"), i * 2 + 1)
                T = nc.tensor.transpose
                for m in range(2):
                    T(psum[0:META, 7, DK + m * P:DK + (m + 1) * P], vT[:, m, 0:META], ident[:, :])
                    for t in range(2):
                        last = T(psum[:, 4 + b, t * 256 + m * P:t * 256 + (m + 1) * P], vT[:, m, TOK[t + 1][0]:TOK[t + 1][1]],
                                 ident[:, :])
                last.then_inc(s("v_turned"), 1)

            def gla_turn(i):
                G = (P_GLA, N_GLA, i)
                pe.wait_ge(s("sr_out"), i * 2 + 1)
                wide(*G, 0, 0, 0, h_pair, 0)
                pe.wait_ge(s("w2_in"), i * 16 + 16)
                pe.wait_ge(s("o_out"), i + 1)
                for dt in range(2):
                    last = M(psum[:, 6 + dt, 0:L], w2h[:, dt * P:(dt + 1) * P], lrT[:, :], start=True, stop=True)
                last.then_inc(s("logits"), 1)
                wide(*G, 1, 1, 0, h_pair, 0)
                wide(*G, 2, 0, 2, h_pair)
                wide(*G, 3, 1, 2, h_pair)
                pe.wait_ge(s("kd_done"), i + 1)
                pe.wait_ge(s("ro_done"), i + 1)
                wide(*G, 4, 0, 0, h_pair, 0)
                wide(*G, 5, 1, 0, h_pair, 0)
                T = nc.tensor.transpose
                for dt in range(2):
                    d = slice(dt * P, (dt + 1) * P)
                    T(psum[:, 6, d], kd[:, dt, META:META + P], ident[:, :])
                    T(psum[0:META, 6, DK + dt * P:DK + (dt + 1) * P], kd[:, dt, 0:META], ident[:, :])
                    last = T(psum[0:CHUNK, 7, d], kd[:, dt, META + P:META + P + CHUNK], ident[:, :])
                last.then_inc(s("kd_turned"), 1)
                pe.wait_ge(s("qd_done"), i + 1)
                for c in range(2):
                    for dt in range(2):
                        last = M(psum[:, 5, c * P:(c + 1) * P], ke[:, dt, META + c * P:META + (c + 1) * P],
                                 qd[:, dt, c * P:(c + 1) * P], start=dt == 0, stop=dt == 1)
                last.then_inc(s("a_in"), 1)
                wide(*G, 6, 0, 2, h_pair, 0)
                turn_values(i, 0)
                wide(*G, 7, 1, 2, h_pair, 0)
                wide(*G, 8, 0, 0, h_pair)
                pe.wait_ge(s("am_done"), i + 1)
                turn_values(i, 1)
                wide(*G, 9, 1, 0, h_pair)
                pe.wait_ge(s("v_out"), i * 2 + 2)
                for c in range(4):
                    for dt in range(2):
                        n = 2 * c + dt
                        d = slice(dt * P, (dt + 1) * P)
                        if n >= 4:
                            pe.wait_ge(s("st_done"), i * 8 + (n - 3))
                        o = psum[:, (6, 7, 4, 5)[n % 4], :]
                        if c == 0:
                            last = M(o, kdn0[:, d], va0[:, :], start=True, stop=True)
                        else:
                            t, r = (c - 1) // 2, (c - 1) % 2
                            rows = slice(CHUNK * r, CHUNK * r + CHUNK)
                            last = M(o, kdn[rows, t, d], va[rows, t, :], start=True, stop=True)
                        last.then_inc(s("ds_in"), 1)
                wide(*G, 10, 0, 2, h_pair)
                pe.wait_ge(s("st_done"), i * 8 + 8)
                for v in range(4):
                    vs = slice(v * P, (v + 1) * P)
                    for c in range(2):
                        col = (v % 2) * SEQ + c * P
                        o = psum[:, 6 + v // 2, col:col + P]
                        M(o, va[:, c, vs], am[:, c, :], start=True, stop=False)
                        for r in range(2):
                            q = 2 * c + r
                            for dt in range(2):
                                last = M(o[:, r * CHUNK:(r + 1) * CHUNK], st[:, q, dt, vs],
                                         qd[:, dt, q * CHUNK:(q + 1) * CHUNK], start=False, stop=dt == 1 and r == 1)
                last.then_inc(s("o_added"), 1)
                wide(*G, 11, 1, 2, h_pair)
                pe.wait_ge(s("o_sq"), i + 1)
                for v in range(4):
                    last = M(psum[:, 4, 0:SEQ], ones[:, :], osq[:, v, :], start=v == 0, stop=v == 3)
                last.then_inc(s("o_sums"), 1)

            pe.wait_ge(s("zb_out"), PAIRS)
            pe.wait_ge(s("om_out"), PAIRS)
            with pe.Fori(0, GLA_HEADS) as i:
                gla_turn(i)

            pe.wait_ge(s("sr_out"), 2 * GLA_HEADS)

            def merge_turn(i, first):
                for b in range(2):
                    G = (P_MRG, N_MRG, i)
                    wait(pe, s("sa_done"), i * 2 + b)
                    for kh in range(2):
                        wide(*G, 6 * b + kh, kh, 0, h_pair)
                    wait(pe, s("mf_done"), i * 2 + b)
                    if first and b == 0:
                        pe.wait_ge(s("sr_out"), 2 * GLA_HEADS + 1)
                    for kh in range(2):
                        if first and b == 0:
                            pe.wait_ge(s("o_lo"), 2 * kh + 2)
                        wide(*G, 6 * b + 2 + kh, kh, 2, (o_hi_g, o_lo_g))
                    if first and b == 0:
                        pe.wait_ge(s("ro_done"), GLA_HEADS + 1)
                        pe.wait_ge(s("o_lo"), 8)
                    for kh in range(2):
                        wide(*G, 6 * b + 4 + kh, kh, 4, (o_hi_m, o_lo_m))

            merge_turn(0, True)
            with pe.Fori(1, 4) as i:
                merge_turn(i, False)

            def out_turn(i, first):
                for b in range(2):
                    if not first:
                        pe.wait_ge(s(f"x2_out{b}"), i)
                    elif b:
                        pe.wait_ge(s("mf_done"), 8)
                    for kh in range(2):
                        hi_lo = [w[:, :].rearrange("p (k c) -> p k c", k=8) for w in panel(P_OUT, N_OUT, i, 2 * b + kh)]
                        if first and b == kh == 0:
                            pe.wait_ge(s("merged"), 5)
                        for k in range(8):
                            kk = 8 * kh + k
                            if first and b == 0 and kh == 1 and k % 2 == 0:
                                pe.wait_ge(s("merged"), kk // 2 + 2)
                            for m in range(2):
                                last = three(psum[:, 2 * b + m, 0:SEQ], [w[:, k, m * P:(m + 1) * P] for w in hi_lo],
                                             [m_hi[:, kk, :], m_lo[:, kk, :]], kk == 0, False, skip=True)
                            if k == 3:
                                second_half(P_OUT, N_OUT, i, 2 * b + kh, last)
                        if kh == 0:
                            last.then_inc(used, 1)
                    pe.wait_ge(s(f"xs_in{b}"), i * 16 + 16)
                    for m in range(2):
                        for t in range(2):
                            last = M(psum[:, 2 * b + m, t * P:(t + 1) * P], xs[:, b, t, m * P:(m + 1) * P], ident[:, :],
                                     start=False, stop=t == 1, skip_group_check=True)
                    last.then_inc(used, 1)

            pe.wait_ge(s("sa_done"), 8)
            out_turn(0, True)
            with pe.Fori(1, 4) as i:
                out_turn(i, False)

            def ff_turn(i, first):
                if first:
                    pe.wait_ge(s("x2_out0"), 5)
                    pe.wait_ge(s("h2_lo_done"), 4)
                else:
                    pe.wait_ge(s("gate_out"), i)
                wide(P_FF, N_FF, i, 0, 0, 0, (h2_hi, h2_lo))
                if first:
                    pe.wait_ge(s("h2_lo_done"), 8)
                wide(P_FF, N_FF, i, 1, 1, 0, (h2_hi, h2_lo))
                if first:
                    pe.wait_ge(s("x2_sum"), 1)
                    M(psum[:, 4, 0:SEQ], ones[:, :], ssum[:, 0, :], start=True, stop=True).then_inc(s("x2_sums"), 1)
                pe.wait_ge(s("af_done"), i + 1)
                for kh in range(2):
                    wide(P_FF, N_FF, i, 2 + kh, kh, 2, (h2_hi, h2_lo))

            ff_turn(0, True)
            with pe.Fori(1, FF // 256) as i:
                ff_turn(i, False)

            def down(i, c, first, last_one):
                hi_lo = [w[:, :].rearrange("p (k c) -> p k c", k=4) for w in panel(P_DN, N_DN, i, c)]
                for k in range(4):
                    if k == 2:
                        second_half(P_DN, N_DN, i, c, last)
                    rhs = [t[:, bass.ds(i * 4 + k, 1), :].rearrange("p a q -> p (a q)") for t in (a_hi, a_lo)]
                    for m in range(4):
                        o = psum[:, 2 * c + m // 2, (m % 2) * SEQ:(m % 2 + 1) * SEQ]
                        last = three(o, [w[:, k, m * P:(m + 1) * P] for w in hi_lo], rhs,
                                     first and k == 0 and m % 2 == 0, last_one and k == 3, skip=True)
                last.then_inc(used, 1)

            pe.wait_ge(s("gate_out"), FF // 256)
            down(0, 0, True, False)
            pe.wait_ge(s("af_done"), FF // 256 + 1)
            down(0, 1, True, False)
            pe.wait_ge(s("a_lo_done"), FF // 256 + 1)
            for c in range(2, 4):
                down(0, c, True, False)
            last_turn = FT // 4 - 1
            with pe.Fori(1, last_turn) as i:
                for c in range(4):
                    down(i, c, False, False)

            def turn(c):
                pe.wait_ge(s("y_done"), c + 1)
                for t in range(2):
                    for m in range(4):
                        last = nc.tensor.transpose(psum[:, 2 * c + t, m * P:(m + 1) * P], yT[:, c % 2, m, t * P:(t + 1) * P],
                                                   ident[:, :])
                last.then_inc(s("y_turned"), 1)

            for c in range(4):
                down(last_turn, c, False, True)
                if c:
                    turn(c - 1)
            turn(3)


def tables():
    i = np.arange(P)
    f32 = np.float32
    swap = np.zeros((ROPE, ROPE), f32)
    h = ROPE // 2
    swap[np.arange(h) + h, np.arange(h)] = -1.0
    swap[np.arange(h), np.arange(h) + h] = 1.0
    eye = np.eye(ROPE, dtype=f32)
    causal = np.zeros((P, L), f32)
    causal[:, META + P:] = np.where(i[None, :] <= i[:, None], 0.0, NEG)
    inv = (1.0 / (f32(10000.0) ** (np.arange(0, ROPE, 2, dtype=f32) / f32(ROPE)))).astype(f32)
    ang = np.tile(np.arange(L, dtype=f32)[None, :] * inv[:, None], (4, 1))
    keep = np.ones((P, L), f32)
    keep[:, 0] = 0.0
    keep[:, META::CHUNK] = 0.0
    return {
        "ident": np.eye(P, dtype=f32),
        "rot2": np.kron(np.eye(2, dtype=f32), swap),
        "dup": np.stack([np.tile(eye, (1, 2)), np.tile(swap, (1, 2))], 1),
        "causal": causal,
        "cos2": np.cos(ang),
        "sin2": np.sin(ang),
        "inchunk": ((i[:, None] <= i[None, :]) & (i[:, None] // CHUNK == i[None, :] // CHUNK)).astype(np.int32),
        "keep": keep,
    }


def kernel(x, meta_tokens, norm1_g, w_in, gla_gate_w2, gla_gate_b, gla_onorm_g, w_branch_a, q_a_norm_g, w_uq,
           kv_a_norm_g, w_ukv, q_norm_g, k_norm_g, w_branch_b, w_out, norm2_g, w_gate_up, w_down):
    import concourse.bacc as bacc
    from concourse.bass_utils import run_bass_kernel_spmd

    def columns(g):
        return np.asarray(g).reshape(-1, P).T

    qg, kg = np.asarray(q_norm_g)[0], np.asarray(k_norm_g)[0]
    gains = np.concatenate(
        [columns(norm1_g), columns(norm2_g), columns(gla_onorm_g), columns(q_a_norm_g), columns(kv_a_norm_g),
         columns(qg[:NOPE]), columns(np.concatenate([qg[NOPE:], qg[NOPE:]])),
         columns(kg[:NOPE]), columns(np.concatenate([kg[NOPE:], kg[NOPE:]])), columns(gla_gate_b)], axis=1)
    arrays = {
        "x": x, "meta": meta_tokens, "w_in": w_in, "w2": gla_gate_w2, "w_a": w_branch_a, "w_uq": w_uq, "w_ukv": w_ukv,
        "w_b": w_branch_b, "w_out": w_out, "w_gu": w_gate_up, "w_dn": w_down, "gains": gains,
    }
    arrays = {f"in_{n}": np.ascontiguousarray(a) for n, a in arrays.items()}
    fixed = tables()
    arrays |= {f"const_{n}": np.ascontiguousarray(a) for n, a in fixed.items()}
    nc = bacc.Bacc("TRN2", target_bir_lowering=False, num_devices=1)
    ap = {n: nc.dram_tensor(n, a.shape, mybir.dt.from_np(a.dtype), kind="ExternalInput").ap() for n, a in arrays.items()}
    out = nc.dram_tensor("out", (1, SEQ, D), F32, kind="ExternalOutput").ap()

    def two_d(n):
        a = ap[f"in_{n}"]
        return a.rearrange("o k c -> (o k) c")

    build(nc, ap["in_x"], ap["in_meta"], two_d("w_in"), two_d("w2"), two_d("w_a"), two_d("w_uq"), two_d("w_ukv"),
          two_d("w_b"), two_d("w_out"), two_d("w_gu"), two_d("w_dn"), ap["in_gains"],
          {n: ap[f"const_{n}"] for n in fixed}, out)
    r = run_bass_kernel_spmd(nc, [arrays], core_ids=[0])
    return r.results[0]["out"]
```

```python
from contextlib import ExitStack

import numpy as np

import concourse.bass as bass
from concourse import mybir

F32 = mybir.dt.float32
F32R = mybir.dt.float32r
I32 = mybir.dt.int32
ACT = mybir.ActivationFunctionType
ALU = mybir.AluOpType

P = 128
D = 2048
META = 16
SEQ = 256
L = META + SEQ
KT = D // P
EPS = 1e-6
GLA_HEADS, DK, DV, RANK, TAU, CHUNK = 4, 256, 512, 16, 16.0, 64
HEADS, LORA, NOPE, ROPE, DVM = 16, 512, 128, 64, 128
QK = NOPE + ROPE
LT = LORA // P
FF = 5632
FT = FF // P
NEG = -1e30
LN_EXP = "natural_log_exp_and_others"

C_Q, C_K, C_V, C_R = 0, 1024, 2048, 4096
C_LR = 6144
C_CQ = C_LR + RANK
C_CKV = C_CQ + LORA
C_KR = C_CKV + LORA
C_ZA = C_KR + ROPE
C_ZB = C_ZA + D

PANEL = 2048
RAW, SPL = 4, 2
PAIRS = HEADS // 2
P_LAT = 1
P_MLA, N_MLA = P_LAT + 8, 4
P_GLA, N_GLA = P_MLA + N_MLA * PAIRS, 12
P_MRG, N_MRG = P_GLA + N_GLA * GLA_HEADS, 12
P_OUT, N_OUT = P_MRG + N_MRG * 4, 4
P_FF, N_FF = P_OUT + N_OUT * 4, 4
P_DN, N_DN = P_FF + N_FF * (FF // 256), 4
PANELS = P_DN + N_DN * (FT // 4)

G_1, G_2, G_O, G_QA, G_KVA, G_QN, G_QR, G_KN, G_KR, G_B, G_ALL = 0, 16, 32, 36, 40, 44, 45, 46, 47, 48, 56

TOK = ((0, META), (META, META + P), (META + P, L))


def wait(eng, sem, value):
    if isinstance(value, int) and value <= 0:
        return
    eng.wait_ge(sem, value)


class Chain:

    def __init__(self, eng, sem):
        self.eng, self.sem, self.total, self.base, self.k = eng, sem, 0, 0, 0

    def link(self, ins):
        self.k += 1
        ins.then_inc(self.sem, 1)
        self.eng.wait_ge(self.sem, self.base + self.k)

    def enter(self, turn, per):
        self.close()
        self.base, self.per = turn * per + self.total, per

    def leave(self, turns):
        assert self.k == self.per, (self.k, self.per)
        self.total += turns * self.per
        self.base, self.k = self.total, 0

    def close(self):
        self.total += self.k
        self.base, self.k = self.total, 0


def build(nc, x, meta, w_in, w2, w_a, w_uq, w_ukv, w_b, w_out, w_gu, w_dn, gains, consts, out):
    ctx = ExitStack()
    with ctx:
        def sem(name):
            return ctx.enter_context(nc.semaphore(name))

        BASE = 16512
        top = [0]

        def put(name, shape, dt=F32, at=None):
            size = -(-4 * int(np.prod(shape[1:])) // 32) * 32
            if at is None:
                at = top[0]
                top[0] += size
            return nc.alloc_sbuf_tensor_at(name, list(shape), dt, offset=BASE + at)

        raw = [put(f"raw{s}", [P, PANEL]) for s in range(RAW)]
        whi = [put(f"whi{s}", [P, PANEL], F32R) for s in range(SPL)]
        wlo = [put(f"wlo{s}", [P, PANEL], F32R) for s in range(SPL)]
        ident = put("ident", [P, P])
        ones = put("ones", [P, P])
        gain = put("gain", [P, G_ALL])
        tick = put("tick", [P, 1])
        after_const = top[0]
        rot2 = put("rot2", [P, P])
        LR = slice(ROPE, ROPE + RANK)
        w2h = put("w2h", [ROPE + RANK, DK], at=top[0])
        dup = put("dup", [ROPE, 2, P])
        causal = put("causal", [P, L])
        cos2 = put("cos2", [P, L])
        sin2 = put("sin2", [P, L])
        inchunk = put("inchunk", [P, P], I32)
        keep = put("keep", [P, L])
        h_hi = put("h_hi", [P, KT, L], F32R)
        h_lo = put("h_lo", [P, KT, L], F32R)
        mixers = top[0]
        o_mla = put("o_mla", [P, KT, SEQ])
        zb = put("zb", [P, KT, SEQ])
        lrT = put("lrT", [ROPE + RANK, L])
        work = top[0]
        ckv_hi = put("ckv_hi", [P, LT, L], F32R)
        ckv_lo = put("ckv_lo", [P, LT, L], F32R)
        cq_hi = put("cq_hi", [P, LT, SEQ], F32R)
        cq_lo = put("cq_lo", [P, LT, SEQ], F32R)
        krr = put("krr", [P, L])
        krsq = put("krsq", [ROPE, 2, L])
        after_lat = top[0]
        qn = put("qn", [P, 2, SEQ])
        qr = put("qr", [P, SEQ])
        qrg = put("qrg", [P, SEQ])
        kn = put("kn", [P, 2, L])
        vm0 = put("vm0", [META, 2, DVM])
        vm = put("vm", [P, 2, 2, DVM])
        qnsq = put("qnsq", [P, 2, SEQ])
        qrsq = put("qrsq", [P, SEQ])
        knsq = put("knsq", [P, 2, L])
        rq = put("rq", [P, 2, SEQ])
        rk = put("rk", [P, 2, L])
        qs = put("qs", [P, 2, SEQ])
        ks = put("ks", [P, 2, L])
        qc = put("qc", [P, SEQ])
        qsn = put("qsn", [P, SEQ])
        qrs = put("qrs", [P, SEQ])
        krs = put("krs", [P, 2, L])
        sc0 = put("sc0", [P, 2, META + P])
        sc1 = put("sc1", [P, 2, L])
        pt0 = put("pt0", [META, 2, SEQ])
        pt1 = put("pt1", [P, 2, SEQ])
        pt2 = put("pt2", [P, 2, P])
        mx = put("mx", [P, 4])
        nb = put("nb", [P, 4])
        sm = put("sm", [P, 4])
        rs = put("rs", [P, 4])
        end_mla = top[0]
        top[0] = after_lat
        kr = put("kr", [ROPE, L])
        krg = put("krg", [ROPE, L])
        krc = put("krc", [P, L])
        krn = put("krn", [P, L])
        lat = put("lat", [P, 2, LT, L])
        latsq = put("latsq", [P, 2, LT, L])
        rlat = put("rlat", [P, 2, L])
        end_lat = top[0]
        top[0] = mixers
        xm = put("xm", [META, D])
        xn = put("xn", [P, 2, D])
        xT = put("xT", [P, KT, L])
        xsq = put("xsq", [P, KT, L])
        r1 = put("r1", [P, L])
        end_x = top[0]
        top[0] = work
        o_gla = put("o_gla", [P, KT, SEQ])
        gx = put("gx", [P, 2, L])
        gl = put("gl", [P, 2, L])
        gb = put("gb", [P, 2, L])
        eb = put("eb", [P, 2, L])
        enb = put("enb", [P, 2, L])
        vT = gx
        kf = gl
        ebp = put("ebp", [P, 2, 1])
        qd = put("qd", [P, 2, SEQ])
        qx = put("qx", [P, 2, SEQ])
        kx = put("kx", [P, 2, CHUNK])
        ke = put("ke", [P, 2, L])
        kd = put("kd", [P, 2, L])
        kdn0 = put("kdn0", [P, DK])
        kdn = put("kdn", [P, DK])
        va0 = put("va0", [P, DV])
        va = put("va", [P, 2, DV])
        am = put("am", [P, 2, P])
        st = put("st", [P, 2, 2, DV])
        osq = put("osq", [P, 4, SEQ])
        sr = put("sr", [P, 4, SEQ])
        ro = enb[:, 0, 0:SEQ]
        end_gla = top[0]
        o_lo_m = put("o_lo_m", [P, KT, SEQ], F32R, at=mixers)
        m_lo = put("m_lo", [P, KT, SEQ], F32R, at=mixers + 4 * KT * SEQ)
        o_lo_g = put("o_lo_g", [P, KT, SEQ], F32R, at=work)
        top[0] = work + 4 * KT * SEQ
        o_hi_m = put("o_hi_m", [P, KT, SEQ], F32R)
        o_hi_g = put("o_hi_g", [P, KT, SEQ], F32R)
        m_hi = put("m_hi", [P, KT, SEQ], F32R)
        sb = put("sb", [P, 2, SEQ])
        end_mrg = top[0]
        sa = put("sa", [P, 2, SEQ], at=after_const)
        mb = put("mb", [P, 2, SEQ], at=after_const + 2048)
        mf = put("mf", [P, 2, SEQ], at=after_const + 4096)
        top[0] = after_const
        x2 = put("x2", [P, KT, SEQ])
        h2_hi = put("h2_hi", [P, KT, SEQ], F32R)
        h2_lo = put("h2_lo", [P, KT, SEQ], F32R)
        a_hi = put("a_hi", [P, FT, SEQ], F32R)
        a_lo = put("a_lo", [P, FT, SEQ], F32R)
        sg = put("sg", [P, 2, SEQ])
        af = put("af", [P, 2, SEQ])
        r2 = put("r2", [P, 2, SEQ])
        end_ff = top[0]
        for name, end in (("mla", end_mla), ("lat", end_lat), ("x", end_x), ("gla", end_gla), ("mrg", end_mrg), ("ff", end_ff)):
            assert BASE + end <= nc.sbuf_usable_end, (name, BASE + end - nc.sbuf_usable_end)
        top[0] = work
        xs = put("xs", [P, 2, 2, 2 * P])
        x2sq = put("x2sq", [P, 2, SEQ])
        ssum = put("ssum", [P, 2, SEQ])
        yT = put("yT", [P, 2, 4, SEQ], at=after_const + 4 * KT * SEQ)
        yn = put("yn", [P, 2, 2, 4 * P], at=after_const + 4 * KT * SEQ + 8192)

        psum = ctx.enter_context(nc.psum_tensor("psum", [P, 8, 512], F32))

        def pair(b, n):
            return psum[:, b:b + 2, 0:n]

        raw_in = [sem(f"raw_in{s}") for s in range(RAW)]
        hi_done = sem("hi_done")
        lo_done = sem("lo_done")
        used = sem("used")
        act_own, dve_own, pool_own = sem("act_own"), sem("dve_own"), sem("pool_own")

        block = ctx.enter_context(nc.Block())

        def after(p0, per, i, j):
            return i * (2 * per) + 2 * (p0 + j + 1)

        def raw_value(p0, per, i, j):
            p = p0 + j
            return i * (16 * per // RAW) + 16 * (p // RAW + 1)

        def slot(p0, j, n):
            return (p0 + j) % n

        UQ_PARTS = ((0, NOPE, 0), (NOPE, QK, LT * 2 * NOPE))

        def uq_part(t, a, b, at, from_raw):
            if from_raw:
                return t[:, 0:LT * 2 * QK].rearrange("p (k h c) -> p k h c", k=LT, h=2)[:, :, :, a:b]
            return t[:, at:at + LT * 2 * (b - a)].rearrange("p (k h c) -> p k h c", k=LT, h=2)

        named = {}

        def s(name):
            if name not in named:
                named[name] = sem(name)
            return named[name]

        FREE = {"pe": ("norm_sums", "o_added", "p_turned", "pv_done"),
                "act": ("sr_out", "o_out", "ro_done"),
                "dve": ("x2_out0", "x2_out1", "af_done", "gated", "merged", "a_lo_done")}

        def free_at_start(eng, owner):
            for name in FREE[owner]:
                eng.sem_inc(s(name), 1)

        @block.sync
        def _(sp):
            def load(p0, per, i, j, dst, src):
                if p0 + j >= RAW:
                    sp.wait_ge(lo_done, after(p0, per, i, j) - 2 * RAW)
                sp.dma_start(dst, src).then_inc(raw_in[slot(p0, j, RAW)], 16)

            def wide(p0, per, i, j, w, row0, col0):
                dst = raw[slot(p0, j, RAW)][:, :].rearrange("p (k c) -> p k c", k=8)
                src = w[row0:row0 + 8 * P, :].rearrange("(k p) c -> p k c", p=P)[:, :, bass.ds(col0, 256)]
                load(p0, per, i, j, dst, src)

            sp.dma_start(ident[:, :], consts["ident"]).then_inc(s("ident_in"), 16)
            sp.dma_start(xm[:, :], meta).then_inc(s("xm_in"), 16)
            xv = x.rearrange("o (t p) d -> p (o t) d", p=P)
            for f in range(4):
                sp.dma_start(xn[:, :, f * 512:(f + 1) * 512], xv[:, :, f * 512:(f + 1) * 512]).then_inc(s(f"xn_in{f}"), 16)
            sp.dma_start(gain[:, :], gains).then_inc(s("gain_in"), 16)
            small = raw[0][:, 0:KT * (RANK + ROPE)].rearrange("p (k c) -> p k c", k=KT)
            wk = w_in.rearrange("(k p) c -> p k c", p=P)
            sp.dma_start(small[:, :, LR], wk[:, :, C_LR:C_LR + RANK]).then_inc(s("lr_in"), 16)
            sp.dma_start(small[:, :, 0:ROPE], wk[:, :, C_KR:C_KR + ROPE]).then_inc(raw_in[0], 16)

            def latent(j):
                wide(P_LAT, 8, 0, j, w_in, (j % 2) * 8 * P, (C_CKV, C_CQ)[j // 4] + 256 * (j // 2 % 2))

            for j in range(3):
                latent(j)
            for t, name in ((rot2, "rot2"), (dup, "dup"), (causal, "causal"), (cos2, "cos2"), (sin2, "sin2"),
                            (inchunk, "inchunk"), (keep, "keep")):
                sp.dma_start(t[:], consts[name]).then_inc(s(f"const_{name}"), 16)
            for j in range(3, 8):
                latent(j)
            uq = w_uq.rearrange("(k p) c -> p k c", p=P)
            ukv = w_ukv.rearrange("(k p) c -> p k c", p=P)

            def load_uq(i, j, col):
                load(P_MLA, N_MLA, i, j, raw[slot(P_MLA, j, RAW)][:, 0:LT * 2 * QK].rearrange("p (k c) -> p k c", k=LT),
                     uq[:, :, bass.ds(col, 2 * QK)])

            def load_ukv(i, j, col):
                load(P_MLA, N_MLA, i, j, raw[slot(P_MLA, j, RAW)][:, :].rearrange("p (k c) -> p k c", k=LT),
                     ukv[:, :, bass.ds(col, 512)])

            load_ukv(0, 0, 0)
            load_uq(0, 1, 0)
            for kh in range(2):
                wide(P_MLA, N_MLA, 0, 2 + kh, w_in, kh * 8 * P, C_ZB)
            with sp.Fori(1, PAIRS) as i:
                uq_col, ukv_col = sp.snap(i * (2 * QK)), sp.snap(i * 512)
                load_uq(i, 0, uq_col)
                load_ukv(i, 1, ukv_col)
                for kh in range(2):
                    wide(P_MLA, N_MLA, i, 2 + kh, w_in, kh * 8 * P, i * 256 + C_ZB)
            with sp.Fori(0, GLA_HEADS) as i:
                for j, col in enumerate((C_K, C_Q)):
                    for kh in range(2):
                        wide(P_GLA, N_GLA, i, 2 * j + kh, w_in, kh * 8 * P, i * DK + col)
                    if j == 0:
                        sp.wait_ge(s("kr_dup"), 1)
                        sp.dma_start(w2h[LR, :], w2[:, bass.ds(i * DK, DK)]).then_inc(s("w2_in"), 16)
                for b in range(2):
                    for kh in range(2):
                        wide(P_GLA, N_GLA, i, 4 + 2 * b + kh, w_in, kh * 8 * P, i * DV + (C_V + 256 * b))
                for b in range(2):
                    for kh in range(2):
                        wide(P_GLA, N_GLA, i, 8 + 2 * b + kh, w_in, kh * 8 * P, i * DV + (C_R + 256 * b))
            with sp.Fori(0, 4) as i:
                for b in range(2):
                    for j, (w, col) in enumerate(((w_in, C_ZA), (w_a, 0), (w_b, 0))):
                        for kh in range(2):
                            step = P >> j
                            at = (i * (512 // step) + 256 * b // step) * step + col if j else i * 512 + (col + 256 * b)
                            wide(P_MRG, N_MRG, i, 6 * b + 2 * j + kh, w, kh * 8 * P, at)
            with sp.Fori(0, 4) as i:
                for b in range(2):
                    for kh in range(2):
                        wide(P_OUT, N_OUT, i, 2 * b + kh, w_out, kh * 8 * P, i * 512 + 256 * b)
                    sp.wait_ge(used, after(P_MRG, N_MRG, 3, 11))
                    sp.wait_ge(used, after(P_OUT, N_OUT, i, 2 * b + 1) - 2 * N_OUT)
                    sp.dma_start(xs[:, b], xv[:, :, bass.ds(i * 512 + 256 * b, 256)]).then_inc(s(f"xs_in{b}"), 16)
            with sp.Fori(0, FF // 256) as i:
                for j in range(2):
                    for kh in range(2):
                        wide(P_FF, N_FF, i, 2 * j + kh, w_gu, kh * 8 * P, i * 256 + FF * j)
            dn = w_dn.rearrange("(g k p) c -> g p k c", p=P, k=4)
            with sp.Fori(0, FT // 4) as i:
                for c in range(4):
                    load(P_DN, N_DN, i, c, raw[slot(P_DN, c, RAW)][:, :].rearrange("p (k c) -> p k c", k=4),
                         dn[bass.ds(i, 1), :, :, c * 512:(c + 1) * 512].rearrange("g p k c -> p (g k) c"))
            ov = out.rearrange("o (t p) d -> p (o t) d", p=P)
            for c in range(4):
                sp.wait_ge(s("yn_done"), 2 * (c + 1))
                sp.dma_start(ov[:, :, c * 512:(c + 1) * 512], yn[:, c % 2]).then_inc(s(f"out_done{c}"), 16)
            for c in range(4):
                sp.wait_ge(s(f"out_done{c}"), 16)

        @block.gpsimd
        def _(pool):
            own = Chain(pool, pool_own)

            def mult(o, a):
                return nc.gpsimd.tensor_tensor(o, a, a, ALU.mult)

            nc.gpsimd.memset(ones[:, :], 1.0).then_inc(s("ones_set"), 1)
            for q in range(3):
                pool.wait_ge(s("x_sq"), 4 * q + 4)
                nc.gpsimd.tensor_tensor(xsq[:, 4 * q:4 * q + 2, :], xsq[:, 4 * q:4 * q + 2, :], xsq[:, 4 * q + 2:4 * q + 4, :],
                                        ALU.add).then_inc(s("x_sq2"), 1)
            for g in range(1, KT // 2, 2):
                t = slice(2 * g, 2 * g + 2)
                pool.wait_ge(s("h_hi_done"), g + 1)
                nc.gpsimd.tensor_tensor(h_lo[:, t, :], xT[:, t, :], h_hi[:, t, :].bitcast(F32),
                                        ALU.subtract).then_inc(s("h_lo_pool"), 1)
            pool.wait_ge(s("kr_sq"), 2)
            pool.wait_ge(s("lat_lo"), 2)
            with pool.Fori(0, PAIRS) as i:
                own.enter(i, 3)
                pool.wait_ge(s("norm_sums"), i + 1)
                pool.wait_ge(s("qn_out"), i + 1)
                mult(qnsq[:, :, :], qn[:, :, :])
                pool.wait_ge(s("qr_out"), i + 1)
                own.link(mult(qrsq[:, :], qr[:, :]))
                for h in range(2):
                    rows = slice(ROPE * h, ROPE * h + ROPE)
                    own.link(nc.gpsimd.tensor_tensor(qnsq[rows, h, :], qnsq[rows, h, :], qrsq[rows, :], ALU.add))
                pool.wait_ge(s("kn_sq"), i + 1)
                nc.gpsimd.tensor_tensor(knsq[0:ROPE, :, :], knsq[0:ROPE, :, :], krsq[:, :, :], ALU.add).then_inc(s("mla_sq"), 1)
            own.leave(PAIRS)
            with pool.Fori(0, GLA_HEADS) as i:
                own.enter(i, 1)
                pool.wait_ge(s("o_sq"), i + 1)
                own.link(nc.gpsimd.tensor_tensor(osq[:, 0:2, :], osq[:, 0:2, :], osq[:, 2:4, :], ALU.add))
                nc.gpsimd.tensor_tensor(osq[:, 0, :], osq[:, 0, :], osq[:, 1, :], ALU.add).then_inc(s("o_sq_sum"), 1)
            own.leave(GLA_HEADS)
            pool.wait_ge(used, after(P_MRG, N_MRG, 3, 11))
            own.link(nc.gpsimd.memset(ssum[:, :, :], 0.0))
            with pool.Fori(0, 4) as i:
                own.enter(i, 4)
                for b in range(2):
                    pool.wait_ge(s(f"x2_out{b}"), i + 2)
                    xb = x2[:, bass.ds(i * 4 + 2 * b, 2), :]
                    own.link(nc.gpsimd.tensor_tensor(x2sq[:, :, :], xb, xb, ALU.mult))
                    own.link(nc.gpsimd.tensor_tensor(ssum[:, :, :], ssum[:, :, :], x2sq[:, :, :], ALU.add))
            own.leave(4)
            nc.gpsimd.tensor_tensor(ssum[:, 0, :], ssum[:, 0, :], ssum[:, 1, :], ALU.add).then_inc(s("x2_sum"), 1)
            pool.wait_ge(s("r2_done"), 1)
            with pool.Fori(0, FF // 256) as i:
                pool.wait_ge(s("sg_done"), i + 1)
                nc.gpsimd.tensor_tensor(sg[:, :, :], sg[:, :, :], r2[:, :, :], ALU.mult).then_inc(s("sgr_done"), 1)

        @block.scalar
        def _(act):
            own = Chain(act, act_own)
            free_at_start(act, "act")
            A = nc.scalar.activation

            def split(p0, per, i, j, n=PANEL, uq=False):
                if p0 + j >= PANELS and isinstance(i, int) and i == 0:
                    return
                act.wait_ge(raw_in[slot(p0, j, RAW)], raw_value(p0, per, i, j))
                hi, src = whi[slot(p0, j, SPL)], raw[slot(p0, j, RAW)]
                for half in range(2):
                    if p0 + j >= SPL:
                        act.wait_ge(used, after(p0, per, i, j) - 2 * SPL - 1 + half)
                    if uq:
                        part = UQ_PARTS[half]
                        A(uq_part(hi, *part, False), uq_part(src, *part, True), ACT.Copy).then_inc(hi_done, 1)
                    else:
                        cols = slice(half * n // 2, (half + 1) * n // 2)
                        A(hi[:, cols], src[:, cols], ACT.Copy).then_inc(hi_done, 1)

            def panel_over(p0, per, i, j, uq=False):
                split(p0, per, i, j + SPL, uq=uq)
                act.wait_ge(used, after(p0, per, i, j))

            def rstd(o, sums, n):
                own.link(A(o, sums, ACT.Ln, bias=EPS, scale=1.0 / n))
                return A(o, o, ACT.Exp, scale=-0.5)

            act.preload_act_table_set(LN_EXP)
            for f in range(KT):
                act.wait_ge(s("x_turned"), f + 1)
                A(xT[:, f, :], psum[:, f % 4, 0:L], ACT.Copy).then_inc(s("xT_out"), 1)
            act.wait_ge(s("lr_in"), 16)
            split(0, 1, 0, 0, KT * (RANK + ROPE))
            act.wait_ge(s("x_sums"), 1)
            rstd(r1[:, :], psum[:, 4, 0:L], D).then_inc(s("r1_done"), 1)
            for g in range(KT // 2):
                act.wait_ge(s("h_done"), g + 1)
                A(h_hi[:, 2 * g:2 * g + 2, :], xT[:, 2 * g:2 * g + 2, :], ACT.Copy).then_inc(s("h_hi_done"), 1)
            split(0, 1, 0, 1)
            panel_over(0, 1, 0, 0)
            A(lrT[LR, :], psum[LR, 6, 0:L], ACT.Copy).then_inc(s("lr_out"), 1)
            A(kr[:, :], psum[0:ROPE, 6, 0:L], ACT.Copy).then_inc(s("kr_out"), 1)
            def latent_norm(side):
                lo, n = (META, SEQ) if side else (0, L)
                act.wait_ge(s("lat_sums"), side + 1)
                rstd(rlat[:, side, lo:L], psum[:, 6 + side, 0:n], LORA).then_inc(s("rlat_done"), 1)
                act.wait_ge(s("lat_done"), side + 1)
                A((cq_hi if side else ckv_hi)[:, :, :], lat[:, side, :, lo:L], ACT.Copy).then_inc(s("lat_hi"), 1)

            for b in range(4):
                side, lo, n = (0, 0, L) if b < 2 else (1, META, SEQ)
                for kh in range(2):
                    panel_over(P_LAT, 8, 0, 2 * b + kh, uq=b == 3 and kh == 1)
                    if b == 2 and kh == 0:
                        latent_norm(0)
                A(lat[:, side, 2 * (b % 2):2 * (b % 2) + 2, lo:L], pair(2 * (b % 2), n), ACT.Copy).then_inc(s("lat_out"), 1)
            latent_norm(1)

            def pt_out(i):
                act.wait_ge(s("p_turned"), i + 1)
                act.wait_ge(s("pv_done"), i)
                A(pt0[:, :, :], psum[0:META, 6:8, 0:SEQ], ACT.Copy)
                A(pt1[:, :, :], psum[:, 6:8, SEQ:2 * SEQ], ACT.Copy)
                A(pt2[:, :, :], psum[:, 4, 0:2 * P].rearrange("p (h q) -> p h q", h=2), ACT.Copy).then_inc(s("pt_out"), 1)

            def om_out(i):
                act.wait_ge(s("pv_done"), i + 1)
                dst = o_mla[:, bass.ds(i * 2 - 2, 2), :]
                A(dst, psum[:, 7, :].rearrange("p (h q) -> p h q", h=2), ACT.Copy).then_inc(s("om_out"), 1)

            def mla_turn(i, first, last):
                def queries_out():
                    A(qn[:, :, :], psum[:, 0, :].rearrange("p (h q) -> p h q", h=2), ACT.Copy).then_inc(s("qn_out"), 1)

                def rope_out():
                    A(qr[:, :], psum[:, 1, 0:SEQ], ACT.Copy).then_inc(s("qr_out"), 1)

                def rope_gain():
                    A(qrg[:, :], psum[:, 1, 0:SEQ], ACT.Copy, scale=gain[:, G_QR:G_QR + 1]).then_inc(s("qrg_out"), 1)

                def values_out():
                    A(vm0[:, :, :], psum[0:META, 1, SEQ:2 * SEQ].rearrange("p (h d) -> p h d", h=2), ACT.Copy)
                    A(vm[:, :, :, :].rearrange("p t h d -> p (t h d)"), psum[:, 5, :], ACT.Copy).then_inc(s("vm_out"), 1)

                panel_over(P_MLA, N_MLA, i, 0)
                if first:
                    act.wait_ge(s("lat_lo"), 2)
                    values_out()
                    A(kn[:, :, :], pair(2, L), ACT.Copy).then_inc(s("kn_out"), 1)
                    panel_over(P_MLA, N_MLA, i, 1)
                    queries_out()
                    rope_out()
                    rope_gain()
                else:
                    queries_out()
                    pt_out(i)
                    panel_over(P_MLA, N_MLA, i, 1)
                    rope_out()
                    A(kn[:, :, :], pair(2, L), ACT.Copy).then_inc(s("kn_out"), 1)
                    rope_gain()
                    om_out(i)
                    values_out()
                panel_over(P_MLA, N_MLA, i, 2, uq=not last)
                act.wait_ge(s("norm_sums"), i + 2)
                own.link(A(rq[:, :, :], psum[:, 4, :].rearrange("p (h q) -> p h q", h=2), ACT.Ln, bias=EPS, scale=1.0 / QK))
                A(rq[:, :, :], rq[:, :, :], ACT.Exp, scale=-0.5).then_inc(s("rq_done"), 1)
                A(rk[:, 0, :], psum[:, 1, 0:L], ACT.Ln, bias=EPS, scale=1.0 / QK)
                own.link(A(rk[:, 1, :], psum[:, 5, 0:L], ACT.Ln, bias=EPS, scale=1.0 / QK))
                A(rk[:, :, :], rk[:, :, :], ACT.Exp, scale=-0.5).then_inc(s("rk_done"), 1)
                panel_over(P_MLA, N_MLA, i, 3)
                A(zb[:, bass.ds(i * 2, 1), :], psum[:, 0:1, 0:SEQ], ACT.Copy)
                A(zb[:, bass.ds(i * 2 + 1, 1), :], psum[:, 6:7, 0:SEQ], ACT.Copy).then_inc(s("zb_out"), 1)
                act.wait_ge(s("nb_done"), i + 1)
                for h in range(2):
                    A(sc0[:, h, :], sc0[:, h, :], ACT.Exp, bias=nb[:, 2 * h:2 * h + 1], scale=QK ** -0.5,
                      accum_out=sm[:, 2 * h:2 * h + 1])
                    A(sc1[:, h, :], sc1[:, h, :], ACT.Exp, bias=nb[:, 2 * h + 1:2 * h + 2], scale=QK ** -0.5,
                      accum_out=sm[:, 2 * h + 1:2 * h + 2]).then_inc(s("p_exp"), 1)

            own.enter(0, 2)
            mla_turn(0, True, False)
            own.leave(1)
            with act.Fori(1, PAIRS - 1) as i:
                own.enter(i - 1, 2)
                mla_turn(i, False, False)
            own.leave(PAIRS - 2)
            own.enter(0, 2)
            mla_turn(PAIRS - 1, False, True)
            own.leave(1)

            def gla_turn(i, first):
                own.enter(0 if first else i - 1, 2)
                panel_over(P_GLA, N_GLA, i, 0)
                if first:
                    pt_out(PAIRS)
                act.wait_ge(s("logits"), i + 1)
                for dt in range(2):
                    bias = gain[:, bass.ds(i * 2 + (G_B + dt), 1)]
                    A(gx[:, dt, :], psum[:, 2 + dt, 0:L], ACT.Identity, bias=bias)
                    last = A(gl[:, dt, :], psum[:, 2 + dt, 0:L], ACT.Abs, bias=bias)
                last.then_inc(s("logits_out"), 1)
                act.wait_ge(s("logits_out"), i + 1)
                own.link(A(gl[:, :, :], gl[:, :, :], ACT.Exp, scale=-1.0))
                A(gl[:, :, :], gl[:, :, :], ACT.Ln, bias=1.0).then_inc(s("gl_done"), 1)
                panel_over(P_GLA, N_GLA, i, 1)
                if first:
                    om_out(PAIRS)
                act.wait_ge(s("decay"), i + 1)
                A(eb[:, :, :], gb[:, :, :], ACT.Exp, scale=1.0 / TAU)
                A(enb[:, :, :], gb[:, :, :], ACT.Exp, scale=-1.0 / TAU)
                kr3 = kf[:, :, 0:META + 3 * CHUNK]
                A(kr3, kr3, ACT.Exp, scale=1.0 / TAU).then_inc(s("decay_exp"), 1)
                for j in (2, 3, 4, 5):
                    panel_over(P_GLA, N_GLA, i, j)
                A(vT[:, :, :], pair(0, L), ACT.Copy).then_inc(s("vT_out"), 1)
                act.wait_ge(s("kd_turned"), i + 1)
                if first:
                    act.wait_ge(s("zeros_set"), 1)
                A(kdn[:, :], psum[:, 6, 0:DK], ACT.Copy)
                A(kdn0[0:META, :], psum[0:META, 6, DK:2 * DK], ACT.Copy).then_inc(s("kdn_out"), 1)

                def v_out(b):
                    act.wait_ge(s("v_turned"), i * 2 + (b + 1))
                    act.wait_ge(s("o_added"), i + 1)
                    c = slice(256 * b, 256 * b + 256)
                    A(va[:, :, c], psum[:, 4 + b, :].rearrange("p (t d) -> p t d", t=2), ACT.Copy)
                    A(va0[0:META, c], psum[0:META, 7, DK:2 * DK], ACT.Copy).then_inc(s("v_out"), 1)

                panel_over(P_GLA, N_GLA, i, 6)
                v_out(0)
                panel_over(P_GLA, N_GLA, i, 7)
                A(vT[:, :, :], pair(2, L), ACT.Copy).then_inc(s("vT_out"), 1)
                panel_over(P_GLA, N_GLA, i, 8)
                v_out(1)
                panel_over(P_GLA, N_GLA, i, 9)
                act.wait_ge(s("gated"), i + 1)
                A(sr[:, 0:2, :], pair(0, SEQ), ACT.Silu).then_inc(s("sr_out"), 1)
                panel_over(P_GLA, N_GLA, i, 10)
                act.wait_ge(s("o_added"), i + 2)
                o = psum[:, 6:8, :].rearrange("p b (v q) -> p (b v) q", q=SEQ)
                A(osq[:, :, :], o, ACT.Square).then_inc(s("o_sq"), 1)
                A(o_gla[:, bass.ds(i * 4, 4), :], o, ACT.Copy).then_inc(s("o_out"), 1)
                panel_over(P_GLA, N_GLA, i, 11)
                A(sr[:, 2:4, :], pair(2, SEQ), ACT.Silu).then_inc(s("sr_out"), 1)
                act.preload_act_table_set(LN_EXP)
                act.wait_ge(s("o_sums"), i + 1)
                own.link(A(ro, psum[:, 4, 0:SEQ], ACT.Ln, bias=EPS, scale=1.0 / DV))
                A(ro, ro, ACT.Exp, scale=-0.5).then_inc(s("ro_done"), 1)

            gla_turn(0, True)
            own.leave(1)
            with act.Fori(1, GLA_HEADS) as i:
                gla_turn(i, False)
            own.leave(GLA_HEADS - 1)

            def o_his(dst, src, groups):
                for q in groups:
                    A(dst[:, 4 * q:4 * q + 4, :], src[:, 4 * q:4 * q + 4, :], ACT.Copy).then_inc(s("o_hi"), 1)

            def merge_turn(i, first):
                for b in range(2):
                    blk = i * 2 + b
                    for j in range(2):
                        panel_over(P_MRG, N_MRG, i, 6 * b + j)
                        if first and b == 0:
                            if j == 0:
                                act.wait_ge(s("gated"), GLA_HEADS + 1)
                            o_his(*((o_hi_g, o_gla, (2, 3)), (o_hi_m, o_mla, range(4)))[j])
                    act.wait_ge(s("merged"), blk + 1)
                    A(sa[:, :, :], pair(0, SEQ), ACT.Sigmoid).then_inc(s("sa_done"), 1)
                    A(sb[:, :, :], zb[:, bass.ds(i * 4 + 2 * b, 2), :], ACT.Sigmoid).then_inc(s("sb_done"), 1)
                    for j in range(2, 6):
                        panel_over(P_MRG, N_MRG, i, 6 * b + j)
                    act.wait_ge(s("mf_done"), blk + 1)
                    A(m_hi[:, bass.ds(i * 4 + 2 * b, 2), :], mf[:, :, :], ACT.Copy).then_inc(s("m_hi_done"), 1)

            o_his(o_hi_g, o_gla, (0, 1))
            merge_turn(0, True)
            with act.Fori(1, 4) as i:
                merge_turn(i, False)
            with act.Fori(0, 4) as i:
                for b in range(2):
                    panel_over(P_OUT, N_OUT, i, 2 * b)
                    act.wait_ge(s("xs_turned"), i * 2 + (b + 1))
                    act.wait_ge(s("merged"), 9)
                    A(x2[:, bass.ds(i * 4 + 2 * b, 2), :], pair(4 + 2 * b, SEQ), ACT.Copy).then_inc(s("xs_out"), 1)
                    panel_over(P_OUT, N_OUT, i, 2 * b + 1)
                    act.wait_ge(s(f"x2_out{b}"), i + 2)
                    for m in range(2):
                        f = i * 4 + (2 * b + m)
                        last = A(h2_hi[:, bass.ds(f, 1), :], x2[:, bass.ds(f, 1), :], ACT.Copy,
                                 scale=gain[:, bass.ds(i * 4 + (G_2 + 2 * b + m), 1)])
                    last.then_inc(s("h2_hi_done"), 1)

            def ff_turn(i, first):
                panel_over(P_FF, N_FF, i, 0)
                panel_over(P_FF, N_FF, i, 1)
                if first:
                    act.preload_act_table_set(LN_EXP)
                    act.wait_ge(s("x2_sums"), 1)
                    own.link(A(r2[:, 0, :], psum[:, 4, 0:SEQ], ACT.Ln, bias=EPS, scale=1.0 / D))
                    own.link(A(r2[:, 0, :], r2[:, 0, :], ACT.Exp, scale=-0.5))
                    A(r2[:, 1, :], r2[:, 0, :], ACT.Copy).then_inc(s("r2_done"), 1)
                act.wait_ge(s("gate_out"), i + 1)
                A(sg[:, :, :], sg[:, :, :], ACT.Silu).then_inc(s("sg_done"), 1)
                panel_over(P_FF, N_FF, i, 2)
                panel_over(P_FF, N_FF, i, 3)
                act.wait_ge(s("af_done"), i + 2)
                A(a_hi[:, bass.ds(i * 2, 2), :], af[:, :, :], ACT.Copy).then_inc(s("a_hi_done"), 1)

            ff_turn(0, True)
            with act.Fori(1, FF // 256) as i:
                ff_turn(i, False)
            last_turn = FT // 4 - 1
            with act.Fori(0, last_turn) as i:
                for c in range(4):
                    panel_over(P_DN, N_DN, i, c)
            for c in range(2):
                split(P_DN, N_DN, last_turn, c + 2)
            for c in range(4):
                act.wait_ge(s("y_turned"), c + 1)
                if c >= 2:
                    act.wait_ge(s(f"out_done{c - 2}"), 16)
                A(yn[:, c % 2, 0, :], psum[:, 2 * c, :], ACT.Copy).then_inc(s("yn_done"), 1)
                A(yn[:, c % 2, 1, :], psum[:, 2 * c + 1, :], ACT.Copy).then_inc(s("yn_done"), 1)

        @block.vector
        def _(dve):
            own = Chain(dve, dve_own)
            V = nc.vector
            free_at_start(dve, "dve")

            def split(p0, per, i, j, n=PANEL, uq=False):
                k = slot(p0, j, SPL)
                lo, hi, src = wlo[k], whi[k], raw[slot(p0, j, RAW)]
                for half in range(2):
                    dve.wait_ge(hi_done, after(p0, per, i, j) - 1 + half)
                    if uq:
                        part = UQ_PARTS[half]
                        V.tensor_tensor(uq_part(lo, *part, False), uq_part(src, *part, True),
                                        uq_part(hi, *part, False).bitcast(F32), ALU.subtract).then_inc(lo_done, 1)
                    else:
                        cols = slice(half * n // 2, (half + 1) * n // 2)
                        V.tensor_tensor(lo[:, cols], src[:, cols], hi[:, cols].bitcast(F32), ALU.subtract).then_inc(lo_done, 1)

            def panel_over(p0, per, i, j, uq=False):
                split(p0, per, i, j + SPL, uq=uq)
                dve.wait_ge(used, after(p0, per, i, j))

            for f in range(KT):
                dve.wait_ge(s("xT_out"), f + 1)
                V.tensor_tensor(xsq[:, f, :], xT[:, f, :], xT[:, f, :], ALU.mult).then_inc(s("x_sq"), 1)
            split(0, 1, 0, 0, KT * (RANK + ROPE))
            dve.wait_ge(s("r1_done"), 1)
            dve.wait_ge(s("gain_in"), 16)
            for g in range(KT // 2 + 1):
                if g < KT // 2:
                    for f in range(2 * g, 2 * g + 2):
                        last = V.scalar_tensor_tensor(xT[:, f, :], xT[:, f, :], gain[:, G_1 + f:G_1 + f + 1], r1[:, :],
                                                      ALU.mult, ALU.mult)
                    last.then_inc(s("h_done"), 1)
                if g % 2:
                    t = slice(2 * g - 2, 2 * g)
                    dve.wait_ge(s("h_hi_done"), g)
                    V.tensor_tensor(h_lo[:, t, :], xT[:, t, :], h_hi[:, t, :].bitcast(F32),
                                    ALU.subtract).then_inc(s("h_lo_done"), 1)
            split(0, 1, 0, 1)
            panel_over(0, 1, 0, 0)
            dve.wait_ge(s("kr_out"), 1)
            for h in range(2):
                V.tensor_tensor(krsq[:, h, :], kr[:, :], kr[:, :], ALU.mult).then_inc(s("kr_sq"), 1)
            V.tensor_scalar(krg[:, :], kr[:, :], gain[0:ROPE, G_KR:G_KR + 1], None, ALU.mult).then_inc(s("krg_done"), 1)

            def latent_norm(side):
                lo = META if side else 0
                dve.wait_ge(s("rlat_done"), side + 1)
                g0 = G_QA if side else G_KVA
                for k in range(LT):
                    last = V.scalar_tensor_tensor(lat[:, side, k, lo:L], lat[:, side, k, lo:L],
                                                  gain[:, g0 + k:g0 + k + 1], rlat[:, side, lo:L], ALU.mult, ALU.mult)
                last.then_inc(s("lat_done"), 1)
                dve.wait_ge(s("lat_hi"), side + 1)
                hi, lw = (cq_hi, cq_lo) if side else (ckv_hi, ckv_lo)
                V.tensor_tensor(lw[:, :, :], lat[:, side, :, lo:L], hi[:, :, :].bitcast(F32),
                                ALU.subtract).then_inc(s("lat_lo"), 1)

            for b in range(4):
                side, lo = (0, 0) if b < 2 else (1, META)
                for kh in range(2):
                    panel_over(P_LAT, 8, 0, 2 * b + kh, uq=b == 3 and kh == 1)
                    if b == 2 and kh == 0:
                        latent_norm(0)
                if b == 0:
                    dve.wait_ge(s("kr_dup"), 1)
                    dve.wait_ge(s("const_cos2"), 16)
                    dve.wait_ge(s("const_sin2"), 16)
                    V.tensor_tensor(krc[:, :], cos2[:, :], psum[:, 4, 0:L], ALU.mult)
                    own.link(V.tensor_tensor(krn[:, :], sin2[:, :], psum[:, 5, 0:L], ALU.mult))
                    V.tensor_tensor(krr[:, :], krc[:, :], krn[:, :], ALU.add).then_inc(s("krr_done"), 1)
                dve.wait_ge(s("lat_out"), b + 1)
                t = slice(2 * (b % 2), 2 * (b % 2) + 2)
                V.tensor_tensor(latsq[:, side, t, lo:L], lat[:, side, t, lo:L], lat[:, side, t, lo:L],
                                ALU.mult).then_inc(s("lat_sq"), 1)
            latent_norm(1)

            def half(h):
                return slice(ROPE * h, ROPE * h + ROPE)

            def mla_turn(i, last_one):
                panel_over(P_MLA, N_MLA, i, 0)
                panel_over(P_MLA, N_MLA, i, 1)
                dve.wait_ge(s("kn_out"), i + 1)
                dve.wait_ge(s("norm_sums"), i + 1)
                V.tensor_tensor(knsq[:, :, :], kn[:, :, :], kn[:, :, :], ALU.mult).then_inc(s("kn_sq"), 1)
                panel_over(P_MLA, N_MLA, i, 2, uq=not last_one)
                dve.wait_ge(s("norm_sums"), i + 2)
                dve.wait_ge(s("qrg_out"), i + 1)
                V.tensor_tensor(qc[:, :], qrg[:, :], cos2[:, META:L], ALU.mult)
                own.link(V.tensor_tensor(qsn[:, :], sin2[:, META:L], psum[:, 7, 0:SEQ], ALU.mult))
                own.link(V.tensor_tensor(qc[:, :], qc[:, :], qsn[:, :], ALU.add))
                dve.wait_ge(s("rq_done"), i + 1)
                for h in range(2):
                    V.scalar_tensor_tensor(qs[:, h, :], qn[:, h, :], gain[:, G_QN:G_QN + 1], rq[:, h, :], ALU.mult, ALU.mult)
                    V.tensor_tensor(qrs[half(h), :], qc[half(h), :], rq[half(h), h, :], ALU.mult)
                dve.wait_ge(s("rk_done"), i + 1)
                for h in range(2):
                    V.scalar_tensor_tensor(ks[:, h, :], kn[:, h, :], gain[:, G_KN:G_KN + 1], rk[:, h, :], ALU.mult, ALU.mult)
                    last = V.tensor_tensor(krs[half(h), h, :], krr[half(h), :], rk[half(h), h, :], ALU.mult)
                last.then_inc(s("qk_done"), 1)
                panel_over(P_MLA, N_MLA, i, 3)
                dve.wait_ge(s("scores"), i + 1)
                dve.wait_ge(s("p_turned"), i + 1)
                dve.wait_ge(s("const_causal"), 16)
                V.memset(tick[:, :], 0.0)
                for h in range(2):
                    V.tensor_tensor_reduce(out=sc0[:, h, :], in0=psum[:, 4 + h, 0:META + P], in1=causal[:, P:L], scale=1.0,
                                           scalar=-3e38, op0=ALU.add, op1=ALU.max, accum_out=mx[:, 2 * h:2 * h + 1])
                    last = V.tensor_tensor_reduce(out=sc1[:, h, :], in0=psum[:, 4 + h, META + P:META + P + L], in1=causal[:, :],
                                                  scale=1.0, scalar=-3e38, op0=ALU.add, op1=ALU.max,
                                                  accum_out=mx[:, 2 * h + 1:2 * h + 2])
                own.link(last)
                V.tensor_scalar(nb[:, :], mx[:, :], -(QK ** -0.5), None, ALU.mult).then_inc(s("nb_done"), 1)
                dve.wait_ge(s("p_exp"), 2 * i + 2)
                own.link(V.reciprocal(rs[:, :], sm[:, :]))
                for h in range(2):
                    V.tensor_scalar(sc0[:, h, :], sc0[:, h, :], rs[:, 2 * h:2 * h + 1], None, ALU.mult)
                    last = V.tensor_scalar(sc1[:, h, :], sc1[:, h, :], rs[:, 2 * h + 1:2 * h + 2], None, ALU.mult)
                last.then_inc(s("p_done"), 1)

            dve.wait_ge(s("krr_done"), 1)
            for h in range(2):
                V.memset(krs[half(1 - h), h, :], 0.0)
            with dve.Fori(0, PAIRS - 1) as i:
                own.enter(i, 4)
                mla_turn(i, False)
            own.leave(PAIRS - 1)
            own.enter(0, 4)
            mla_turn(PAIRS - 1, True)
            own.leave(1)

            dve.wait_ge(s("const_keep"), 16)

            def gla_turn(i, first):
                own.enter(0 if first else i - 1, 6)
                panel_over(P_GLA, N_GLA, i, 0)
                dve.wait_ge(s("gl_done"), i + 1)
                own.link(V.scalar_tensor_tensor(gx[:, :, :], gx[:, :, :], 0.0, gl[:, :, :], ALU.min, ALU.subtract))
                for dt in range(2):
                    last = V.tensor_tensor_scan(gb[:, dt, :], keep[:, :], gx[:, dt, :], 0.0, ALU.mult, ALU.add)
                own.link(last)
                for dt in range(2):
                    V.tensor_tensor(kf[:, dt, 0:META], gb[:, dt, META - 1:META].broadcast_to([P, META]),
                                    gb[:, dt, 0:META], ALU.subtract)
                    g3 = gb[:, dt, META:META + 3 * CHUNK].rearrange("p (c t) -> p c t", t=CHUNK)
                    last = V.tensor_tensor(kf[:, dt, META:META + 3 * CHUNK].rearrange("p (c t) -> p c t", t=CHUNK),
                                           g3[:, :, CHUNK - 1:CHUNK].broadcast_to([P, 3, CHUNK]), g3, ALU.subtract)
                last.then_inc(s("decay"), 1)
                panel_over(P_GLA, N_GLA, i, 1)
                if first:
                    dve.wait_ge(s("om_out"), PAIRS)
                    V.memset(am[:, :, :], 0.0)
                    V.memset(va0[:, :], 0.0)
                    V.memset(kdn0[:, :], 0.0).then_inc(s("zeros_set"), 1)
                dve.wait_ge(s("decay_exp"), i + 1)
                V.tensor_tensor(ke[:, :, :], enb[:, :, :], pair(0, L), ALU.mult)
                n = META + 3 * CHUNK
                own.link(V.tensor_tensor(kd[:, :, 0:n], kf[:, :, 0:n], pair(0, n), ALU.mult))
                c0 = slice(META, META + CHUNK)
                e0, e1 = META + CHUNK - 1, META + 2 * CHUNK - 1
                V.tensor_tensor(ebp[:, :, :], eb[:, :, e0:e0 + 1], eb[:, :, e1:e1 + 1], ALU.mult)
                own.link(V.tensor_copy(kx[:, :, :], kd[:, :, c0]))
                for dt in range(2):
                    last = V.tensor_scalar(kd[:, dt, c0], kd[:, dt, c0], eb[:, dt, e1:e1 + 1], None, ALU.mult)
                last.then_inc(s("kd_done"), 1)
                panel_over(P_GLA, N_GLA, i, 2)
                panel_over(P_GLA, N_GLA, i, 3)
                V.scalar_tensor_tensor(qd[:, :, :], pair(2, SEQ), DK ** -0.5, eb[:, :, META:L], ALU.mult,
                                       ALU.mult).then_inc(s("qd_done"), 1)
                dve.wait_ge(s("qd_done"), i + 1)
                q4 = [t[:, :, :].rearrange("p d (c t) -> p d c t", t=CHUNK) for t in (qx, qd)]
                for dt in range(2):
                    V.tensor_copy(q4[0][:, dt, 0:4:2, :], q4[1][:, dt, 0:4:2, :])
                    for c in (1, 3):
                        e = META + c * CHUNK - 1
                        last = V.tensor_scalar(q4[0][:, dt, c, :], q4[1][:, dt, c, :], eb[:, dt, e:e + 1], None, ALU.mult)
                last.then_inc(s("qx_done"), 1)
                panel_over(P_GLA, N_GLA, i, 4)
                panel_over(P_GLA, N_GLA, i, 5)
                dve.wait_ge(s("a_in"), i + 1)
                dve.wait_ge(s("zeros_set"), 1)
                dve.wait_ge(s("const_inchunk"), 16)
                V.memset(tick[:, :], 0.0)
                for c in range(2):
                    last = V.copy_predicated(am[:, c, :], inchunk[:, :], psum[:, 5, c * P:(c + 1) * P])
                own.link(last)
                V.tensor_copy(am[0:CHUNK, :, CHUNK:P],
                              psum[0:CHUNK, 5, 2 * P:3 * P].rearrange("p (c t) -> p c t", c=2)).then_inc(s("am_done"), 1)
                panel_over(P_GLA, N_GLA, i, 6)
                panel_over(P_GLA, N_GLA, i, 7)
                panel_over(P_GLA, N_GLA, i, 8)
                panel_over(P_GLA, N_GLA, i, 9)
                for n in range(4):
                    c, dt = n // 2, n % 2
                    dve.wait_ge(s("ds_in"), i * 4 + (n + 1))
                    src = psum[:, (6, 7, 4, 5)[n], :]
                    if c == 0:
                        V.tensor_copy(st[:, 0, dt, :], src).then_inc(s("st_done"), 1)
                    else:
                        dve.wait_ge(s("st_done"), i * 4 + (dt + 1))
                        V.scalar_tensor_tensor(st[:, 1, dt, :], st[:, 0, dt, :], ebp[:, dt, :], src,
                                               ALU.mult, ALU.add).then_inc(s("st_done"), 1)
                panel_over(P_GLA, N_GLA, i, 10)
                panel_over(P_GLA, N_GLA, i, 11)
                dve.wait_ge(s("ro_done"), i + 2)
                for v in range(4):
                    ov = o_gla[:, bass.ds(i * 4 + v, 1), :].rearrange("p a q -> p (a q)")
                    last = V.scalar_tensor_tensor(ov, ov, gain[:, G_O + v:G_O + v + 1], ro, ALU.mult, ALU.mult)
                own.link(last)
                dve.wait_ge(s("sr_out"), i * 2 + 3)
                og = o_gla[:, bass.ds(i * 4, 4), :]
                V.tensor_tensor(og, og, sr[:, :, :], ALU.mult).then_inc(s("gated"), 1)

            gla_turn(0, True)
            own.leave(1)
            with dve.Fori(1, GLA_HEADS) as i:
                gla_turn(i, False)
            own.leave(GLA_HEADS - 1)

            def o_los(n, groups, dst, src, hi):
                for q in groups:
                    t = slice(4 * q, 4 * q + 4)
                    dve.wait_ge(s("o_hi"), 4 * n + q + 1)
                    V.tensor_tensor(dst[:, t, :], src[:, t, :], hi[:, t, :].bitcast(F32), ALU.subtract).then_inc(s("o_lo"), 1)

            def merge_turn(i, first):
                own.enter(0 if first else i - 1, 4)
                for b in range(2):
                    blk = i * 2 + b
                    for j in range(4):
                        panel_over(P_MRG, N_MRG, i, 6 * b + j)
                        if first and b == 0 and j < 2:
                            o_los(j, range(2 - 2 * j, 4), *((o_lo_g, o_gla, o_hi_g), (o_lo_m, o_mla, o_hi_m))[j])
                    dve.wait_ge(s("sa_done"), blk + 1)
                    own.link(V.tensor_tensor(mf[:, :, :], sa[:, :, :], pair(2, SEQ), ALU.mult))
                    for j in range(4, 6):
                        panel_over(P_MRG, N_MRG, i, 6 * b + j)
                    dve.wait_ge(s("sb_done"), blk + 1)
                    own.link(V.tensor_tensor(mb[:, :, :], sb[:, :, :], pair(4, SEQ), ALU.mult))
                    V.tensor_tensor(mf[:, :, :], mf[:, :, :], mb[:, :, :], ALU.add).then_inc(s("mf_done"), 1)
                    dve.wait_ge(s("m_hi_done"), blk + 1)
                    t = bass.ds(i * 4 + 2 * b, 2)
                    V.tensor_tensor(m_lo[:, t, :], mf[:, :, :], m_hi[:, t, :].bitcast(F32),
                                    ALU.subtract).then_inc(s("merged"), 1)

            o_los(0, (0, 1), o_lo_g, o_gla, o_hi_g)
            merge_turn(0, True)
            own.leave(1)
            with dve.Fori(1, 4) as i:
                merge_turn(i, False)
            own.leave(3)
            with dve.Fori(0, 4) as i:
                for b in range(2):
                    for kh in range(2):
                        panel_over(P_OUT, N_OUT, i, 2 * b + kh)
                    dve.wait_ge(s("xs_out"), i * 2 + (b + 1))
                    xb = x2[:, bass.ds(i * 4 + 2 * b, 2), :]
                    V.tensor_tensor(xb, xb, pair(2 * b, SEQ), ALU.add).then_inc(s(f"x2_out{b}"), 1)
                    dve.wait_ge(s("h2_hi_done"), i * 2 + (b + 1))
                    for m in range(2):
                        f = i * 4 + (2 * b + m)
                        last = V.scalar_tensor_tensor(h2_lo[:, bass.ds(f, 1), :], x2[:, bass.ds(f, 1), :],
                                                      gain[:, bass.ds(i * 4 + (G_2 + 2 * b + m), 1)],
                                                      h2_hi[:, bass.ds(f, 1), :].bitcast(F32), ALU.mult, ALU.subtract)
                    last.then_inc(s("h2_lo_done"), 1)
            def ff_turn(i, first):
                for j in range(2):
                    panel_over(P_FF, N_FF, i, j)
                if first:
                    dve.wait_ge(s("r2_done"), 1)
                dve.wait_ge(s("af_done"), i + 1)
                V.tensor_tensor(sg[:, :, :], r2[:, :, :], pair(0, SEQ), ALU.mult).then_inc(s("gate_out"), 1)
                for j in range(2, 4):
                    panel_over(P_FF, N_FF, i, j)
                dve.wait_ge(s("sgr_done"), i + 1)
                dve.wait_ge(s("a_lo_done"), i + 1)
                V.tensor_tensor(af[:, :, :], sg[:, :, :], pair(2, SEQ), ALU.mult).then_inc(s("af_done"), 1)
                dve.wait_ge(s("a_hi_done"), i + 1)
                t = bass.ds(i * 2, 2)
                V.tensor_tensor(a_lo[:, t, :], af[:, :, :], a_hi[:, t, :].bitcast(F32),
                                ALU.subtract).then_inc(s("a_lo_done"), 1)

            ff_turn(0, True)
            with dve.Fori(1, FF // 256) as i:
                ff_turn(i, False)
            last_turn = FT // 4 - 1
            with dve.Fori(0, last_turn) as i:
                for c in range(4):
                    panel_over(P_DN, N_DN, i, c)
            for c in range(4):
                if c < 2:
                    split(P_DN, N_DN, last_turn, c + 2)
                dve.wait_ge(used, after(P_DN, N_DN, last_turn, c))
                if c >= 2:
                    dve.wait_ge(s("y_turned"), c - 1)
                y = psum[:, 2 * c:2 * c + 2, :].rearrange("p b (v q) -> p (b v) q", q=SEQ)
                V.tensor_tensor(yT[:, c % 2], x2[:, 4 * c:4 * c + 4, :], y, ALU.add).then_inc(s("y_done"), 1)

        @block.tensor
        def _(pe):
            M = nc.tensor.matmul
            free_at_start(pe, "pe")

            def three(o, a, b, start, stop, skip=False):
                M(o, a[0], b[0], start=start, stop=False, skip_group_check=skip)
                M(o, a[0], b[1], start=False, stop=False, skip_group_check=skip)
                return M(o, a[1], b[0], start=False, stop=stop, skip_group_check=skip)

            def panel(p0, per, i, j):
                pe.wait_ge(lo_done, after(p0, per, i, j) - 1)
                k = slot(p0, j, SPL)
                return whi[k], wlo[k]

            def second_half(p0, per, i, j, last=None):
                if last is not None:
                    last.then_inc(used, 1)
                pe.wait_ge(lo_done, after(p0, per, i, j))

            def wide(p0, per, i, j, kh, b0, src, lo=META, start=True):
                banks = b0 if isinstance(b0, tuple) else (b0, b0 + 1)
                hi_lo = [w[:, :].rearrange("p (k c) -> p k c", k=8) for w in panel(p0, per, i, j)]
                n = L - lo if src is h_pair else SEQ
                for k in range(8):
                    kk = 8 * kh + k
                    rhs = [t[:, kk, lo:L] if src is h_pair else t[:, kk, :] for t in src]
                    for m in range(2):
                        lhs = [w[:, k, m * P:(m + 1) * P] for w in hi_lo]
                        last = three(psum[:, banks[m], 0:n], lhs, rhs, start and kh == 0 and k == 0, kh == 1 and k == 7)
                    if k == 3:
                        second_half(p0, per, i, j, last)
                last.then_inc(used, 1)

            h_pair = (h_hi, h_lo)

            pe.wait_ge(s("ident_in"), 16)
            pe.wait_ge(s("xm_in"), 16)

            def x_sum(f):
                if f < 12:
                    pe.wait_ge(s("x_sq2"), f // 4 + 1)
                else:
                    pe.wait_ge(s("x_sq"), f + 1)
                return M(psum[:, 4, 0:L], ones[:, :], xsq[:, f, :], start=f == 0, stop=f == KT - 1)

            pe.wait_ge(s("ones_set"), 1)
            for f in range(KT):
                if f % 4 == 0:
                    pe.wait_ge(s(f"xn_in{f // 4}"), 16)
                if f >= 4:
                    pe.wait_ge(s("xT_out"), f - 3)
                cols = slice(f * P, (f + 1) * P)
                nc.tensor.transpose(psum[:, f % 4, 0:META], xm[:, cols], ident[0:META, 0:META])
                for t in range(2):
                    last = nc.tensor.transpose(psum[:, f % 4, META + t * P:META + (t + 1) * P], xn[:, t, cols], ident[:, :])
                last.then_inc(s("x_turned"), 1)
                if f in (8, 12):
                    x_sum(f - 8)
                    x_sum(f - 7)
            for f in (8, 9, 12, 13, 14, 15):
                last = x_sum(f)
            last.then_inc(s("x_sums"), 1)

            hi_lo = [w[:, 0:KT * (RANK + ROPE)].rearrange("p (k c) -> p k c", k=KT) for w in panel(0, 1, 0, 0)]
            for k in range(KT):
                if k == KT // 2:
                    second_half(0, 1, 0, 0)
                if k % 4 == 0:
                    pe.wait_ge(s("h_lo_done"), k // 4 + 1)
                if k % 4 == 2:
                    pe.wait_ge(s("h_lo_pool"), k // 4 + 1)
                last = three(psum[0:ROPE + RANK, 6, 0:L], [w[:, k, :] for w in hi_lo], [t[:, k, :] for t in h_pair],
                             k == 0, k == KT - 1)
            last.then_inc(used, 2)

            def lat_sum(side):
                lo = 0 if side == 0 else META
                pe.wait_ge(s("lat_sq"), 2 * side + 2)
                for k in range(LT):
                    last = M(psum[:, 6 + side, 0:L - lo], ones[:, :], latsq[:, side, k, lo:L], start=k == 0, stop=k == LT - 1)
                last.then_inc(s("lat_sums"), 1)

            for b in range(4):
                if b > 1:
                    pe.wait_ge(s("lat_out"), b - 1)
                for kh in range(2):
                    wide(P_LAT, 8, 0, 2 * b + kh, kh, 2 * (b % 2), h_pair, 0 if b < 2 else META)
                    if b == 0 and kh == 0:
                        pe.wait_ge(s("krg_done"), 1)
                        pe.wait_ge(s("const_dup"), 16)
                        M(psum[:, 4, 0:L], dup[:, 0, :], krg[:, :], start=True, stop=True)
                        M(psum[:, 5, 0:L], dup[:, 1, :], krg[:, :], start=True, stop=True).then_inc(s("kr_dup"), 1)
                    if b == 2 and kh == 0:
                        lat_sum(0)

            def mla_norms(i):
                pe.wait_ge(s("mla_sq"), i + 1)
                pe.wait_ge(s("vm_out"), i + 1)
                pe.wait_ge(s("qrg_out"), i + 1)
                for h in range(2):
                    M(psum[:, 4, h * SEQ:(h + 1) * SEQ], ones[:, :], qnsq[:, h, :], start=True, stop=True)
                    M(psum[:, 1 + 4 * h, 0:L], ones[:, :], knsq[:, h, :], start=True, stop=True)
                M(psum[:, 7, 0:SEQ], rot2[:, :], qrg[:, :], start=True, stop=True).then_inc(s("norm_sums"), 1)

            def mla_scores(i):
                pe.wait_ge(s("qk_done"), i + 1)
                for h in range(2):
                    for t, (c0, n) in enumerate(((0, META + P), (META + P, L))):
                        o = psum[:, 4 + h, c0:c0 + n]
                        q = slice(t * P, (t + 1) * P)
                        M(o, qs[:, h, q], ks[:, h, 0:n], start=True, stop=False)
                        last = M(o, qrs[:, q], krs[:, h, 0:n], start=False, stop=True)
                last.then_inc(s("scores"), 1)

            def mla_turn_p(i):
                T = nc.tensor.transpose
                pe.wait_ge(s("p_done"), i)
                for h in range(2):
                    for t, sc in enumerate((sc0, sc1)):
                        q = slice(t * P, (t + 1) * P)
                        T(psum[0:META, 6 + h, q], sc[:, h, 0:META], ident[:, :])
                        T(psum[:, 6 + h, SEQ + t * P:SEQ + (t + 1) * P], sc[:, h, META:META + P], ident[:, :])
                    last = T(psum[:, 4, h * P:(h + 1) * P], sc1[:, h, META + P:L], ident[:, :])
                last.then_inc(s("p_turned"), 1)

            def mla_pv(i):
                pe.wait_ge(s("pt_out"), i)
                for h in range(2):
                    o = psum[:, 7, h * SEQ:(h + 1) * SEQ]
                    M(o, vm0[:, h, :], pt0[:, h, :], start=True, stop=False)
                    M(o, vm[:, 0, h, :], pt1[:, h, :], start=False, stop=False)
                    last = M(o[:, P:SEQ], vm[:, 1, h, :], pt2[:, h, :], start=False, stop=True)
                last.then_inc(s("pv_done"), 1)

            def mla_queries(i, j):
                hi_lo = panel(P_MLA, N_MLA, i, j)
                nope = [uq_part(w, *UQ_PARTS[0], False) for w in hi_lo]
                rope = [w[:, LT * 2 * NOPE:LT * 2 * QK].rearrange("p (k c) -> p k c", k=LT) for w in hi_lo]
                c_q = (cq_hi, cq_lo)
                for h in range(2):
                    for k in range(LT):
                        last = three(psum[:, 0, h * SEQ:(h + 1) * SEQ], [w[:, k, h, :] for w in nope],
                                     [t[:, k, :] for t in c_q], k == 0, k == LT - 1)
                second_half(P_MLA, N_MLA, i, j, last)
                if j:
                    pe.wait_ge(s("vm_out"), 1)
                for k in range(LT):
                    last = three(psum[:, 1, 0:SEQ], [w[:, k, :] for w in rope], [t[:, k, :] for t in c_q],
                                 k == 0, k == LT - 1)
                last.then_inc(used, 1)

            def mla_keys(w_ukv):
                for h in range(2):
                    for k in range(LT):
                        last = three(psum[:, 2 + h, 0:L], [w[:, k, h, 0:NOPE] for w in w_ukv],
                                     [ckv_hi[:, k, :], ckv_lo[:, k, :]], k == 0, k == LT - 1)
                return last

            def mla_values(w_ukv, t):
                a, b = TOK[t]
                o = psum[0:META, 1, SEQ:2 * SEQ] if t == 0 else psum[:, 5, (t - 1) * SEQ:t * SEQ]
                o = o.rearrange("p (h d) -> p h d", h=2)
                for k in range(LT):
                    last = three(o, [ckv_hi[:, k, a:b], ckv_lo[:, k, a:b]], [w[:, k, :, NOPE:] for w in w_ukv],
                                 k == 0, k == LT - 1)
                return last

            def mla_turn(i, first):
                if not first:
                    pe.wait_ge(s("zb_out"), i)
                    mla_queries(i, 0)
                j = 0 if first else 1
                w_ukv = [w[:, :].rearrange("p (k h c) -> p k h c", k=LT, h=2) for w in panel(P_MLA, N_MLA, i, j)]
                second_half(P_MLA, N_MLA, i, j)
                if first:
                    pe.wait_ge(s("lat_lo"), 1)
                    pe.wait_ge(s("lat_out"), 3)
                    mla_values(w_ukv, 0)
                    lat_sum(1)
                    mla_values(w_ukv, 1)
                    mla_values(w_ukv, 2)
                    pe.wait_ge(s("lat_out"), 4)
                    mla_keys(w_ukv).then_inc(used, 2)
                    pe.wait_ge(s("lat_lo"), 2)
                    mla_queries(i, 1)
                else:
                    mla_keys(w_ukv)
                    mla_turn_p(i)
                    for t in range(3):
                        last = mla_values(w_ukv, t)
                    last.then_inc(used, 2)
                if not first:
                    mla_pv(i)
                pe.wait_ge(s("qn_out"), i + 1)
                wide(P_MLA, N_MLA, i, 2, 0, (0, 6), h_pair)
                if not first:
                    pe.wait_ge(s("om_out"), i)
                mla_norms(i)
                wide(P_MLA, N_MLA, i, 3, 1, (0, 6), h_pair)
                mla_scores(i)

            pe.wait_ge(s("const_rot2"), 16)
            mla_turn(0, True)
            with pe.Fori(1, PAIRS) as i:
                mla_turn(i, False)

            def turn_values(i, b):
                pe.wait_ge(s("vT_out"), i * 2 + (b + 1))
                if b == 0:
                    pe.wait_ge(s("kdn_out"), i + 1)
                else:
                    pe.wait_ge(s("v_out"), i * 2 + 1)
                T = nc.tensor.transpose
                for m in range(2):
                    T(psum[0:META, 7, DK + m * P:DK + (m + 1) * P], vT[:, m, 0:META], ident[:, :])
                    for t in range(2):
                        last = T(psum[:, 4 + b, t * 256 + m * P:t * 256 + (m + 1) * P], vT[:, m, TOK[t + 1][0]:TOK[t + 1][1]],
                                 ident[:, :])
                last.then_inc(s("v_turned"), 1)

            def gla_turn(i, first):
                G = (P_GLA, N_GLA, i)
                wait(pe, s("sr_out"), i * 2)
                wide(*G, 0, 0, 0, h_pair, 0)
                if first:
                    mla_turn_p(PAIRS)
                pe.wait_ge(s("sr_out"), i * 2 + 1)
                if first:
                    pe.wait_ge(s("lr_out"), 1)
                pe.wait_ge(s("w2_in"), i * 16 + 16)
                for dt in range(2):
                    last = M(psum[:, 2 + dt, 0:L], w2h[LR, dt * P:(dt + 1) * P], lrT[LR, :], start=True, stop=True)
                last.then_inc(s("logits"), 1)
                wide(*G, 1, 1, 0, h_pair, 0)
                if first:
                    mla_pv(PAIRS)
                pe.wait_ge(s("logits_out"), i + 1)
                wide(*G, 2, 0, 2, h_pair)
                wide(*G, 3, 1, 2, h_pair)
                pe.wait_ge(s("kd_done"), i + 1)
                pe.wait_ge(s("ro_done"), i + 1)
                wide(*G, 4, 0, 0, h_pair, 0)
                wide(*G, 5, 1, 0, h_pair, 0)
                T = nc.tensor.transpose
                if first:
                    pe.wait_ge(s("om_out"), PAIRS)
                pe.wait_ge(s("o_out"), i + 1)
                for dt in range(2):
                    d = slice(dt * P, (dt + 1) * P)
                    T(psum[:, 6, d], kd[:, dt, META:META + P], ident[:, :])
                    last = T(psum[0:META, 6, DK + dt * P:DK + (dt + 1) * P], kd[:, dt, 0:META], ident[:, :])
                last.then_inc(s("kd_turned"), 1)
                pe.wait_ge(s("qd_done"), i + 1)
                for c in range(2):
                    for dt in range(2):
                        last = M(psum[:, 5, c * P:(c + 1) * P], ke[:, dt, META + c * P:META + (c + 1) * P],
                                 qd[:, dt, c * P:(c + 1) * P], start=dt == 0, stop=dt == 1)
                for c in range(2):
                    for dt in range(2):
                        k0 = kx[:, dt, :] if c == 0 else kd[:, dt, META + P:META + P + CHUNK]
                        last = M(psum[0:CHUNK, 5, 2 * P + c * CHUNK:2 * P + (c + 1) * CHUNK], k0,
                                 qd[:, dt, c * P + CHUNK:(c + 1) * P], start=dt == 0, stop=dt == 1)
                last.then_inc(s("a_in"), 1)
                wide(*G, 6, 0, 2, h_pair, 0)
                turn_values(i, 0)
                wide(*G, 7, 1, 2, h_pair, 0)
                wide(*G, 8, 0, 0, h_pair)
                pe.wait_ge(s("am_done"), i + 1)
                turn_values(i, 1)
                wide(*G, 9, 1, 0, h_pair)
                pe.wait_ge(s("v_out"), i * 2 + 2)
                for n in range(4):
                    dt = n % 2
                    d = slice(dt * P, (dt + 1) * P)
                    k, v = (kdn0, va0[:, :]) if n < 2 else (kdn, va[:, 0, :])
                    M(psum[:, (6, 7, 4, 5)[n], :], k[:, d], v, start=True, stop=True).then_inc(s("ds_in"), 1)
                wide(*G, 10, 0, 2, h_pair)
                pe.wait_ge(s("qx_done"), i + 1)
                pe.wait_ge(s("st_done"), i * 4 + 4)
                for v in range(4):
                    vs = slice(v * P, (v + 1) * P)
                    for c in range(2):
                        col = (v % 2) * SEQ + c * P
                        o = psum[:, 6 + v // 2, col:col + P]
                        M(o, va[:, c, vs], am[:, c, :], start=True, stop=False)
                        for dt in range(2):
                            last = M(o, st[:, c, dt, vs], qx[:, dt, c * P:(c + 1) * P], start=False, stop=dt == 1)
                last.then_inc(s("o_added"), 1)
                wide(*G, 11, 1, 2, h_pair)
                pe.wait_ge(s("o_sq_sum"), i + 1)
                M(psum[:, 4, 0:SEQ], ones[:, :], osq[:, 0, :], start=True, stop=True).then_inc(s("o_sums"), 1)

            pe.wait_ge(s("zb_out"), PAIRS)
            gla_turn(0, True)
            with pe.Fori(1, GLA_HEADS) as i:
                gla_turn(i, False)

            pe.wait_ge(s("sr_out"), 2 * GLA_HEADS)

            def merge_turn(i, first):
                for b in range(2):
                    G = (P_MRG, N_MRG, i)
                    wait(pe, s("sa_done"), i * 2 + b)
                    for kh in range(2):
                        wide(*G, 6 * b + kh, kh, 0, h_pair)
                    wait(pe, s("mf_done"), i * 2 + b)
                    if first and b == 0:
                        pe.wait_ge(s("sr_out"), 2 * GLA_HEADS + 1)
                    for kh in range(2):
                        if first and b == 0:
                            pe.wait_ge(s("o_lo"), 2 * kh + 2)
                        wide(*G, 6 * b + 2 + kh, kh, 2, (o_hi_g, o_lo_g))
                    if first and b == 0:
                        pe.wait_ge(s("ro_done"), GLA_HEADS + 1)
                        pe.wait_ge(s("o_lo"), 8)
                    for kh in range(2):
                        wide(*G, 6 * b + 4 + kh, kh, 4, (o_hi_m, o_lo_m))

            merge_turn(0, True)
            with pe.Fori(1, 4) as i:
                merge_turn(i, False)

            def out_turn(i, first):
                for b in range(2):
                    if not first:
                        pe.wait_ge(s(f"x2_out{b}"), i)
                    for kh in range(2):
                        hi_lo = [w[:, :].rearrange("p (k c) -> p k c", k=8) for w in panel(P_OUT, N_OUT, i, 2 * b + kh)]
                        if first and b == kh == 0:
                            pe.wait_ge(s("merged"), 5)
                        for k in range(8):
                            kk = 8 * kh + k
                            if first and b == 0 and kh == 1 and k % 2 == 0:
                                pe.wait_ge(s("merged"), kk // 2 + 2)
                            for m in range(2):
                                last = three(psum[:, 2 * b + m, 0:SEQ], [w[:, k, m * P:(m + 1) * P] for w in hi_lo],
                                             [m_hi[:, kk, :], m_lo[:, kk, :]], kk == 0, kk == KT - 1)
                            if k == 3:
                                second_half(P_OUT, N_OUT, i, 2 * b + kh, last)
                        last.then_inc(used, 1)
                        if kh == 0:
                            if first and b == 0:
                                pe.wait_ge(s("mf_done"), 8)
                            pe.wait_ge(s(f"xs_in{b}"), i * 16 + 16)
                            for m in range(2):
                                for t in range(2):
                                    last = nc.tensor.transpose(psum[:, 4 + 2 * b + m, t * P:(t + 1) * P],
                                                               xs[:, b, t, m * P:(m + 1) * P], ident[:, :])
                            last.then_inc(s("xs_turned"), 1)

            pe.wait_ge(s("sa_done"), 8)
            out_turn(0, True)
            with pe.Fori(1, 4) as i:
                out_turn(i, False)

            def ff_turn(i, first):
                if first:
                    pe.wait_ge(s("x2_out0"), 5)
                    pe.wait_ge(s("h2_lo_done"), 4)
                else:
                    pe.wait_ge(s("gate_out"), i)
                wide(P_FF, N_FF, i, 0, 0, 0, (h2_hi, h2_lo))
                if first:
                    pe.wait_ge(s("h2_lo_done"), 8)
                wide(P_FF, N_FF, i, 1, 1, 0, (h2_hi, h2_lo))
                if first:
                    pe.wait_ge(s("x2_sum"), 1)
                    M(psum[:, 4, 0:SEQ], ones[:, :], ssum[:, 0, :], start=True, stop=True).then_inc(s("x2_sums"), 1)
                pe.wait_ge(s("af_done"), i + 1)
                for kh in range(2):
                    wide(P_FF, N_FF, i, 2 + kh, kh, 2, (h2_hi, h2_lo))

            ff_turn(0, True)
            with pe.Fori(1, FF // 256) as i:
                ff_turn(i, False)

            def down(i, c, first, last_one):
                hi_lo = [w[:, :].rearrange("p (k c) -> p k c", k=4) for w in panel(P_DN, N_DN, i, c)]
                for k in range(4):
                    if k == 2:
                        second_half(P_DN, N_DN, i, c, last)
                    rhs = [t[:, bass.ds(i * 4 + k, 1), :].rearrange("p a q -> p (a q)") for t in (a_hi, a_lo)]
                    for m in range(4):
                        o = psum[:, 2 * c + m // 2, (m % 2) * SEQ:(m % 2 + 1) * SEQ]
                        last = three(o, [w[:, k, m * P:(m + 1) * P] for w in hi_lo], rhs,
                                     first and k == 0 and m % 2 == 0, last_one and k == 3, skip=True)
                last.then_inc(used, 1)

            pe.wait_ge(s("gate_out"), FF // 256)
            down(0, 0, True, False)
            pe.wait_ge(s("af_done"), FF // 256 + 1)
            down(0, 1, True, False)
            pe.wait_ge(s("a_lo_done"), FF // 256 + 1)
            for c in range(2, 4):
                down(0, c, True, False)
            last_turn = FT // 4 - 1
            with pe.Fori(1, last_turn) as i:
                for c in range(4):
                    down(i, c, False, False)

            def turn(c):
                pe.wait_ge(s("y_done"), c + 1)
                for t in range(2):
                    for m in range(4):
                        last = nc.tensor.transpose(psum[:, 2 * c + t, m * P:(m + 1) * P], yT[:, c % 2, m, t * P:(t + 1) * P],
                                                   ident[:, :])
                last.then_inc(s("y_turned"), 1)

            for c in range(4):
                down(last_turn, c, False, True)
                if c:
                    turn(c - 1)
            turn(3)


def tables():
    i = np.arange(P)
    f32 = np.float32
    swap = np.zeros((ROPE, ROPE), f32)
    h = ROPE // 2
    swap[np.arange(h) + h, np.arange(h)] = -1.0
    swap[np.arange(h), np.arange(h) + h] = 1.0
    eye = np.eye(ROPE, dtype=f32)
    causal = np.zeros((P, L), f32)
    causal[:, META + P:] = np.where(i[None, :] <= i[:, None], 0.0, NEG)
    inv = (1.0 / (f32(10000.0) ** (np.arange(0, ROPE, 2, dtype=f32) / f32(ROPE)))).astype(f32)
    ang = np.tile(np.arange(L, dtype=f32)[None, :] * inv[:, None], (4, 1))
    keep = np.ones((P, L), f32)
    keep[:, 0] = 0.0
    keep[:, META::CHUNK] = 0.0
    return {
        "ident": np.eye(P, dtype=f32),
        "rot2": np.kron(np.eye(2, dtype=f32), swap),
        "dup": np.stack([np.tile(eye, (1, 2)), np.tile(swap, (1, 2))], 1),
        "causal": causal,
        "cos2": np.cos(ang),
        "sin2": np.sin(ang),
        "inchunk": ((i[:, None] <= i[None, :]) & (i[:, None] // CHUNK == i[None, :] // CHUNK)).astype(np.int32),
        "keep": keep,
    }


def kernel(x, meta_tokens, norm1_g, w_in, gla_gate_w2, gla_gate_b, gla_onorm_g, w_branch_a, q_a_norm_g, w_uq,
           kv_a_norm_g, w_ukv, q_norm_g, k_norm_g, w_branch_b, w_out, norm2_g, w_gate_up, w_down):
    import concourse.bacc as bacc
    from concourse.bass_utils import run_bass_kernel_spmd

    def columns(g):
        return np.asarray(g).reshape(-1, P).T

    qg, kg = np.asarray(q_norm_g)[0], np.asarray(k_norm_g)[0]
    gains = np.concatenate(
        [columns(norm1_g), columns(norm2_g), columns(gla_onorm_g), columns(q_a_norm_g), columns(kv_a_norm_g),
         columns(qg[:NOPE]), columns(np.concatenate([qg[NOPE:], qg[NOPE:]])),
         columns(kg[:NOPE]), columns(np.concatenate([kg[NOPE:], kg[NOPE:]])), columns(gla_gate_b)], axis=1)
    arrays = {
        "x": x, "meta": meta_tokens, "w_in": w_in, "w2": gla_gate_w2, "w_a": w_branch_a, "w_uq": w_uq, "w_ukv": w_ukv,
        "w_b": w_branch_b, "w_out": w_out, "w_gu": w_gate_up, "w_dn": w_down, "gains": gains,
    }
    arrays = {f"in_{n}": np.ascontiguousarray(a) for n, a in arrays.items()}
    fixed = tables()
    arrays |= {f"const_{n}": np.ascontiguousarray(a) for n, a in fixed.items()}
    nc = bacc.Bacc("TRN2", target_bir_lowering=False, num_devices=1)
    ap = {n: nc.dram_tensor(n, a.shape, mybir.dt.from_np(a.dtype), kind="ExternalInput").ap() for n, a in arrays.items()}
    out = nc.dram_tensor("out", (1, SEQ, D), F32, kind="ExternalOutput").ap()

    def two_d(n):
        a = ap[f"in_{n}"]
        return a.rearrange("o k c -> (o k) c")

    build(nc, ap["in_x"], ap["in_meta"], two_d("w_in"), two_d("w2"), two_d("w_a"), two_d("w_uq"), two_d("w_ukv"),
          two_d("w_b"), two_d("w_out"), two_d("w_gu"), two_d("w_dn"), ap["in_gains"],
          {n: ap[f"const_{n}"] for n in fixed}, out)
    r = run_bass_kernel_spmd(nc, [arrays], core_ids=[0])
    return r.results[0]["out"]
```
